# Optimizing a Trainium2 kernel written in Bass

```python
import math
import jax
import jax.numpy as jnp
from jax import lax
import numpy as np
import jax, jax.numpy as jnp

D_MODEL = 1024
BATCH = 1
SEQ = 512
DEPTH = 1

LRU_WIDTH = 512
LRU_BLOCKS = 8
LRU_BD = LRU_WIDTH // LRU_BLOCKS
LRU_C = 8.0
CONV_W = 4
DIFF_HEADS = 4
DIFF_HD = 64
DIFF_QBLK = 128
SWA_HEADS = 8
SWA_KV_HEADS = 2
SWA_GROUP = SWA_HEADS // SWA_KV_HEADS
SWA_HD = 64
WINDOW = 128
SWA_BLK = WINDOW
N_BRANCHES = 3
BRANCH_WIDTH = 512
REL_BUCKETS = 32
REL_MAX_DIST = 128
N_ATTN_HEADS = DIFF_HEADS + SWA_HEADS
N_EXPERTS = 32
TOP_K = 4
D_FF = 1024
SWIGLU_LIMIT = 7.0
SWIGLU_ALPHA = 1.702
MOE_BLK = 128
NORM_EPS = 1e-6
NEG_INF = -1e30

IN_SPLITS = (LRU_WIDTH, LRU_WIDTH,
             DIFF_HEADS * 2 * DIFF_HD, DIFF_HEADS * 2 * DIFF_HD, DIFF_HEADS * 2 * DIFF_HD,
             SWA_HEADS * SWA_HD, SWA_KV_HEADS * SWA_HD, SWA_KV_HEADS * SWA_HD,
             N_BRANCHES * D_MODEL)
IN_WIDTH = sum(IN_SPLITS)


def rms_norm(x, gain):
    xf = x.astype(jnp.float32)
    y = xf * lax.rsqrt(jnp.mean(xf * xf, axis=-1, keepdims=True) + NORM_EPS)
    return (y * gain.astype(jnp.float32)).astype(x.dtype)

def t5_bucket(dist):
    exact = REL_BUCKETS // 2
    is_small = dist < exact
    log_ratio = jnp.log(jnp.maximum(dist, 1).astype(jnp.float32) / exact) / math.log(REL_MAX_DIST / exact)
    large = exact + (log_ratio * (REL_BUCKETS - exact)).astype(jnp.int32)
    return jnp.where(is_small, dist, jnp.minimum(large, REL_BUCKETS - 1))

def rglru_branch(xr, gr, conv_w, conv_b, wa, ba, wx, bx, lam):
    B, S, C = xr.shape
    xp = jnp.pad(xr, ((0, 0), (CONV_W - 1, 0), (0, 0)))
    xc = conv_b + sum(xp[:, tap:tap + S] * conv_w[tap] for tap in range(CONV_W))
    xh = xc.reshape(B, S, LRU_BLOCKS, LRU_BD)
    gate_a = jnp.einsum('bshi,hij->bshj', xh, wa).reshape(B, S, C) + ba
    gate_x = jnp.einsum('bshi,hij->bshj', xh, wx).reshape(B, S, C) + bx
    r = jax.nn.sigmoid(gate_a.astype(jnp.float32))
    i = jax.nn.sigmoid(gate_x.astype(jnp.float32))
    log_a = -LRU_C * r * jax.nn.softplus(-lam.astype(jnp.float32))
    a = jnp.exp(log_a)
    mult = jnp.sqrt(-jnp.expm1(2.0 * log_a))
    b = xc.astype(jnp.float32) * i * mult

    def combine(left, right):
        a1, b1 = left
        a2, b2 = right
        return a1 * a2, a2 * b1 + b2

    _, h = lax.associative_scan(combine, (a, b), axis=1)
    return (h * jax.nn.gelu(gr.astype(jnp.float32), approximate=True)).astype(xr.dtype)

def diff_attention(q, k, v, q_gain, k_gain, lam_vecs, subln_gain, bias_table, lambda_init):
    B, S = q.shape[:2]
    nb = S // DIFF_QBLK
    q = rms_norm(q, q_gain)
    k = rms_norm(k, k_gain)
    lv = lam_vecs.astype(jnp.float32)
    lam = jnp.exp(jnp.sum(lv[0] * lv[1])) - jnp.exp(jnp.sum(lv[2] * lv[3])) + lambda_init
    bias_by_dist = bias_table[t5_bucket(jnp.arange(S))][:, :DIFF_HEADS].astype(jnp.float32)
    k_pos = jnp.arange(S)
    q_blocks = jnp.moveaxis(q.reshape(B, nb, DIFF_QBLK, DIFF_HEADS, 2, DIFF_HD), 1, 0)

    def attend_block(args):
        q_blk, blk = args
        dist = (blk * DIFF_QBLK + jnp.arange(DIFF_QBLK))[:, None] - k_pos[None, :]
        bias = jnp.moveaxis(bias_by_dist[jnp.maximum(dist, 0)], -1, 0)
        s = jnp.einsum('bqhmd,bkhmd->bhmqk', q_blk, k).astype(jnp.float32) * DIFF_HD ** -0.5
        s = jnp.where(dist >= 0, s + bias[None, :, None], NEG_INF)
        p = jax.nn.softmax(s, axis=-1)
        attn = (p[:, :, 0] - lam * p[:, :, 1]).astype(v.dtype)
        return jnp.einsum('bhqk,bkhe->bqhe', attn, v)

    o = lax.map(attend_block, (q_blocks, jnp.arange(nb)))
    o = jnp.moveaxis(o, 0, 1).reshape(B, S, DIFF_HEADS, 2 * DIFF_HD)
    o = rms_norm(o, subln_gain) * (1.0 - lambda_init)
    return o.reshape(B, S, DIFF_HEADS * 2 * DIFF_HD)

def swa_attention(q, k, v, q_gain, k_gain, sinks, bias_table):
    B, S = q.shape[:2]
    nb = S // SWA_BLK
    q = rms_norm(q, q_gain).reshape(B, nb, SWA_BLK, SWA_KV_HEADS, SWA_GROUP, SWA_HD)
    k = rms_norm(k, k_gain).reshape(B, nb, SWA_BLK, SWA_KV_HEADS, SWA_HD)
    v = v.reshape(B, nb, SWA_BLK, SWA_KV_HEADS, SWA_HD)

    def band(t):
        prev = jnp.pad(t, ((0, 0), (1, 0), (0, 0), (0, 0), (0, 0)))[:, :-1]
        return jnp.concatenate([prev, t], axis=2)

    k_band, v_band = band(k), band(v)
    qi = jnp.arange(SWA_BLK)[:, None]
    kj = jnp.arange(2 * SWA_BLK)[None, :]
    dist = SWA_BLK + qi - kj
    in_window = (dist >= 0) & (dist < WINDOW)
    has_prev = (jnp.arange(nb) > 0)[:, None, None] | (kj >= SWA_BLK)[None]
    mask = in_window[None] & has_prev
    bias = bias_table[t5_bucket(jnp.clip(dist, 0, WINDOW - 1))][..., DIFF_HEADS:].astype(jnp.float32)
    bias = bias.reshape(SWA_BLK, 2 * SWA_BLK, SWA_KV_HEADS, SWA_GROUP).transpose(2, 3, 0, 1)
    s = jnp.einsum('bnqhgd,bnkhd->bnhgqk', q, k_band).astype(jnp.float32) * SWA_HD ** -0.5 + bias
    s = jnp.where(mask[None, :, None, None], s, NEG_INF)
    sink = jnp.broadcast_to(sinks.astype(jnp.float32).reshape(SWA_KV_HEADS, SWA_GROUP, 1, 1),
                            s.shape[:-1] + (1,))
    p = jax.nn.softmax(jnp.concatenate([s, sink], axis=-1), axis=-1)[..., :-1]
    o = jnp.einsum('bnhgqk,bnkhd->bnqhgd', p.astype(v.dtype), v_band)
    return o.reshape(B, S, SWA_HEADS * SWA_HD)

def hybrid_mixer(h, w_in, conv_w, conv_b, lru_wa, lru_ba, lru_wx, lru_bx, lru_lambda,
                 diff_qnorm, diff_knorm, diff_lambda, diff_subln,
                 swa_qnorm, swa_knorm, swa_sinks, rel_bias, w_branch, w_out, lambda_init):
    B, S, D = h.shape
    proj = h @ w_in
    offsets = []
    acc = 0
    for width in IN_SPLITS[:-1]:
        acc += width
        offsets.append(acc)
    xr, gr, dq, dk, dv, sq, sk, sv, gl = jnp.split(proj, offsets, axis=-1)
    o_lru = rglru_branch(xr, gr, conv_w, conv_b, lru_wa, lru_ba, lru_wx, lru_bx, lru_lambda)
    o_diff = diff_attention(dq.reshape(B, S, DIFF_HEADS, 2, DIFF_HD),
                            dk.reshape(B, S, DIFF_HEADS, 2, DIFF_HD),
                            dv.reshape(B, S, DIFF_HEADS, 2 * DIFF_HD),
                            diff_qnorm, diff_knorm, diff_lambda, diff_subln, rel_bias, lambda_init)
    o_swa = swa_attention(sq.reshape(B, S, SWA_HEADS, SWA_HD),
                          sk.reshape(B, S, SWA_KV_HEADS, SWA_HD),
                          sv.reshape(B, S, SWA_KV_HEADS, SWA_HD),
                          swa_qnorm, swa_knorm, swa_sinks, rel_bias)
    branches = jnp.stack([o_lru, o_diff, o_swa], axis=2)
    branch_proj = jnp.einsum('bsnc,ncd->bsnd', branches, w_branch)
    gates = jax.nn.sigmoid(gl).reshape(B, S, N_BRANCHES, D)
    merged = jnp.einsum('bsnd,bsnd->bsd', gates, branch_proj)
    return merged @ w_out

def moe_ffn(h, w_router, b_router, w1, b1, w2, b2):
    B, S, D = h.shape
    T = B * S
    xt = h.reshape(T, D)
    logits = xt.astype(jnp.float32) @ w_router.astype(jnp.float32) + b_router.astype(jnp.float32)
    top_v, top_e = lax.top_k(logits, TOP_K)
    weights = jax.nn.softmax(top_v, axis=-1).astype(xt.dtype)
    n_pairs = T * TOP_K
    flat_e = top_e.reshape(-1)
    order = jnp.argsort(flat_e)
    sorted_e = flat_e[order]
    counts = jnp.bincount(flat_e, length=N_EXPERTS)
    starts = jnp.cumsum(counts) - counts
    padded = (counts + MOE_BLK - 1) // MOE_BLK * MOE_BLK
    pad_ends = jnp.cumsum(padded)
    pad_starts = pad_ends - padded
    dest_sorted = pad_starts[sorted_e] + (jnp.arange(n_pairs) - starts[sorted_e])
    n_rows = (n_pairs + MOE_BLK - 1) // MOE_BLK * MOE_BLK + N_EXPERTS * MOE_BLK
    n_blocks = n_rows // MOE_BLK
    row_token = jnp.full((n_rows,), T, jnp.int32).at[dest_sorted].set((order // TOP_K).astype(jnp.int32))
    dest = jnp.zeros_like(order).at[order].set(dest_sorted)
    block_expert = jnp.minimum(jnp.searchsorted(pad_ends, jnp.arange(n_blocks) * MOE_BLK, side='right'),
                               N_EXPERTS - 1)
    x_pad = jnp.concatenate([xt, jnp.zeros((1, D), xt.dtype)], axis=0)

    def expert_block(args):
        tok, e = args
        hcat = x_pad[tok] @ w1[e] + b1[e]
        x_glu = jnp.minimum(hcat[:, ::2], SWIGLU_LIMIT)
        x_lin = jnp.clip(hcat[:, 1::2], -SWIGLU_LIMIT, SWIGLU_LIMIT)
        act = x_glu * jax.nn.sigmoid(SWIGLU_ALPHA * x_glu) * (x_lin + 1.0)
        return act @ w2[e] + b2[e]

    y = lax.map(expert_block, (row_token.reshape(n_blocks, MOE_BLK), block_expert)).reshape(n_rows, D)
    out = jnp.sum(y[dest].reshape(T, TOP_K, D) * weights[..., None], axis=1)
    return out.reshape(B, S, D)

def first_inputs(seed: int = 0) -> dict:
    key = jax.random.key(seed)
    keys = jax.random.split(key, 40)
    counter = [0]

    def next_key():
        k = keys[counter[0]]
        counter[0] += 1
        return k

    def nrm(shape, scale):
        return jax.random.normal(next_key(), shape, jnp.float32) * scale

    L = DEPTH
    D = D_MODEL
    x = nrm((BATCH, SEQ, D), 1.0)
    c = nrm((BATCH, D), 1.0)
    w_ada = nrm((L, D, 6 * D), 0.5 * D ** -0.5)
    b_ada = nrm((L, 6 * D), 0.02)
    norm_mix = 1.0 + nrm((L, D), 0.02)
    norm_ffn = 1.0 + nrm((L, D), 0.02)
    w_in = nrm((L, D, IN_WIDTH), D ** -0.5)
    conv_w = nrm((L, CONV_W, LRU_WIDTH), CONV_W ** -0.5)
    conv_b = nrm((L, LRU_WIDTH), 0.02)
    lru_wa = nrm((L, LRU_BLOCKS, LRU_BD, LRU_BD), LRU_BD ** -0.5)
    lru_ba = nrm((L, LRU_WIDTH), 0.02)
    lru_wx = nrm((L, LRU_BLOCKS, LRU_BD, LRU_BD), LRU_BD ** -0.5)
    lru_bx = nrm((L, LRU_WIDTH), 0.02)
    radius = jax.random.uniform(next_key(), (L, LRU_WIDTH), jnp.float32, 0.9, 0.999)
    lru_lambda = -jnp.log(jnp.expm1(-jnp.log(radius) / LRU_C))
    diff_qnorm = 1.0 + nrm((L, DIFF_HD), 0.02)
    diff_knorm = 1.0 + nrm((L, DIFF_HD), 0.02)
    diff_lambda = nrm((L, 4, DIFF_HD), 0.1)
    diff_subln = 1.0 + nrm((L, 2 * DIFF_HD), 0.02)
    swa_qnorm = 1.0 + nrm((L, SWA_HD), 0.02)
    swa_knorm = 1.0 + nrm((L, SWA_HD), 0.02)
    swa_sinks = nrm((L, SWA_HEADS), 0.5)
    rel_bias = nrm((REL_BUCKETS, N_ATTN_HEADS), 0.5)
    w_branch = nrm((L, N_BRANCHES, BRANCH_WIDTH, D), BRANCH_WIDTH ** -0.5)
    w_out = nrm((L, D, D), D ** -0.5)
    w_router = nrm((L, D, N_EXPERTS), D ** -0.5)
    b_router = nrm((L, N_EXPERTS), 0.01)
    w1 = nrm((L, N_EXPERTS, D, 2 * D_FF), D ** -0.5)
    b1 = nrm((L, N_EXPERTS, 2 * D_FF), 0.02)
    w2 = nrm((L, N_EXPERTS, D_FF, D), D_FF ** -0.5)
    b2 = nrm((L, N_EXPERTS, D), 0.02)
    return {'x': x, 'c': c, 'w_ada': w_ada, 'b_ada': b_ada, 'norm_mix': norm_mix, 'norm_ffn': norm_ffn,
            'w_in': w_in, 'conv_w': conv_w, 'conv_b': conv_b, 'lru_wa': lru_wa, 'lru_ba': lru_ba,
            'lru_wx': lru_wx, 'lru_bx': lru_bx, 'lru_lambda': lru_lambda, 'diff_qnorm': diff_qnorm,
            'diff_knorm': diff_knorm, 'diff_lambda': diff_lambda, 'diff_subln': diff_subln,
            'swa_qnorm': swa_qnorm, 'swa_knorm': swa_knorm, 'swa_sinks': swa_sinks, 'rel_bias': rel_bias,
            'w_branch': w_branch, 'w_out': w_out, 'w_router': w_router, 'b_router': b_router,
            'w1': w1, 'b1': b1, 'w2': w2, 'b2': b2}

def first_block(x, c, w_ada, b_ada, norm_mix, norm_ffn, w_in, conv_w, conv_b, lru_wa, lru_ba,
              lru_wx, lru_bx, lru_lambda, diff_qnorm, diff_knorm, diff_lambda, diff_subln,
              swa_qnorm, swa_knorm, swa_sinks, rel_bias, w_branch, w_out, w_router, b_router,
              w1, b1, w2, b2):
    cond = jax.nn.silu(c)
    for layer in range(DEPTH):
        mod = cond @ w_ada[layer] + b_ada[layer]
        sh_m, sc_m, g_m, sh_f, sc_f, g_f = [m[:, None, :] for m in jnp.split(mod, 6, axis=-1)]
        lambda_init = 0.8 - 0.6 * math.exp(-0.3 * layer)
        h = rms_norm(x, norm_mix[layer]) * (1.0 + sc_m) + sh_m
        x = x + g_m * hybrid_mixer(h, w_in[layer], conv_w[layer], conv_b[layer], lru_wa[layer],
                                   lru_ba[layer], lru_wx[layer], lru_bx[layer], lru_lambda[layer],
                                   diff_qnorm[layer], diff_knorm[layer], diff_lambda[layer],
                                   diff_subln[layer], swa_qnorm[layer], swa_knorm[layer],
                                   swa_sinks[layer], rel_bias, w_branch[layer], w_out[layer],
                                   lambda_init)
        h = rms_norm(x, norm_ffn[layer]) * (1.0 + sc_f) + sh_f
        x = x + g_f * moe_ffn(h, w_router[layer], b_router[layer], w1[layer], b1[layer],
                              w2[layer], b2[layer])
    return x


DN_HEADS = 8
DN_HEAD_DIM = 64
DN_WIDTH = DN_HEADS * DN_HEAD_DIM
DN_CONV = 3
DN_CHUNK = 64
ATT_GROUPS = ((128, 1), (512, 4), (2048, 16))
N_GROUPS = 3
ATT_HEADS_PER_GROUP = 8
ATT_HEAD_DIM = 64
ATT_HEADS = N_GROUPS * ATT_HEADS_PER_GROUP
ATT_WIDTH = ATT_HEADS * ATT_HEAD_DIM
ATT_OUT_WIDTH = ATT_HEADS_PER_GROUP * ATT_HEAD_DIM
ATT_BLOCK = 64
ALIBI_MAX = 8.0
D_FF_2 = 2816
FFN_CONV = 3
IN_PROJ_SIZES = (3 * DN_WIDTH, DN_WIDTH, 2 * DN_HEADS, 2 * DN_HEADS,
                 ATT_WIDTH, ATT_WIDTH, ATT_WIDTH, D_MODEL, D_MODEL)
D_IN_PROJ = 3 * DN_WIDTH + DN_WIDTH + 4 * DN_HEADS + 3 * ATT_WIDTH + 2 * D_MODEL
EPS = 1e-6
NEG_INF_2 = -1e30


def rms_norm_2(x, w):
    xf = x.astype(jnp.float32)
    y = xf * lax.rsqrt(jnp.mean(xf * xf, axis=-1, keepdims=True) + EPS)
    return (y * w.astype(jnp.float32)).astype(x.dtype)

def l2_normalize(t):
    tf = t.astype(jnp.float32)
    return tf * lax.rsqrt(jnp.sum(tf * tf, axis=-1, keepdims=True) + EPS)

def depthwise_conv_centred(x, w):
    width, c = w.shape
    return lax.conv_general_dilated(
        x, w[:, None, :].astype(x.dtype), window_strides=(1,),
        padding=[((width - 1) // 2, width // 2)],
        dimension_numbers=('NWC', 'WIO', 'NWC'), feature_group_count=c)

def alibi_slopes(n):
    return 2.0 ** (-ALIBI_MAX * jnp.arange(1, n + 1, dtype=jnp.float32) / n)

def gated_delta_rule_chunked(q, k, v, g, beta):
    f32 = jnp.float32
    n, h, t, dk = q.shape
    dv = v.shape[-1]
    c = DN_CHUNK
    nc = t // c
    q = q.astype(f32).reshape(n, h, nc, c, dk) * (dk ** -0.5)
    k = k.astype(f32).reshape(n, h, nc, c, dk)
    v = v.astype(f32).reshape(n, h, nc, c, dv)
    beta = beta.astype(f32).reshape(n, h, nc, c)
    g = jnp.cumsum(g.astype(f32).reshape(n, h, nc, c), axis=-1)
    idx = jnp.arange(c)
    incl = idx[:, None] >= idx[None, :]
    strict = idx[:, None] > idx[None, :]
    decay = jnp.exp(jnp.where(incl, g[..., :, None] - g[..., None, :], -jnp.inf))
    kb = k * beta[..., None]
    a_low = jnp.where(strict, jnp.einsum('nhcid,nhcjd->nhcij', kb, k) * decay, 0.0)
    eye = jnp.eye(c, dtype=f32)
    tmat = lax.linalg.triangular_solve(eye + a_low, jnp.broadcast_to(eye, a_low.shape),
                                       left_side=True, lower=True, unit_diagonal=True)
    u = jnp.einsum('nhcij,nhcjv->nhciv', tmat, v * beta[..., None])
    w = jnp.einsum('nhcij,nhcjk->nhcik', tmat, kb * jnp.exp(g)[..., None])
    qk = jnp.einsum('nhcid,nhcjd->nhcij', q, k) * decay
    g_last = g[..., -1]
    q_dec = q * jnp.exp(g)[..., None]
    k_dec = k * jnp.exp(g_last[..., None] - g)[..., None]
    xs = tuple(jnp.moveaxis(arr, 2, 0) for arr in (u, w, qk, q_dec, k_dec, g_last))

    def step(state, inp):
        u_i, w_i, qk_i, qd_i, kd_i, gl_i = inp
        v_new = u_i - jnp.einsum('nhck,nhkv->nhcv', w_i, state)
        o_i = jnp.einsum('nhck,nhkv->nhcv', qd_i, state) + jnp.einsum('nhij,nhjv->nhiv', qk_i, v_new)
        state = state * jnp.exp(gl_i)[..., None, None] + jnp.einsum('nhck,nhcv->nhkv', kd_i, v_new)
        return state, o_i

    _, o = lax.scan(step, jnp.zeros((n, h, dk, dv), f32), xs)
    return jnp.moveaxis(o, 0, 2).reshape(n, h, t, dv)

def dilated_window_attention(q, k, v, slopes, dilation, radius):
    b, s, h, dh = q.shape
    blk = ATT_BLOCK
    sub = s // dilation
    nb = -(-sub // blk)
    lp = nb * blk

    def to_sub(a):
        return a.reshape(b, sub, dilation, h, dh).transpose(0, 2, 3, 1, 4)

    qs = jnp.pad(to_sub(q), ((0, 0),) * 3 + ((0, lp - sub), (0, 0))).reshape(b, dilation, h, nb, blk, dh)

    def windows(a):
        ap = jnp.pad(to_sub(a), ((0, 0),) * 3 + ((blk, lp - sub + blk), (0, 0)))
        ap = ap.reshape(b, dilation, h, nb + 2, blk, dh)
        return jnp.concatenate([ap[:, :, :, 0:nb], ap[:, :, :, 1:nb + 1], ap[:, :, :, 2:nb + 2]], axis=-2)

    kw, vw = windows(k), windows(v)
    blocks = jnp.arange(nb)[:, None, None]
    qi = blocks * blk + jnp.arange(blk)[None, :, None]
    kj = (blocks - 1) * blk + jnp.arange(3 * blk)[None, None, :]
    rel = jnp.abs(qi - kj)
    valid = (rel <= radius) & (kj >= 0) & (kj < sub)
    scores = jnp.einsum('bdhnqe,bdhnke->bdhnqk', qs, kw) * (dh ** -0.5)
    scores = scores - slopes[:, None, None, None] * (rel * dilation).astype(jnp.float32)
    scores = jnp.where(valid, scores, NEG_INF_2)
    m = jnp.max(scores, axis=-1, keepdims=True)
    lse = m + jnp.log(jnp.sum(jnp.exp(scores - m), axis=-1, keepdims=True))
    o = jnp.einsum('bdhnqk,bdhnke->bdhnqe', jnp.exp(scores - lse), vw)
    o = o.reshape(b, dilation, h, lp, dh)[:, :, :, :sub].transpose(0, 3, 1, 2, 4).reshape(b, s, h, dh)
    lse = lse.reshape(b, dilation, h, lp)[..., :sub].transpose(0, 3, 1, 2).reshape(b, s, h)
    return o, lse

def hybrid_block(x, norm1_w, w_in, dn_conv_w, dn_a_log, dn_dt_bias, dn_out_norm_w,
                 attn_q_norm_w, attn_k_norm_w, w_dn_out, w_attn_out, w_o,
                 norm2_w, w_ffn_up, ffn_conv_w, w_ffn_down):
    f32 = jnp.float32
    b, s, _ = x.shape
    h = rms_norm_2(x, norm1_w)
    proj = h @ w_in
    points = np.cumsum(np.array(IN_PROJ_SIZES))[:-1].tolist()
    qkv_a, z_a, a_in, b_in, q_b, k_b, v_b, gate_a, gate_b = jnp.split(proj, points, axis=-1)

    qkv_a = jax.nn.silu(depthwise_conv_centred(qkv_a, dn_conv_w))
    q_a, k_a, v_a = [t.reshape(b, s, DN_HEADS, DN_HEAD_DIM).transpose(0, 2, 1, 3)
                     for t in jnp.split(qkv_a, 3, axis=-1)]
    q_a, k_a = l2_normalize(q_a), l2_normalize(k_a)
    a_dir = a_in.astype(f32).reshape(b, s, 2, DN_HEADS)
    beta = jax.nn.sigmoid(b_in.astype(f32).reshape(b, s, 2, DN_HEADS))
    g = -jnp.exp(dn_a_log.astype(f32)) * jax.nn.softplus(a_dir + dn_dt_bias.astype(f32))
    g = g.transpose(2, 0, 3, 1)
    beta = beta.transpose(2, 0, 3, 1)
    both = lambda t: jnp.concatenate([t, jnp.flip(t, axis=2)], axis=0)
    o2 = gated_delta_rule_chunked(both(q_a), both(k_a), both(v_a),
                                  jnp.concatenate([g[0], jnp.flip(g[1], axis=2)], axis=0),
                                  jnp.concatenate([beta[0], jnp.flip(beta[1], axis=2)], axis=0))
    o_a = (o2[:b] + jnp.flip(o2[b:], axis=2)).transpose(0, 2, 1, 3)
    z = z_a.astype(f32).reshape(b, s, DN_HEADS, DN_HEAD_DIM)
    o_a = rms_norm_2(o_a, dn_out_norm_w) * jax.nn.silu(z)
    y_a = o_a.reshape(b, s, DN_WIDTH).astype(x.dtype) @ w_dn_out

    heads = lambda t: t.astype(f32).reshape(b, s, N_GROUPS, ATT_HEADS_PER_GROUP, ATT_HEAD_DIM)
    q_b = rms_norm_2(heads(q_b), attn_q_norm_w)
    k_b = rms_norm_2(heads(k_b), attn_k_norm_w)
    v_b = heads(v_b)
    slopes = alibi_slopes(ATT_HEADS).reshape(N_GROUPS, ATT_HEADS_PER_GROUP)
    outs, lses = [], []
    for gi, (window, dil) in enumerate(ATT_GROUPS):
        o_g, l_g = dilated_window_attention(q_b[:, :, gi], k_b[:, :, gi], v_b[:, :, gi],
                                            slopes[gi], dil, window // (2 * dil))
        outs.append(o_g)
        lses.append(l_g)
    wts = jax.nn.softmax(jnp.stack(lses), axis=0)
    o_b = jnp.einsum('gbsh,gbshe->bshe', wts, jnp.stack(outs))
    y_b = o_b.reshape(b, s, ATT_OUT_WIDTH).astype(x.dtype) @ w_attn_out

    mixed = jax.nn.sigmoid(gate_a) * y_a + jax.nn.sigmoid(gate_b) * y_b
    x = x + mixed @ w_o

    h2 = rms_norm_2(x, norm2_w)
    gate, up = jnp.split(depthwise_conv_centred(h2 @ w_ffn_up, ffn_conv_w), 2, axis=-1)
    return x + (jax.nn.silu(gate) * up) @ w_ffn_down

def second_inputs(seed: int = 0) -> dict:
    key = jax.random.key(seed)
    ks = jax.random.split(key, 17)
    f32 = jnp.float32
    normal = lambda k, shape, scale: jax.random.normal(k, shape, f32) * scale
    dt = jnp.exp(jax.random.uniform(ks[5], (DEPTH, 2, DN_HEADS), f32, np.log(1e-3), np.log(1e-1)))
    return {
        "x": normal(ks[0], (BATCH, SEQ, D_MODEL), 1.0),
        "norm1_w": 1.0 + normal(ks[1], (DEPTH, D_MODEL), 0.05),
        "w_in": normal(ks[2], (DEPTH, D_MODEL, D_IN_PROJ), D_MODEL ** -0.5),
        "dn_conv_w": normal(ks[3], (DEPTH, DN_CONV, 3 * DN_WIDTH), DN_CONV ** -0.5),
        "dn_a_log": jnp.log(jax.random.uniform(ks[4], (DEPTH, 2, DN_HEADS), f32, 1.0, 16.0)),
        "dn_dt_bias": dt + jnp.log(-jnp.expm1(-dt)),
        "dn_out_norm_w": 1.0 + normal(ks[6], (DEPTH, DN_HEAD_DIM), 0.05),
        "attn_q_norm_w": 1.0 + normal(ks[7], (DEPTH, ATT_HEAD_DIM), 0.05),
        "attn_k_norm_w": 1.0 + normal(ks[8], (DEPTH, ATT_HEAD_DIM), 0.05),
        "w_dn_out": normal(ks[9], (DEPTH, DN_WIDTH, D_MODEL), DN_WIDTH ** -0.5),
        "w_attn_out": normal(ks[10], (DEPTH, ATT_OUT_WIDTH, D_MODEL), ATT_OUT_WIDTH ** -0.5),
        "w_o": normal(ks[11], (DEPTH, D_MODEL, D_MODEL), D_MODEL ** -0.5),
        "norm2_w": 1.0 + normal(ks[12], (DEPTH, D_MODEL), 0.05),
        "w_ffn_up": normal(ks[13], (DEPTH, D_MODEL, 2 * D_FF_2), D_MODEL ** -0.5),
        "ffn_conv_w": normal(ks[14], (DEPTH, FFN_CONV, 2 * D_FF_2), FFN_CONV ** -0.5),
        "w_ffn_down": normal(ks[15], (DEPTH, D_FF_2, D_MODEL), D_FF_2 ** -0.5),
    }

def second_block(x, norm1_w, w_in, dn_conv_w, dn_a_log, dn_dt_bias, dn_out_norm_w,
              attn_q_norm_w, attn_k_norm_w, w_dn_out, w_attn_out, w_o,
              norm2_w, w_ffn_up, ffn_conv_w, w_ffn_down):
    for layer in range(DEPTH):
        x = hybrid_block(x, norm1_w[layer], w_in[layer], dn_conv_w[layer], dn_a_log[layer],
                         dn_dt_bias[layer], dn_out_norm_w[layer], attn_q_norm_w[layer],
                         attn_k_norm_w[layer], w_dn_out[layer], w_attn_out[layer], w_o[layer],
                         norm2_w[layer], w_ffn_up[layer], ffn_conv_w[layer], w_ffn_down[layer])
    return x


def setup_inputs(seed=0):
    out = dict(first_inputs(seed))
    for name, value in second_inputs(seed + 1).items():
        if name != "x":
            out[name + "_2"] = value
    return out


def reference(
    x, c, w_ada, b_ada, norm_mix, norm_ffn, w_in, conv_w, conv_b, lru_wa, lru_ba, lru_wx,
    lru_bx, lru_lambda, diff_qnorm, diff_knorm, diff_lambda, diff_subln, swa_qnorm, swa_knorm,
    swa_sinks, rel_bias, w_branch, w_out, w_router, b_router, w1, b1, w2, b2, norm1_w_2, w_in_2,
    dn_conv_w_2, dn_a_log_2, dn_dt_bias_2, dn_out_norm_w_2, attn_q_norm_w_2, attn_k_norm_w_2,
    w_dn_out_2, w_attn_out_2, w_o_2, norm2_w_2, w_ffn_up_2, ffn_conv_w_2, w_ffn_down_2,
):
    x = first_block(
        x, c, w_ada, b_ada, norm_mix, norm_ffn, w_in, conv_w, conv_b, lru_wa, lru_ba, lru_wx,
        lru_bx, lru_lambda, diff_qnorm, diff_knorm, diff_lambda, diff_subln, swa_qnorm,
        swa_knorm, swa_sinks, rel_bias, w_branch, w_out, w_router, b_router, w1, b1, w2, b2,
    )
    return second_block(
        x, norm1_w_2, w_in_2, dn_conv_w_2, dn_a_log_2, dn_dt_bias_2, dn_out_norm_w_2,
        attn_q_norm_w_2, attn_k_norm_w_2, w_dn_out_2, w_attn_out_2, w_o_2, norm2_w_2,
        w_ffn_up_2, ffn_conv_w_2, w_ffn_down_2,
    )


_drawn_inputs = setup_inputs


def setup_inputs(seed=0):
    import zlib

    import numpy as np

    out = dict(_drawn_inputs(seed))
    spreads = {}
    factors = {'norm_mix': 5.698,
     'norm_ffn': 2.866,
     'conv_b': 3.281,
     'lru_ba': 8.0,
     'lru_bx': 8.0,
     'diff_qnorm': 8.0,
     'diff_knorm': 8.0,
     'diff_lambda': 4.247,
     'diff_subln': 38.121,
     'swa_qnorm': 8.0,
     'swa_knorm': 8.0,
     'swa_sinks': 200.0,
     'b_router': 14.574,
     'b1': 8.0,
     'b2': 42.304,
     'dn_out_norm_w_2': 21.092,
     'attn_q_norm_w_2': 23.759,
     'attn_k_norm_w_2': 22.407,
     'norm2_w_2': 6.488}
    for name, (base, spread) in spreads.items():
        noise = np.random.default_rng([zlib.crc32(name.encode()), seed]).standard_normal(out[name].shape)
        drawn = base * np.exp(spread * noise) if base else spread * noise
        out[name] = jnp.asarray(drawn.astype(out[name].dtype))
    for name, factor in factors.items():
        out[name] = (out[name] * factor).astype(out[name].dtype)
    return out
```

```python
from contextlib import ExitStack, contextmanager
import math

import numpy as np

import concourse.bass as bass
from concourse import mybir

F32 = mybir.dt.float32
U32 = mybir.dt.uint32
I32 = mybir.dt.int32
ACT = mybir.ActivationFunctionType
ALU = mybir.AluOpType
AX = mybir.AxisListType

P = 128
T = 512
TT = T // P
D = 1024
DK = D // P
EPS = 1e-6
NEG = -1e30
BW = 512
BC = BW // P
HD = 64
E = 32
TOPK = 4
DFF = 1024
FFC = 2816 // P
BUCKETS, N_BIAS_HEADS = 32, 12
TOEP = 640
LAMBDA_INIT = 0.8 - 0.6 * math.exp(0.0)
SWA_ORDER = (0, 2, 1, 3)
SLOTS = 6
TILE_F = 4096


def constants():
    c = {}
    eye = np.eye(P, dtype=np.float32)
    i = np.arange(P)
    c["ident"] = eye
    c["flip"] = eye[::-1].copy()
    c["head_sum"] = (i[:, None] // HD == i[None, :] // HD).astype(np.float32)
    c["ones"] = np.ones((P, P), np.float32)
    same = i[:, None] // HD == i[None, :] // HD
    c["cum_f"] = (same & (i[:, None] <= i[None, :])).astype(np.float32)
    c["cum_b"] = (same & (i[:, None] >= i[None, :])).astype(np.float32)
    c["before"] = (i[:, None] < i[None, :]).astype(np.float32)
    c["slot_iota"] = np.broadcast_to(i.astype(np.float32), (P, P)).copy()
    c["ge_mask"] = np.where(same & (i[:, None] >= i[None, :]), 0, NEG).astype(np.float32)
    c["le_mask"] = np.ascontiguousarray(c["ge_mask"].T)
    lev = np.zeros((6, P, P), np.float32)
    for l in range(6):
        b = 1 << l
        lev[l] = (i[:, None] // (2 * b) == i[None, :] // (2 * b)) & (i[:, None] // b % 2 == 1) & (i[None, :] // b % 2 == 0)
    c["join_lo"] = lev.transpose(1, 0, 2).reshape(P, 6 * P).copy()
    c["join_up"] = lev.transpose(2, 0, 1).reshape(P, 6 * P).copy()
    return c


CONST_W = [("ident", P), ("flip", P), ("head_sum", P), ("ones", P), ("cum_f", P), ("cum_b", P), ("before", P),
           ("slot_iota", P), ("ge_mask", P), ("le_mask", P)]
JOIN_W = 12 * P


def t5_bucket_np(dist):
    exact = BUCKETS // 2
    ratio = np.log(np.maximum(dist, 1).astype(np.float32) / exact) / math.log(128 / exact)
    large = exact + (ratio * (BUCKETS - exact)).astype(np.int32)
    return np.where(dist < exact, dist, np.minimum(large, BUCKETS - 1))


def bias_constants():
    dist = 511 - np.arange(TOEP)
    ok = dist >= 0
    onehot = np.zeros((BUCKETS, TOEP), np.float32)
    onehot[t5_bucket_np(np.maximum(dist, 0)), np.arange(TOEP)] = 1.0
    onehot[:, ~ok] = 0
    mask = np.zeros((N_BIAS_HEADS, TOEP), np.float32)
    mask[:, ~ok] = NEG
    mask[4:, dist >= P] = NEG
    return onehot, mask


def alibi_constants():
    slopes = (2.0 ** (-8.0 * np.arange(1, 25, dtype=np.float32) / 24)).astype(np.float32).reshape(3, 8)
    q = np.arange(P)[:, None]
    k = np.arange(3 * P)[None, :] - P
    rel = np.abs(q - k)
    g0 = np.stack([np.where(rel <= 64, -slopes[0, h] * rel.astype(np.float32), NEG) for h in range(8)], 1)
    k = np.arange(P)[None, :]
    rel = np.abs(q - k)
    g1 = np.stack([np.where(rel <= 64, -slopes[1, h] * (rel * 4).astype(np.float32), NEG) for h in range(8)], 1)
    rel = np.abs(q // 4 - k // 4)
    g2 = np.stack([np.where(q % 4 == k % 4, -slopes[2, h] * (rel * 16).astype(np.float32), NEG) for h in range(8)], 1)
    by_parity = [0, 2, 4, 6, 1, 3, 5, 7]
    return [np.ascontiguousarray(x.reshape(P, -1).astype(np.float32)) for x in (g0, g1[:, by_parity], g2[:, by_parity])]


COLS, _at = {}, 0
for _name, _n in [("c", DK), ("norm_mix", DK), ("norm_ffn", DK), ("b_ada", 48), ("conv_w", 4 * BC), ("conv_b", BC),
                  ("lru_ba", BC), ("lru_bx", BC), ("lru_lambda", BC), ("diff_qnorm", 1), ("diff_knorm", 1),
                  ("swa_qnorm", 1), ("swa_knorm", 1), ("diff_subln", 1), ("diff_lambda", 4 * HD), ("swa_sinks", 8),
                  ("b_router", E), ("norm1", DK), ("norm2", DK), ("dn_conv", 36), ("ffn_conv", 132),
                  ("attn_qnorm", 1), ("attn_knorm", 1), ("dn_a_log", 16), ("dn_dt_bias", 16), ("dn_out_norm", HD),
                  ("eps", 1), ("one", 1)]:
    COLS[_name] = (_at, _n)
    _at += _n
NCOLS = _at


def pack_columns(i):
    def col(a):
        return np.asarray(a).reshape(-1, P).T

    def rep(a):
        return np.broadcast_to(np.asarray(a).reshape(1, -1), (P, np.asarray(a).size))

    def taps(a):
        a = np.asarray(a)
        return a.reshape(a.shape[0], -1, P).transpose(2, 1, 0).reshape(P, -1)

    def twice(a):
        return np.concatenate([np.asarray(a).reshape(-1)] * 2).reshape(P, 1)

    parts = {
        "c": col(i["c"]), "norm_mix": col(i["norm_mix"]), "norm_ffn": col(i["norm_ffn"]), "b_ada": col(i["b_ada"]),
        "conv_w": taps(i["conv_w"][0]), "conv_b": col(i["conv_b"]), "lru_ba": col(i["lru_ba"]),
        "lru_bx": col(i["lru_bx"]), "lru_lambda": col(i["lru_lambda"]), "diff_qnorm": twice(i["diff_qnorm"]),
        "diff_knorm": twice(i["diff_knorm"]), "swa_qnorm": twice(i["swa_qnorm"]), "swa_knorm": twice(i["swa_knorm"]),
        "diff_subln": col(i["diff_subln"]), "diff_lambda": rep(i["diff_lambda"]), "swa_sinks": rep(np.asarray(i["swa_sinks"]).reshape(2, 4)[:, list(SWA_ORDER)]),
        "b_router": rep(i["b_router"]), "norm1": col(i["norm1_w_2"]), "norm2": col(i["norm2_w_2"]),
        "dn_conv": taps(i["dn_conv_w_2"][0]), "ffn_conv": taps(i["ffn_conv_w_2"][0]),
        "attn_qnorm": twice(i["attn_q_norm_w_2"]), "attn_knorm": twice(i["attn_k_norm_w_2"]),
        "dn_a_log": rep(i["dn_a_log_2"]), "dn_dt_bias": rep(i["dn_dt_bias_2"]), "dn_out_norm": rep(i["dn_out_norm_w_2"]),
        "eps": np.full((P, 1), EPS, np.float32), "one": np.ones((P, 1), np.float32),
    }
    for name, (_, n) in COLS.items():
        assert parts[name].shape == (P, n), name
    return np.ascontiguousarray(np.concatenate([parts[n] for n in COLS], 1))


def pack_blocks(a):
    a = np.asarray(a)[0]
    out = np.zeros((P, BC, P), np.float32)
    for h in range(8):
        r = HD * (h % 2)
        out[r:r + HD, h // 2, r:r + HD] = a[h]
    return out.reshape(P, -1)


class WeightRing:

    def __init__(self, nc, ctx):
        self.buf = ctx.enter_context(nc.sbuf_tensor("weight_ring", [P, SLOTS, TILE_F], F32))
        self.loaded = [ctx.enter_context(nc.semaphore(f"weights_loaded{s}")) for s in range(SLOTS)]
        self.used = ctx.enter_context(nc.semaphore("weights_used"))
        self.tiles = []
        self.issued = 0
        self.taken = 0
        self.base = 0
        self.slots = SLOTS

    def add(self, source, *dims):
        self.tiles.append((source, dims))

    def add_ffn(self, up, j):
        self.tiles.append(((up, j), (DK, 512)))

    def view(self, slot, dims):
        n = 1
        for d in dims:
            n *= d
        flat = self.buf[:, slot, 0:n]
        if len(dims) == 2:
            return flat.rearrange("p (a b) -> p a b", a=dims[0])
        return flat

    def parts(self, t):
        return 2 if isinstance(self.tiles[t][0], tuple) else 1

    def slot(self, t):
        return (t - self.base) % self.slots

    def load(self, sp, n):
        for _ in range(n):
            if self.issued >= len(self.tiles):
                return
            t = self.issued
            source, dims = self.tiles[t]
            s = self.slot(t)
            if t - self.base >= self.slots:
                sp.wait_ge(self.used, t - self.base - self.slots + 1)
            if isinstance(source, tuple):
                up, j = source
                view = self.view(s, dims).rearrange("p k (g f) -> p k g f", g=2)
                for g in range(2):
                    sp.dma_start(view[:, :, g], up[:, :, g, 256 * j:256 * j + 256]).then_inc(self.loaded[s], 16)
            else:
                sp.dma_start(self.view(s, dims), source).then_inc(self.loaded[s], 16)
            self.issued += 1

    def settle(self, sp):
        for s in range(SLOTS):
            n = sum(self.parts(u) for u in range(self.base, self.issued) if self.slot(u) == s)
            if n:
                sp.wait_ge(self.loaded[s], 16 * n)

    def take(self, pe):
        t = self.taken
        self.taken += 1
        s = self.slot(t)
        count = sum(self.parts(u) for u in range(self.base, t + 1) if self.slot(u) == s)
        pe.wait_ge(self.loaded[s], 16 * count)
        return self.view(s, self.tiles[t][1])


def build(nc, a, out):
    ctx = ExitStack()
    with ctx:
        dma_ok = ctx.enter_context(nc.allow_non_contiguous_dma(reason="weight tiles are strided"))
        ring = WeightRing(nc, ctx)

        def sb(stack, name, shape, dt=F32):
            return stack.enter_context(nc.sbuf_tensor(name, shape, dt))

        x_tok = sb(ctx, "x_tok", [P, TT, D])
        xn_tok = sb(ctx, "xn_tok", [P, TT, D])
        cols = sb(ctx, "cols", [P, NCOLS])
        const_w = sum(n for _, n in CONST_W)
        const = sb(ctx, "const", [P, const_w])
        small = sb(ctx, "small", [P, 64])
        ps = ctx.enter_context(nc.psum_tensor("ps", [P, 8, 512], F32))
        K = {}
        at = 0
        for name, n in CONST_W:
            K[name] = const[:, at:at + n]
            at += n
        ident, head_sum, ones = K["ident"], K["head_sum"], K["ones"]

        def col(name, j=0, n=1):
            base, _ = COLS[name]
            return cols[:, base + j:base + j + n]

        @contextmanager
        def stage(*names):
            with ExitStack() as s:
                sems = [s.enter_context(nc.semaphore(n)) for n in names]
                with nc.Block() as block:
                    yield [block] + sems
                nums = [x.num for x in sems]
                nc.all_engine_barrier(sems_to_clear=range(min(nums), max(nums) + 1))

        def wide(w, c0):
            return w[:, c0:c0 + 512].rearrange("(k p) n -> p k n", p=P)

        def tall(w, r0, k=4):
            return w[r0:r0 + P * k, :].rearrange("(k p) n -> p k n", p=P)

        w_ada, w_in, w_in2 = a["w_ada"][0], a["w_in"][0], a["w_in_2"][0]
        for j in range(12):
            ring.add(wide(w_ada, 512 * j), DK, 512)
        for j in range(6):
            ring.add(wide(w_in, 512 * j), DK, 512)
        ring.add(w_in[:, 3072:3328].rearrange("(k p) n -> p k n", p=P), DK, 256)
        for n in range(3):
            ring.add(tall(a["w_branch"][0, n], 0), BC, D)
            for j in range(2):
                ring.add(wide(w_in, 3328 + 1024 * n + 512 * j), DK, 512)
        for j in range(2):
            ring.add(wide(a["w_out"][0], 512 * j), DK, 512)
        moe_at = len(ring.tiles)

        def expert_tiles(e):
            if isinstance(e, int):
                w1, w2 = a["w1"][0, e], a["w2"][0, e]
            else:
                w1 = a["w1"][0, bass.ds(e, 1)].rearrange("e k n -> (e k) n")
                w2 = a["w2"][0, bass.ds(e, 1)].rearrange("e k n -> (e k) n")
            t = [(w1[256 * j:256 * j + 256, :].rearrange("(k p) n -> p k n", p=P), (2, 2 * DFF)) for j in range(4)]
            return t + [(w2[512 * j:512 * j + 512, :].rearrange("(k p) n -> p k n", p=P), (4, D)) for j in range(2)]

        for src, dims in expert_tiles(0):
            ring.add(src, *dims)
        for j in range(4):
            ring.add(wide(w_in2, 512 * j), DK, 512)
        for g in range(3):
            for j in range(3):
                ring.add(wide(w_in2, 2080 + 1536 * j + 512 * g), DK, 512)
        for w, c0 in (("w_dn_out_2", 6688), ("w_attn_out_2", 7712)):
            ring.add(tall(a[w][0], 0), BC, D)
            for j in range(2):
                ring.add(wide(w_in2, c0 + 512 * j), DK, 512)
        for j in range(2):
            ring.add(wide(a["w_o_2"][0], 512 * j), DK, 512)
        up = a["w_ffn_up_2"][0].rearrange("(k p) (g f) -> p k g f", p=P, g=2)
        for j in range(FFC // 2):
            ring.add_ffn(up, j)
        for j in range(6):
            ring.add(tall(a["w_ffn_down_2"][0], 512 * j, 4 if j < 5 else 2), 4 if j < 5 else 2, D)

        first_block = ctx.enter_context(ExitStack())
        mod_cols = sb(first_block, "mod_cols", [P, 48])
        gate_rows = sb(first_block, "gate_rows", [P, 2, D])
        mod = ctx.enter_context(ExitStack())
        cond = sb(mod, "cond", [P, DK])
        row_buf = sb(mod, "row_buf", [P, 2, 512])
        g_bias = sb(mod, "g_bias", [1, 2, D])
        with stage("small_loaded", "cond_ready", "row_copied", "cols_ready") as (
                block, small_loaded, cond_ready, row_copied, cols_ready):
            @block.sync
            def _(sp):
                sp.dma_start(cols[:, :], a["columns"]).then_inc(small_loaded, 16)
                ring.load(sp, SLOTS + 12)

            @block.gpsimd
            def _(pool):
                pass

            @block.scalar
            def _(act):
                act.dma_start(const[:, :], a["const"]).then_inc(small_loaded, 16)
                act.dma_start(g_bias[:, 0, :], a["b_ada"][0:1, 2048:3072]).then_inc(small_loaded, 16)
                act.dma_start(g_bias[:, 1, :], a["b_ada"][0:1, 5120:6144]).then_inc(small_loaded, 16)
                act.dma_start(x_tok[:, :, :], a["x"][0].rearrange("(t p) d -> p t d", p=P)).then_inc(small_loaded, 16)
                act.wait_ge(small_loaded, 80)
                nc.scalar.activation(cond[:, :], col("c", 0, DK), ACT.Silu).then_inc(cond_ready, 1)
                for j in range(12):
                    act.wait_ge(ring.used, j + 1)
                    if j >= 2:
                        act.wait_ge(cols_ready, j - 1)
                    gate = {4: (0, 0), 5: (0, 1), 10: (1, 0), 11: (1, 1)}.get(j)
                    dst = row_buf[:, j % 2, :] if gate is None else gate_rows[:, gate[0], 512 * gate[1]:512 * gate[1] + 512]
                    nc.scalar.activation(dst, ps[:, j % 2, :], ACT.Copy).then_inc(row_copied, 1)

            @block.tensor
            def _(pe):
                pe.wait_ge(small_loaded, 80)
                pe.wait_ge(cond_ready, 1)

                def pick(j):
                    pe.wait_ge(row_copied, j + 1)
                    src = row_buf[:, j % 2, :]
                    for c in range(4):
                        last = nc.tensor.matmul(ps[:, 2, 4 * j + c:4 * j + c + 1], src[:, P * c:P * c + P] if j not in (4, 5, 10, 11) else ident[:, 0:P],
                                                ident[:, 0:1], start=True, stop=True)
                    last.then_inc(cols_ready, 1)

                for j in range(12):
                    w = ring.take(pe)
                    if j >= 2:
                        pe.wait_ge(row_copied, j - 1)
                    gate = j in (4, 5, 10, 11)
                    if gate:
                        b = g_bias[0:1, 0 if j < 6 else 1, 512 * (j % 2):512 * (j % 2) + 512]
                        nc.tensor.matmul(ps[:, j % 2, :], ones[0:1, :], b, start=True, stop=False)
                    for k in range(DK):
                        last = nc.tensor.matmul(ps[:, j % 2, :], cond[:, k:k + 1].to_broadcast([P, P]), w[:, k, :],
                                                start=(k == 0 and not gate), stop=(k == DK - 1))
                    last.then_inc(ring.used, 1)
                    if j >= 1:
                        pick(j - 1)
                pick(11)

            @block.vector
            def _(dve):
                dve.wait_ge(cols_ready, 12)
                nc.vector.tensor_tensor(mod_cols[:, :], ps[:, 2, 0:48], col("b_ada", 0, 48), ALU.add)
                dve.drain()
                for at_, norm in ((8, "norm_mix"), (32, "norm_ffn")):
                    nc.vector.scalar_tensor_tensor(mod_cols[:, at_:at_ + 8], mod_cols[:, at_:at_ + 8], 1.0,
                                                   col(norm, 0, 8), ALU.add, ALU.mult)
        mod.close()

        def norm_stage(hT, scale, shift):
            with stage("sums_ready", "root_ready", "rows_ready", "turned", "turn_copied") as (
                    block, sums_ready, root_ready, rows_ready, turned, turn_copied):
                @block.scalar
                def _(act):
                    for t in range(TT):
                        nc.scalar.activation(xn_tok[:, t, :], x_tok[:, t, :], ACT.Square, accum_out=small[:, t:t + 1])
                    act.drain()
                    nc.scalar.activation(small[:, 4:8], small[:, 0:4], ACT.Sqrt, scale=1.0 / D, bias=col("eps"))\
                        .then_inc(root_ready, 1)
                    for k in range(DK):
                        act.wait_ge(turned, k + 1)
                        nc.scalar.activation(hT[:, k, :], ps[:, k % 4, :], ACT.Identity, scale=scale(k),
                                             bias=shift(k) if shift else 0.0).then_inc(turn_copied, 1)

                @block.vector
                def _(dve):
                    dve.wait_ge(root_ready, 1)
                    nc.vector.reciprocal(small[:, 8:12], small[:, 4:8])
                    dve.drain()
                    for t in range(TT):
                        nc.vector.tensor_scalar(xn_tok[:, t, :], x_tok[:, t, :], small[:, 8 + t:9 + t], None,
                                                ALU.mult).then_inc(rows_ready, 1)

                @block.tensor
                def _(pe):
                    pe.wait_ge(rows_ready, TT)
                    for k in range(DK):
                        if k >= 4:
                            pe.wait_ge(turn_copied, k - 3)
                        for t in range(TT):
                            last = nc.tensor.transpose(ps[:, k % 4, P * t:P * t + P], xn_tok[:, t, P * k:P * k + P], ident)
                        last.then_inc(turned, 1)

        mixer = ctx.enter_context(ExitStack())
        hT = sb(mixer, "hT", [P, DK, T])
        norm_stage(hT, lambda k: mod_cols[:, 8 + k:9 + k], lambda k: mod_cols[:, k:k + 1])
        def project(hT, tiles, act_scratch):
            groups = [(ti, g) for ti, gs in enumerate(tiles) for g in gs]
            norms = [n for n, (_, g) in enumerate(groups) if g[0] == "norm"]
            with stage("group_ready", "squared", "summed", "rooted", "bank_free0", "bank_free1", "bank_free2",
                       "bank_free3") as (block, group_ready, squared, summed, rooted, *bank_free):
                def freed(eng, n):
                    eng.wait_ge(bank_free[n % 4], n // 4 + 1)

                @block.sync
                def _(sp):
                    ring.load(sp, len(tiles))

                @block.tensor
                def _(pe):
                    def sum_heads(m):
                        pe.wait_ge(squared, m + 1)
                        if m >= 2:
                            pe.wait_ge(rooted, m - 1)
                        nc.tensor.matmul(ps[:, 4 + m % 2, :], head_sum, act_scratch[:, m % 2, :], start=True, stop=True)\
                            .then_inc(summed, 1)

                    n, m = 0, 0
                    for gs in tiles:
                        w = ring.take(pe)
                        for gi, g in enumerate(gs):
                            if n >= 4:
                                freed(pe, n - 4)
                            for k in range(DK):
                                flags = dict(start=(k == 0), stop=(k == DK - 1))
                                if g[0] == "token":
                                    width = g[1].stop - g[1].start
                                    last = nc.tensor.matmul(ps[:, n % 4, 0:width], g[2](k), w[:, k, g[1]], **flags)
                                elif isinstance(g[1], int):
                                    cs = slice(HD * g[1], HD * g[1] + HD)
                                    nc.tensor.matmul(ps[0:HD, n % 4, :], w[:, k, cs], hT[:, k, :], **flags)
                                    last = nc.tensor.matmul(ps[HD:P, n % 4, :], w[:, k, cs], hT[:, k, :], **flags)
                                else:
                                    last = nc.tensor.matmul(ps[:, n % 4, :], w[:, k, g[1]], hT[:, k, :], **flags)
                            last.then_inc(group_ready, 1)
                            n += 1
                            if n >= 2 and groups[n - 2][1][0] == "norm":
                                sum_heads(m)
                                m += 1
                        pe.wait_ge(group_ready, n)
                        nc.tensor.nop().then_inc(ring.used, 1)
                    if groups[-1][1][0] == "norm":
                        sum_heads(m)

                @block.scalar
                def _(act):
                    def root(m):
                        act.wait_ge(summed, m + 1)
                        if m >= 2:
                            freed(act, norms[m - 2])
                        g = groups[norms[m]][1]
                        nc.scalar.activation(act_scratch[:, 2 + m % 2, :], ps[:, 4 + m % 2, :], ACT.Sqrt,
                                             scale=(1.0 / HD if g[4] else 1.0), bias=col("eps")).then_inc(rooted, 1)

                    m, rooted_ = 0, 0
                    for n, (_, g) in enumerate(groups):
                        act.wait_ge(group_ready, n + 1)
                        if g[0] == "norm":
                            if m >= 2:
                                act.wait_ge(summed, m - 1)
                            nc.scalar.activation(act_scratch[:, m % 2, :], ps[:, n % 4, :], ACT.Square).then_inc(squared, 1)
                            m += 1
                        elif g[0] == "chan":
                            nc.scalar.activation(g[3], ps[:, n % 4, :], g[2]).then_inc(bank_free[n % 4], 1)
                        else:
                            nc.scalar.activation(g[4], ps[:, n % 4, 0:g[1].stop - g[1].start], g[3]).then_inc(bank_free[n % 4], 1)
                        if n >= 1 and groups[n - 1][1][0] == "norm":
                            root(rooted_)
                            rooted_ += 1
                    if rooted_ < m:
                        root(rooted_)

                @block.vector
                def _(dve):
                    for m, n in enumerate(norms):
                        _, _, gain, dst, _ = groups[n][1]
                        rinv = act_scratch[:, 2 + m % 2, :]
                        dve.wait_ge(rooted, m + 1)
                        nc.vector.reciprocal(rinv, rinv)
                        dve.drain()
                        if gain is None:
                            ins = nc.vector.tensor_tensor(dst, ps[:, n % 4, :], rinv, ALU.mult)
                        else:
                            ins = nc.vector.scalar_tensor_tensor(dst, ps[:, n % 4, :], gain, rinv, ALU.mult, ALU.mult)
                        ins.then_inc(bank_free[n % 4], 1)

        def chunks(n=4):
            return [slice(P * m, P * m + P) for m in range(n)]

        oT = sb(mixer, "branchesT", [P, 3, BC, T])
        work = sb(mixer, "work", [P, 4096 + 1024])
        x_flat = x_tok[:, :, :].rearrange("p t d -> p (t d)")
        xn_flat = xn_tok[:, :, :].rearrange("p t d -> p (t d)")

        def chan(buf, at_, n=BC, w=T):
            return buf[:, at_:at_ + n * w].rearrange("p (c t) -> p c t", c=n)

        scratch4 = work[:, 0:2048].rearrange("p (a b) -> p a b", a=4)

        XP = T + 4
        xp = chan(x_flat, 0, BC, XP)
        gelu, xc = chan(xn_flat, 0), chan(xn_flat, 2048)
        r_gate, i_gate = oT[:, 1], oT[:, 2]
        a_dec, mult_ = chan(x_flat, 0), chan(x_flat, 2048)
        lru_w = work[:, 2048:3072].rearrange("p (g c j) -> p g c j", g=2, c=BC)
        a_scale = small[:, 16:20]
        project(hT, [[("chan", s, ACT.Copy, xp[:, m, 3:3 + T]) for m, s in enumerate(chunks())],
                     [("chan", s, ACT.Gelu_apprx_tanh, gelu[:, m, :]) for m, s in enumerate(chunks())]], scratch4)
        with stage("lru_loaded", "lam_exp", "lam_abs", "lam_ln", "conv_ready", "gates_ready", "gates_done", "decay_ready",
                   "tanh_ready", "square_ready", "mult_ready") as (
                block, lru_loaded, lam_exp, lam_abs, lam_ln, conv_ready, gates_ready, gates_done, decay_ready,
                tanh_ready, square_ready, mult_ready):
            @block.sync
            def _(sp):
                sp.dma_start(lru_w[:, 0], a["lru_a"].rearrange("p (c j) -> p c j", c=BC)).then_inc(lru_loaded, 16)
                sp.dma_start(lru_w[:, 1], a["lru_x"].rearrange("p (c j) -> p c j", c=BC)).then_inc(lru_loaded, 16)
                sp.wait_ge(lru_loaded, 32)

            @block.vector
            def _(dve):
                nc.vector.scalar_tensor_tensor(small[:, 20:24], col("lru_lambda", 0, BC), -1.0, col("lru_lambda", 0, BC),
                                               ALU.mult, ALU.max).then_inc(lam_abs, 1)
                nc.vector.memset(xp[:, :, 0:3], 0.0)
                dve.drain()
                for c in range(BC):
                    taps = [col("conv_w", 4 * c + k) for k in range(4)]
                    nc.vector.tensor_scalar(xc[:, c, :], xp[:, c, 0:T], taps[0], col("conv_b", c), ALU.mult, ALU.add)
                    for k in range(1, 4):
                        dve.drain()
                        last = nc.vector.scalar_tensor_tensor(xc[:, c, :], xp[:, c, k:k + T], taps[k], xc[:, c, :],
                                                              ALU.mult, ALU.add)
                    last.then_inc(conv_ready, 1)
                dve.wait_ge(lam_exp, 2)
                nc.vector.tensor_scalar(small[:, 24:28], col("lru_lambda", 0, BC), -1.0, 0.0, ALU.mult, ALU.max)
                dve.drain()
                nc.vector.tensor_tensor(small[:, 24:28], small[:, 24:28], small[:, 20:24], ALU.add)
                dve.drain()
                nc.vector.tensor_scalar(a_scale, small[:, 24:28], -8.0, None, ALU.mult).then_inc(lam_ln, 1)
                dve.wait_ge(decay_ready, 1)
                nc.vector.tensor_tensor(xc[:, :, :], xc[:, :, :], i_gate[:, :, :], ALU.mult)
                dve.drain()
                nc.vector.tensor_tensor(i_gate[:, :, :], a_dec[:, :, :], a_dec[:, :, :], ALU.mult)
                dve.wait_ge(tanh_ready, 1)
                dve.drain()
                nc.vector.scalar_tensor_tensor(mult_[:, :, :], i_gate[:, :, :], 1.0, mult_[:, :, :], ALU.add, ALU.mult)\
                    .then_inc(square_ready, 1)
                dve.wait_ge(mult_ready, 1)
                nc.vector.tensor_tensor(xc[:, :, :], xc[:, :, :], mult_[:, :, :], ALU.mult)
                dve.drain()
                for c in range(BC):
                    nc.vector.tensor_tensor_scan(oT[:, 0, c, :], a_dec[:, c, :], xc[:, c, :], 0.0, ALU.mult, ALU.add)
                dve.drain()
                nc.vector.tensor_tensor(oT[:, 0], oT[:, 0], gelu[:, :, :], ALU.mult)

            @block.tensor
            def _(pe):
                pe.wait_ge(lru_loaded, 32)
                for c in range(BC):
                    pe.wait_ge(conv_ready, c + 1)
                    nc.tensor.matmul(ps[:, 2 * c, :], lru_w[:, 0, c, :], xc[:, c, :], start=True, stop=True)
                    nc.tensor.matmul(ps[:, 2 * c + 1, :], lru_w[:, 1, c, :], xc[:, c, :], start=True, stop=True)\
                        .then_inc(gates_ready, 1)

            @block.scalar
            def _(act):
                act.wait_ge(lam_abs, 1)
                nc.scalar.activation(small[:, 20:24], small[:, 20:24], ACT.Exp, scale=-1.0).then_inc(lam_exp, 1)
                act.wait_ge(lam_exp, 1)
                nc.scalar.activation(small[:, 20:24], small[:, 20:24], ACT.Ln, bias=col("one")).then_inc(lam_exp, 1)
                for c in range(BC):
                    act.wait_ge(gates_ready, c + 1)
                    nc.scalar.activation(r_gate[:, c, :], ps[:, 2 * c, :], ACT.Sigmoid, bias=col("lru_ba", c))
                    nc.scalar.activation(i_gate[:, c, :], ps[:, 2 * c + 1, :], ACT.Sigmoid, bias=col("lru_bx", c))
                act.drain()
                act.wait_ge(lam_ln, 1)
                for c in range(BC):
                    last = nc.scalar.activation(a_dec[:, c, :], r_gate[:, c, :], ACT.Exp, scale=a_scale[:, c:c + 1])
                act.drain().then_inc(decay_ready, 1)
                for c in range(BC):
                    nc.scalar.activation(mult_[:, c, :], r_gate[:, c, :], ACT.Tanh, scale=a_scale[:, c:c + 1])
                act.drain().then_inc(tanh_ready, 1)
                act.wait_ge(square_ready, 1)
                nc.scalar.activation(mult_[:, :, :], mult_[:, :, :], ACT.Sqrt, scale=-1.0).then_inc(mult_ready, 1)
        def attention(units, stats, s_buf, p_turned):
            N = len(units)
            at_ = [sum(u["seg"][0] for u in units[:i]) for i in range(N + 1)]

            def seg_view(flat, u):
                n, pitch, w = u["seg"]
                return flat[:, 0:n * pitch].rearrange("p (n w) -> p n w", n=n)[:, :, 0:w]

            s_bank = [ps[:, 2 * b:2 * b + 2, :].rearrange("p b n -> p (b n)") for b in range(2)]
            t_bank = ps[:, 4:6, :].rearrange("p b n -> p (b n)")
            with stage("scores_ready", "scores_read", "maxima_ready", "exps_ready", "probs_ready", "turned", "turned_read",
                       "values_ready", "values_read", "sinks_ready") as (
                    block, scores_ready, scores_read, maxima_ready, exps_ready, probs_ready, turned, turned_read,
                    values_ready, values_read, sinks_ready):
                @block.tensor
                def _(pe):
                    def turn_and_weigh(i):
                        u = units[i]
                        pe.wait_ge(probs_ready, i + 1)
                        if i >= 1:
                            pe.wait_ge(turned_read, i)
                        for j, c in enumerate(u["turns"]):
                            last = nc.tensor.transpose(t_bank[:, P * j:P * j + P], s_buf[:, i % 2, c:c + P], ident)
                        last.then_inc(turned, 1)
                        pe.wait_ge(turned_read, i + 1)
                        if i >= 2:
                            pe.wait_ge(values_read, i - 1)
                        for rows, c, terms in u["pv"]:
                            for n, (v, j) in enumerate(terms):
                                last = nc.tensor.matmul(ps[rows, 6 + i % 2, c:c + P], v, p_turned[:, P * j:P * j + P],
                                                        start=(n == 0), stop=(n == len(terms) - 1))
                        last.then_inc(values_ready, 1)

                    for i, u in enumerate(units):
                        if i >= 2:
                            pe.wait_ge(scores_read, i - 1)
                        for c, w, lhsT, rhs in u["scores"]:
                            last = nc.tensor.matmul(s_bank[i % 2][:, c:c + w], lhsT, rhs, start=True, stop=True)
                        last.then_inc(scores_ready, 1)
                        if i >= 1:
                            turn_and_weigh(i - 1)
                    turn_and_weigh(N - 1)

                @block.scalar
                def _(act):
                    n_sinks = 0
                    for i in range(N + 1):
                        if i < N:
                            u = units[i]
                            n, pitch, w = u["seg"]
                            act.wait_ge(maxima_ready, i + 1)
                            if u.get("sinks") is not None:
                                n_sinks += 1
                                sl = stats[:, 2, at_[i]:at_[i + 1]]
                                nc.scalar.activation(sl, sl, ACT.Exp).then_inc(sinks_ready, 1)
                            for j in range(n):
                                s = s_buf[:, i % 2, pitch * j:pitch * j + w]
                                last = nc.scalar.activation(s, s, ACT.Exp, bias=stats[:, 0, at_[i] + j:at_[i] + j + 1],
                                                            accum_out=stats[:, 1, at_[i] + j:at_[i] + j + 1])
                            act.drain().then_inc(exps_ready, 1)
                        if i >= 1:
                            act.wait_ge(turned, i)
                            if i >= 2:
                                act.wait_ge(values_ready, i - 1)
                            m = P * len(units[i - 1]["turns"])
                            nc.scalar.activation(p_turned[:, 0:m], t_bank[:, 0:m], ACT.Copy).then_inc(turned_read, 1)

                @block.vector
                def _(dve):
                    def read_out(i):
                        dve.wait_ge(values_ready, i + 1)
                        for dst, rows, c in units[i]["out"]:
                            src = ps[rows, 6 + i % 2, c]
                            if len(dst.shape) == 3:
                                src = src.rearrange("p (a b) -> p a b", a=dst.shape[1])
                            last = nc.vector.tensor_copy(dst, src)
                        last.then_inc(values_read, 1)

                    n_sinks = 0
                    for i in range(N + 2):
                        if i < N:
                            u = units[i]
                            n, pitch, w = u["seg"]
                            neg_m = stats[:, 0, at_[i]:at_[i + 1]]
                            dve.wait_ge(scores_ready, i + 1)
                            if i >= 2:
                                dve.wait_ge(turned, i - 1)
                            s = seg_view(s_buf[:, i % 2, :], u)
                            nc.vector.tensor_tensor(s, seg_view(s_bank[i % 2], u), u["bias"], ALU.add).then_inc(scores_read, 1)
                            dve.drain()
                            if u.get("sinks") is None:
                                nc.vector.tensor_reduce(neg_m, s, AX.X, ALU.max, negate=True)
                            else:
                                nc.vector.tensor_reduce(neg_m, s, AX.X, ALU.max)
                                dve.drain()
                                nc.vector.tensor_tensor(neg_m, neg_m, u["sinks"], ALU.max)
                                dve.drain()
                                nc.vector.tensor_scalar(neg_m, neg_m, -1.0, None, ALU.mult)
                                dve.drain()
                                nc.vector.tensor_tensor(stats[:, 2, at_[i]:at_[i + 1]], u["sinks"], neg_m, ALU.add)
                            dve.drain().then_inc(maxima_ready, 1)
                        if 1 <= i <= N:
                            k = i - 1
                            u = units[k]
                            n, pitch, w = u["seg"]
                            sums, recip = stats[:, 1, at_[k]:at_[k + 1]], stats[:, 2, at_[k]:at_[k + 1]]
                            s = seg_view(s_buf[:, k % 2, :], u)
                            dve.wait_ge(exps_ready, k + 1)
                            if u.get("sinks") is not None:
                                n_sinks += 1
                                dve.wait_ge(sinks_ready, n_sinks)
                                nc.vector.tensor_tensor(sums, sums, recip, ALU.add)
                                dve.drain()
                            nc.vector.reciprocal(recip, sums)
                            dve.drain()
                            if u.get("lam") is None:
                                nc.vector.tensor_tensor(s, s, recip.unsqueeze(2).to_broadcast([P, n, w]), ALU.mult)\
                                    .then_inc(probs_ready, 1)
                            else:
                                nc.vector.tensor_tensor(recip[:, 1:2], recip[:, 1:2], u["lam"], ALU.mult)
                                nc.vector.tensor_scalar(s[:, 0, :], s[:, 0, :], recip[:, 0:1], None, ALU.mult)
                                dve.drain()
                                nc.vector.scalar_tensor_tensor(s[:, 0, :], s[:, 1, :], recip[:, 1:2], s[:, 0, :],
                                                               ALU.mult, ALU.add).then_inc(probs_ready, 1)
                        if i >= 2:
                            read_out(i - 2)

        stats = sb(mixer, "stats", [P, 3, 96])
        s_buf = work[:, 0:2048].rearrange("p (a b) -> p a b", a=2)
        p_turned = work[:, 2048:3072]

        dqT, dkT = chan(xn_flat, 0), chan(xn_flat, 2048)
        dv = x_flat[:, 0:2048].rearrange("p (t e) -> p t e", t=TT)
        diff_bias = x_flat[:, 2048:4096].rearrange("p (h x) -> p h x", h=4)
        swa_bias = work[:, 3072:5120].rearrange("p (h x) -> p h x", h=8)
        gains = small[:, 32:34]
        minus_lam = small[:, 34:35]

        def token_groups(dst, width=512):
            return [("token", slice(0, width), (lambda k, t=t: hT[:, k, P * t:P * t + P]), ACT.Copy, dst[:, t, :])
                    for t in range(TT)]

        bias_rows = nc.dram_tensor("bias_rows", (N_BIAS_HEADS, TOEP), F32)
        with stage("bias_loaded", "lam_sums", "lam_exps", "rows_ready", "rows_summed", "rows_stored", "shifted", "flipped") as (
                block, bias_loaded, lam_sums, lam_exps, rows_ready, rows_summed, rows_stored, shifted, flipped):
            onehot, mask = work[0:BUCKETS, 0:TOEP], work[0:N_BIAS_HEADS, 640:1280]
            rel_bias, rows = work[0:BUCKETS, 1280:1280 + N_BIAS_HEADS], work[0:N_BIAS_HEADS, 1408:2048]
            shift_d = xn_flat[:, 0:2048].rearrange("p (h x) -> p h x", h=4)
            shift_s = xn_flat[:, 2048:4096].rearrange("p (h x) -> p h x", h=8)
            half = TOEP // 2

            @block.sync
            def _(sp):
                sp.dma_start(onehot, a["bucket_onehot"]).then_inc(bias_loaded, 16)
                sp.dma_start(mask, a["bucket_mask"]).then_inc(bias_loaded, 16)
                sp.dma_start(rel_bias, a["rel_bias"]).then_inc(bias_loaded, 16)
                sp.wait_ge(rows_summed, 1)
                sp.dma_start(bias_rows.ap(), rows).then_inc(rows_stored, 16)
                sp.wait_ge(rows_stored, 16)
                src = bass.AP(tensor=bias_rows.ap().tensor, offset=0, ap=[[1, P], [TOEP, 4], [1, 512]])
                sp.dma_start(shift_d, src).then_inc(shifted, 16)
                src = bass.AP(tensor=bias_rows.ap().tensor, offset=4 * TOEP + 256, ap=[[1, P], [TOEP, 8], [1, 256]])
                sp.dma_start(shift_s, src).then_inc(shifted, 16)

            @block.tensor
            def _(pe):
                pe.wait_ge(bias_loaded, 48)
                for j in range(2):
                    last = nc.tensor.matmul(ps[0:N_BIAS_HEADS, j, 0:half], rel_bias, onehot[:, half * j:half * j + half],
                                            start=True, stop=True)
                last.then_inc(rows_ready, 1)
                pe.wait_ge(rows_summed, 1)
                pe.wait_ge(shifted, 32)
                for j in range(8):
                    src = shift_d[:, j, :] if j < 4 else shift_s[:, 2 * j - 8:2 * j - 6, :]
                    nc.tensor.matmul(ps[:, j, :], K["flip"], src, start=True, stop=True).then_inc(flipped, 1)

            @block.scalar
            def _(act):
                act.wait_ge(lam_sums, 1)
                nc.scalar.activation(small[:, 36:38], small[:, 36:38], ACT.Exp).then_inc(lam_exps, 1)
                for j in range(4):
                    act.wait_ge(flipped, j + 1)
                    nc.scalar.activation(diff_bias[:, j, :], ps[:, j, :], ACT.Copy)

            @block.vector
            def _(dve):
                nc.vector.tensor_scalar(gains[:, 0:1], col("diff_qnorm"), HD ** -0.5, None, ALU.mult)
                nc.vector.tensor_scalar(gains[:, 1:2], col("swa_qnorm"), HD ** -0.5, None, ALU.mult)
                lv = [col("diff_lambda", HD * j, HD) for j in range(4)]
                prod = work[:, 3072:3072 + 2 * HD].rearrange("p (a b) -> p a b", a=2)
                nc.vector.tensor_tensor(prod[:, 0, :], lv[0], lv[1], ALU.mult)
                nc.vector.tensor_tensor(prod[:, 1, :], lv[2], lv[3], ALU.mult)
                dve.drain()
                nc.vector.tensor_reduce(small[:, 36:38], prod, AX.X, ALU.add).then_inc(lam_sums, 1)
                dve.wait_ge(rows_ready, 1)
                for j in range(2):
                    last = nc.vector.tensor_tensor(rows[:, half * j:half * j + half], ps[0:N_BIAS_HEADS, j, 0:half],
                                                   mask[:, half * j:half * j + half], ALU.add)
                dve.drain().then_inc(rows_summed, 1)
                dve.wait_ge(lam_exps, 1)
                nc.vector.tensor_tensor(minus_lam, small[:, 37:38], small[:, 36:37], ALU.subtract)
                dve.drain()
                nc.vector.tensor_scalar(minus_lam, minus_lam, -LAMBDA_INIT, None, ALU.add)
                for j in range(4, 8):
                    dve.wait_ge(flipped, j + 1)
                    nc.vector.tensor_copy(swa_bias[:, 2 * j - 8:2 * j - 6, :], ps[:, j, :].rearrange("p (h x) -> p h x", h=2))

        project(hT, [[("norm", s, gains[:, 0:1], dqT[:, m, :], True) for m, s in enumerate(chunks())],
                     [("norm", s, col("diff_knorm"), dkT[:, m, :], True) for m, s in enumerate(chunks())],
                     token_groups(dv)], scratch4)
        units = []
        for h in range(4):
            for t in range(TT):
                w = P * (t + 1)
                units.append(dict(
                    scores=[(512 * m, w, dqT[HD * m:HD * m + HD, h, P * t:P * t + P], dkT[HD * m:HD * m + HD, h, 0:w]) for m in range(2)],
                    seg=(2, 512, w), lam=minus_lam,
                    bias=diff_bias[:, h, P * (3 - t):512].unsqueeze(1).to_broadcast([P, 2, w]),
                    turns=[P * j for j in range(t + 1)],
                    pv=[(slice(0, P), 0, [(dv[:, j, P * h:P * h + P], j) for j in range(t + 1)])],
                    out=[(oT[:, 1, h, P * t:P * t + P], slice(0, P), slice(0, P))]))
        attention(units, stats, s_buf, p_turned)

        with stage("squared", "summed", "rooted") as (block, squared, summed, rooted):
            @block.tensor
            def _(pe):
                for h in range(4):
                    pe.wait_ge(squared, h + 1)
                    nc.tensor.matmul(ps[:, h, :], ones, scratch4[:, h, :], start=True, stop=True).then_inc(summed, 1)

            @block.scalar
            def _(act):
                for h in range(4):
                    nc.scalar.activation(scratch4[:, h, :], oT[:, 1, h, :], ACT.Square).then_inc(squared, 1)
                for h in range(4):
                    act.wait_ge(summed, h + 1)
                    nc.scalar.activation(scratch4[:, h, :], ps[:, h, :], ACT.Sqrt, scale=1.0 / P, bias=col("eps")).then_inc(rooted, 1)

            @block.vector
            def _(dve):
                nc.vector.tensor_scalar(small[:, 40:41], col("diff_subln"), 1.0 - LAMBDA_INIT, None, ALU.mult)
                for h in range(4):
                    dve.wait_ge(rooted, h + 1)
                    nc.vector.reciprocal(scratch4[:, h, :], scratch4[:, h, :])
                    dve.drain()
                    nc.vector.scalar_tensor_tensor(oT[:, 1, h, :], oT[:, 1, h, :], small[:, 40:41], scratch4[:, h, :],
                                                   ALU.mult, ALU.mult)

        sqT = chan(xn_flat, 0)
        skT = chan(xn_flat, 2048, 2)
        sv = xn_flat[:, 3072:3584].rearrange("p (t e) -> p t e", t=TT)
        scratch_x = x_flat[:, 0:2048].rearrange("p (a b) -> p a b", a=4)
        project_tiles = [[("norm", s, gains[:, 1:2], sqT[:, m, :], True) for m, s in enumerate(chunks())],
                         [("norm", g, col("swa_knorm"), skT[:, g, :], True) for g in range(2)] +
                         [("token", slice(P, 2 * P), (lambda k, t=t: hT[:, k, P * t:P * t + P]), ACT.Copy, sv[:, t, :])
                          for t in range(TT)]]
        project(hT, project_tiles, scratch_x)
        units = []
        for t in range(TT):
            for g in range(2):
                w = 2 * P if t else P
                k0 = P * (t - 1) if t else 0
                sc, pv, o = [], [], []
                for j in range(4):
                    h = 4 * g + SWA_ORDER[j]
                    r = slice(HD * (h % 2), HD * (h % 2) + HD)
                    sc.append((2 * P * j, w, sqT[r, h // 2, P * t:P * t + P], skT[r, g, k0:k0 + w]))
                    nt = w // P
                    pv.append((r, P * (SWA_ORDER[j] // 2), [(sv[:, (t - 1 if t else 0) + m, HD * g:HD * g + HD], nt * j + m) for m in range(nt)]))
                units.append(dict(
                    scores=sc, seg=(4, 2 * P, w), bias=swa_bias[:, 4 * g:4 * g + 4, 2 * P - w:2 * P],
                    sinks=col("swa_sinks", 4 * g, 4), turns=[2 * P * j + P * m for j in range(4) for m in range(w // P)],
                    pv=pv, out=[(oT[:, 2, 2 * g:2 * g + 2, P * t:P * t + P], slice(0, P), slice(0, 2 * P))]))
        attention(units, stats, s_buf, p_turned)
        def merge_branches(hT, sources, mergedT, sig, gated, load_x=False):
            NI = DK * len(sources)
            with stage("gate_ready", "branch_ready", "sig_ready", "merged", "x_loaded") as (
                    block, gate_ready, branch_ready, sig_ready, merged, x_loaded):
                @block.sync
                def _(sp):
                    if load_x:
                        sp.dma_start(x_tok[:, :, :], a["x"][0].rearrange("(t p) d -> p t d", p=P)).then_inc(x_loaded, 16)
                    ring.load(sp, 3 * len(sources))
                    if load_x:
                        sp.wait_ge(x_loaded, 16)

                @block.tensor
                def _(pe):
                    i = 0
                    for n in range(len(sources)):
                        wb = ring.take(pe)
                        for j in range(2):
                            wg = ring.take(pe)
                            for m in range(4):
                                if i >= 4:
                                    pe.wait_ge(sig_ready, i - 3)
                                for k in range(DK):
                                    last = nc.tensor.matmul(ps[:, i % 4, :], wg[:, k, P * m:P * m + P], hT[:, k, :],
                                                            start=(k == 0), stop=(k == DK - 1))
                                last.then_inc(gate_ready, 1)
                                if i >= 4:
                                    pe.wait_ge(merged, i - 3)
                                for k in range(BC):
                                    last = nc.tensor.matmul(ps[:, 4 + i % 4, :], wb[:, k, 512 * j + P * m:512 * j + P * m + P],
                                                            sources[n][:, k, :], start=(k == 0), stop=(k == BC - 1))
                                last.then_inc(branch_ready, 1)
                                i += 1
                        pe.wait_ge(branch_ready, i)
                        nc.tensor.nop().then_inc(ring.used, 3)

                @block.scalar
                def _(act):
                    for i in range(NI):
                        act.wait_ge(gate_ready, i + 1)
                        if i >= 2:
                            act.wait_ge(merged, i - 1)
                        nc.scalar.activation(sig[:, i % 2, :], ps[:, i % 4, :], ACT.Sigmoid).then_inc(sig_ready, 1)

                @block.vector
                def _(dve):
                    for i in range(NI):
                        n, m = i // 8, i % 8
                        dve.wait_ge(branch_ready, i + 1)
                        dve.wait_ge(sig_ready, i + 1)
                        dst = mergedT[:, m, :] if n == 0 else gated[:, i % 2, :]
                        ins = nc.vector.tensor_tensor(dst, sig[:, i % 2, :], ps[:, 4 + i % 4, :], ALU.mult)
                        ins.then_inc(merged, 1)
                        if n:
                            dve.drain()
                            nc.vector.tensor_tensor(mergedT[:, m, :], mergedT[:, m, :], gated[:, i % 2, :], ALU.add)

        merge_branches(hT, [oT[:, n] for n in range(3)], chan(xn_flat, 0, DK), work[:, 0:1024].rearrange("p (a b) -> p a b", a=2),
                       work[:, 1024:2048].rearrange("p (a b) -> p a b", a=2), load_x=True)

        def project_out(srcT, nk, gate, tiles=2):
            with stage("out_ready", "out_added") as (block, out_ready, out_added):
                @block.sync
                def _(sp):
                    ring.load(sp, 2)

                @block.tensor
                def _(pe):
                    for j in range(2):
                        w = ring.take(pe)
                        for t in range(TT):
                            for k in range(nk):
                                last = nc.tensor.matmul(ps[:, 4 * j + t, :], srcT[:, k, P * t:P * t + P], w[:, k, :],
                                                        start=(k == 0), stop=(k == nk - 1))
                            last.then_inc(out_ready, 1)
                        pe.wait_ge(out_ready, 4 * j + 4)
                        nc.tensor.nop().then_inc(ring.used, 1)

                @block.vector
                def _(dve):
                    for j in range(2):
                        for t in range(TT):
                            x = x_tok[:, t, 512 * j:512 * j + 512]
                            dve.wait_ge(out_ready, 4 * j + t + 1)
                            src = ps[:, 4 * j + t, :]
                            if gate is not None:
                                src = work[:, 512 * t:512 * t + 512]
                                nc.vector.tensor_tensor(src, ps[:, 4 * j + t, :], gate[:, 512 * j:512 * j + 512], ALU.mult)
                                dve.drain()
                            nc.vector.tensor_tensor(x, x, src, ALU.add)

        project_out(chan(xn_flat, 0, DK), DK, gate_rows[:, 0, :])
        mixer.close()
        moe = ctx.enter_context(ExitStack())
        acc = sb(moe, "moe_acc", [P, TT, D])
        weight_te = sb(moe, "weight_te", [P, TT, E])
        slot_te = sb(moe, "slot_te", [P, TT, E + 1])
        most = sb(moe, "most_tokens", [P, 1], I32)
        router = ctx.enter_context(ExitStack())
        hfT = sb(router, "hfT", [P, DK, T])
        norm_stage(hfT, lambda k: mod_cols[:, 32 + k:33 + k], lambda k: mod_cols[:, 24 + k:25 + k])
        w_router = sb(router, "w_router", [P, DK, E])
        b2_sb = sb(router, "b2_sb", [E, D])
        logits = sb(router, "logits", [P, TT, E])
        chosen = sb(router, "chosen", [P, TT, E])
        hot = sb(router, "hot", [P, 2, TT, E])
        top = sb(router, "top", [P, TT, 8])
        top_at = sb(router, "top_at", [P, TT, 8], U32)
        top_atf = sb(router, "top_atf", [P, TT, 8])
        soft = sb(router, "soft", [P, TT, TOPK])
        weight_et = sb(router, "weight_et", [E, T])
        iota_e = K["slot_iota"][:, 0:E].unsqueeze(1).to_broadcast([P, TT, E])
        with stage("router_loaded", "logits_ready", "tops_ready", "exps_ready", "chosen_ready", "places_ready", "places_read",
                   "turned", "turned_read", "init_ready", "init_read") as (
                block, router_loaded, logits_ready, tops_ready, exps_ready, chosen_ready, places_ready, places_read,
                turned, turned_read, init_ready, init_read):
            @block.sync
            def _(sp):
                sp.dma_start(w_router[:, :, :], a["w_router"][0].rearrange("(k p) e -> p k e", p=P)).then_inc(router_loaded, 16)
                sp.dma_start(b2_sb[:, :], a["b2"][0]).then_inc(router_loaded, 16)
                sp.wait_ge(router_loaded, 32)

            @block.tensor
            def _(pe):
                pe.wait_ge(router_loaded, 32)
                for t in range(TT):
                    for k in range(DK):
                        last = nc.tensor.matmul(ps[:, 0, E * t:E * t + E], hfT[:, k, P * t:P * t + P], w_router[:, k, :],
                                                start=(k == 0), stop=(k == DK - 1))
                last.then_inc(logits_ready, 1)
                pe.wait_ge(chosen_ready, 1)
                for t in range(TT):
                    for s in range(t + 1):
                        nc.tensor.matmul(ps[:, 1, E * t:E * t + E], K["before"] if s == t else ones, chosen[:, s, :],
                                         start=(s == 0), stop=(s == t))
                for s in range(TT):
                    last = nc.tensor.matmul(ps[:, 1, E * TT:E * TT + E], ones, chosen[:, s, :], start=(s == 0), stop=(s == TT - 1))
                last.then_inc(places_ready, 1)
                for t in range(TT):
                    last = nc.tensor.transpose(ps[0:E, 2, P * t:P * t + P], weight_te[:, t, :], ident)
                last.then_inc(turned, 1)
                pe.wait_ge(turned_read, 1)
                pe.wait_ge(places_read, 1)
                for t in range(TT):
                    for j in range(2):
                        nc.tensor.matmul(ps[:, 2 * t + j, :], weight_et[:, P * t:P * t + P], b2_sb[:, 512 * j:512 * j + 512],
                                         start=True, stop=True).then_inc(init_ready, 1)

            @block.scalar
            def _(act):
                act.wait_ge(tops_ready, 1)
                nc.scalar.activation(soft[:, :, :], soft[:, :, :], ACT.Exp).then_inc(exps_ready, 1)
                act.wait_ge(turned, 1)
                nc.scalar.activation(weight_et[:, :], ps[0:E, 2, :], ACT.Copy).then_inc(turned_read, 1)
                for t in range(TT):
                    act.wait_ge(init_ready, 2 * t + 2)
                    nc.scalar.activation(acc[:, t, :], ps[:, 2 * t:2 * t + 2, :].rearrange("p b n -> p (b n)"), ACT.Copy)

            @block.vector
            def _(dve):
                nc.vector.memset(weight_te[:, :, :], 0.0)
                nc.vector.memset(chosen[:, :, :], 0.0)
                nc.vector.memset(slot_te[:, :, :], -1.0)
                dve.wait_ge(logits_ready, 1)
                nc.vector.tensor_tensor(logits[:, :, :], ps[:, 0, 0:E * TT].rearrange("p (t e) -> p t e", t=TT),
                                        col("b_router", 0, E).unsqueeze(1).to_broadcast([P, TT, E]), ALU.add)
                dve.drain()
                for t in range(TT):
                    nc.vector.max(top[:, t, :], logits[:, t, :])
                dve.drain()
                for t in range(TT):
                    nc.vector.max_index(top_at[:, t, :], top[:, t, :], logits[:, t, :])
                nc.vector.tensor_tensor(soft[:, :, :], top[:, :, 0:TOPK], top[:, :, 0:1].to_broadcast([P, TT, TOPK]), ALU.subtract)
                dve.drain().then_inc(tops_ready, 1)
                nc.vector.tensor_copy(top_atf[:, :, :], top_at[:, :, :])
                dve.wait_ge(exps_ready, 1)
                nc.vector.tensor_reduce(small[:, 0:TT], soft[:, :, :], AX.X, ALU.add)
                dve.drain()
                nc.vector.reciprocal(small[:, 4:4 + TT], small[:, 0:TT])
                dve.drain()
                nc.vector.tensor_tensor(soft[:, :, :], soft[:, :, :], small[:, 4:4 + TT].unsqueeze(2).to_broadcast([P, TT, TOPK]), ALU.mult)
                dve.drain()
                for j in range(TOPK):
                    nc.vector.tensor_tensor(hot[:, 0], iota_e, top_atf[:, :, j:j + 1].to_broadcast([P, TT, E]), ALU.is_equal)
                    dve.drain()
                    nc.vector.tensor_tensor(chosen[:, :, :], chosen[:, :, :], hot[:, 0], ALU.add)
                    nc.vector.tensor_tensor(hot[:, 1], hot[:, 0], soft[:, :, j:j + 1].to_broadcast([P, TT, E]), ALU.mult)
                    dve.drain()
                    nc.vector.tensor_tensor(weight_te[:, :, :], weight_te[:, :, :], hot[:, 1], ALU.add)
                    dve.drain()
                dve.drain().then_inc(chosen_ready, 1)
                dve.wait_ge(places_ready, 1)
                places = ps[:, 1, 0:E * TT].rearrange("p (t e) -> p t e", t=TT)
                nc.vector.scalar_tensor_tensor(slot_te[:, :, 0:E], places, 1.0, chosen[:, :, :], ALU.add, ALU.mult)
                nc.vector.tensor_reduce(small[:, 12:13], ps[:, 1, E * TT:E * TT + E], AX.X, ALU.max)
                dve.drain()
                nc.vector.tensor_scalar(slot_te[:, :, 0:E], slot_te[:, :, 0:E], -1.0, None, ALU.add)
                nc.vector.tensor_copy(most[:, :], small[:, 12:13])
                dve.drain().then_inc(places_read, 1)
        router.close()

        xgT = sb(moe, "gathered_T", [P, DK, P])
        b1_row = sb(moe, "b1_row", [1, 2 * DFF])
        pick_g = sb(moe, "pick_g", [P, TT, P])
        pick_w = sb(moe, "pick_w", [P, TT, P])
        pick_wT = sb(moe, "pick_wT", [P, T])
        slot_col = sb(moe, "slot_col", [P, 2, TT])
        weight_col = sb(moe, "weight_col", [P, TT])
        glu = sb(moe, "glu", [P, DFF])
        sig_glu = sb(moe, "sig_glu", [P, DFF])
        lin = sb(moe, "lin", [P, DFF])
        hidT = sb(moe, "hiddenT", [P, DK, P])
        y_sb = sb(moe, "expert_out", [P, D])
        LIMIT, ALPHA = 7.0, 1.702

        def experts_pass(rounds, prefetched):
            load0 = sum(1 for u in range(ring.base, moe_at) if u % SLOTS == 0) if prefetched else 0
            used0 = moe_at - ring.base if prefetched else SLOTS

            @contextmanager
            def turns(eng, prologue=None):
                if rounds:
                    with eng.Fori(0, rounds) as r:
                        if prologue:
                            prologue(r * (E + 1))
                        with eng.Fori(0, E) as e:
                            yield r * E + e, r * (E + 1) + e, e
                else:
                    if prologue:
                        prologue(0)
                    with eng.Fori(0, E) as e:
                        yield e, e, e

            @contextmanager
            def when_needed(eng):
                if rounds:
                    n = eng.value_load(most[0:1, 0:1], min_val=0, max_val=T)
                    with eng.If(n > P):
                        yield
                else:
                    yield

            with stage("picked", "gathered", "xg_ready", "glu_ready", "sig_ready", "hidden_ready", "turned", "turned_read",
                       "pick_w_ready", "pick_turned", "pick_read", "y_read", "combined", "added", "b1_loaded") as (
                    block, picked, gathered, xg_ready, glu_ready, sig_ready, hidden_ready, turned, turned_read,
                    pick_w_ready, pick_turned, pick_read, y_read, combined, added, b1_loaded):
                @block.sync
                def _(sp):
                    b1 = a["b1"][0]
                    with when_needed(sp):
                        if prefetched:
                            sp.dma_start(b1_row[:, :], b1[0:1, :]).then_inc(b1_loaded, 16)
                            with sp.Fori(0, E - 1) as e:
                                for j, (src, dims) in enumerate(expert_tiles(e + 1)):
                                    sp.wait_ge(ring.used, e * SLOTS + (used0 + j + 1))
                                    sp.dma_start(ring.view(j, dims), src).then_inc(ring.loaded[j], 16)
                                    if j == 0:
                                        sp.dma_start(b1_row[:, :], b1[bass.ds(e + 1, 1), :]).then_inc(b1_loaded, 16)
                        else:
                            with turns(sp) as (i, g, e):
                                for j, (src, dims) in enumerate(expert_tiles(e)):
                                    sp.wait_ge(ring.used, i * SLOTS + (j + 1))
                                    sp.dma_start(ring.view(j, dims), src).then_inc(ring.loaded[j], 16)
                                    if j == 0:
                                        sp.dma_start(b1_row[:, :], b1[bass.ds(e, 1), :]).then_inc(b1_loaded, 16)

                @block.tensor
                def _(pe):
                    def gather(n):
                        pe.wait_ge(picked, n)
                        for c in range(DK):
                            for t in range(TT):
                                last = nc.tensor.matmul(ps[:, 4 + c // 4, P * (c % 4):P * (c % 4) + P],
                                                        xn_tok[:, t, P * c:P * c + P], pick_g[:, t, :],
                                                        start=(t == 0), stop=(t == TT - 1))
                        last.then_inc(gathered, 1)

                    def first(g):
                        gather(g + 1)

                    with when_needed(pe):
                        if not prefetched:
                            nc.tensor.nop().then_inc(ring.used, SLOTS)
                        with turns(pe, first) as (i, g, e):
                            pe.wait_ge(xg_ready, g + 1)
                            pe.wait_ge(b1_loaded, i * 16 + 16)
                            pe.wait_ge(added, i * 8 + 1)
                            for n in range(4):
                                nc.tensor.matmul(ps[:, n, :], ones[0:1, :], b1_row[0:1, 512 * n:512 * n + 512], start=True, stop=False)
                            for j in range(4):
                                pe.wait_ge(ring.loaded[j], i * 16 + (16 * load0 + 16))
                                w = ring.view(j, (2, 2 * DFF))
                                for k in range(2):
                                    for n in range(4):
                                        last = nc.tensor.matmul(ps[:, n, :], xgT[:, 2 * j + k, :], w[:, k, 512 * n:512 * n + 512],
                                                                start=False, stop=(j == 3 and k == 1))
                                last.then_inc(ring.used, 1)
                            gather(g + 2)
                            for s in range(2):
                                pe.wait_ge(hidden_ready, i * 2 + (s + 1))
                                for c in range(4):
                                    last = nc.tensor.transpose(ps[:, 6 + s, P * c:P * c + P], lin[:, 512 * s + P * c:512 * s + P * c + P], ident)
                                last.then_inc(turned, 1)
                            pe.wait_ge(xg_ready, g + 2)
                            pe.wait_ge(turned_read, i * 2 + 2)
                            for j in range(2):
                                pe.wait_ge(ring.loaded[4 + j], i * 16 + (16 * load0 + 16))
                                w = ring.view(4 + j, (4, D))
                                for k in range(4):
                                    for n in range(2):
                                        last = nc.tensor.matmul(ps[:, 4 + n, :], hidT[:, 4 * j + k, :], w[:, k, 512 * n:512 * n + 512],
                                                                start=(j == 0 and k == 0), stop=(j == 1 and k == 3))
                                last.then_inc(ring.used, 1)
                                if j == 0:
                                    pe.wait_ge(pick_w_ready, i + 1)
                                    for t in range(TT):
                                        last = nc.tensor.transpose(ps[:, 6, P * t:P * t + P], pick_w[:, t, :], ident)
                                    last.then_inc(pick_turned, 1)
                            pe.wait_ge(pick_read, i + 1)
                            pe.wait_ge(y_read, i + 1)
                            for o in range(8):
                                if o >= 4:
                                    pe.wait_ge(added, i * 8 + (o - 4 + 2))
                                nc.tensor.matmul(ps[:, o % 4, :], pick_wT[:, P * (o // 2):P * (o // 2) + P],
                                                 y_sb[:, 512 * (o % 2):512 * (o % 2) + 512], start=True, stop=True).then_inc(combined, 1)

                @block.scalar
                def _(act):
                    def modulate(n):
                        act.wait_ge(gathered, n)
                        for c in range(DK):
                            nc.scalar.activation(xgT[:, c, :], ps[:, 4 + c // 4, P * (c % 4):P * (c % 4) + P], ACT.Identity,
                                                 scale=mod_cols[:, 32 + c:33 + c], bias=mod_cols[:, 24 + c:25 + c])
                        act.drain().then_inc(xg_ready, 1)

                    with when_needed(act):
                        with turns(act, lambda g: modulate(g + 1)) as (i, g, e):
                            for s in range(2):
                                act.wait_ge(glu_ready, i * 2 + (s + 1))
                                nc.scalar.activation(sig_glu[:, 512 * s:512 * s + 512], glu[:, 512 * s:512 * s + 512], ACT.Sigmoid,
                                                     scale=ALPHA).then_inc(sig_ready, 1)
                            modulate(g + 2)
                            for s in range(2):
                                act.wait_ge(turned, i * 2 + (s + 1))
                                nc.scalar.activation(hidT[:, 4 * s:4 * s + 4, :], ps[:, 6 + s, :].rearrange("p (c n) -> p c n", c=4),
                                                     ACT.Copy).then_inc(turned_read, 1)
                            act.wait_ge(pick_turned, i + 1)
                            nc.scalar.activation(pick_wT[:, :], ps[:, 6, :], ACT.Copy).then_inc(pick_read, 1)
                            act.wait_ge(ring.used, i * SLOTS + (used0 + 6))
                            nc.scalar.activation(y_sb[:, :], ps[:, 4:6, :].rearrange("p b n -> p (b n)"), ACT.Copy).then_inc(y_read, 1)

                @block.vector
                def _(dve):
                    def pick_next(e, n):
                        nc.vector.tensor_copy(slot_col[:, 0, :], slot_te[:, :, bass.ds(e, 1)].rearrange("p t e -> p (t e)"))
                        dve.drain()
                        for t in range(TT):
                            nc.vector.tensor_scalar(pick_g[:, t, :], K["slot_iota"], slot_col[:, 0, t:t + 1], None, ALU.is_equal)
                        dve.drain().then_inc(picked, 1)

                    def first(g):
                        if rounds:
                            dve.drain()
                            nc.vector.tensor_scalar(slot_te[:, :, :], slot_te[:, :, :], -float(P), None, ALU.add)
                            dve.drain()
                        pick_next(0, g)

                    with when_needed(dve):
                        nc.vector.engine_nop().then_inc(added, 1)
                        with turns(dve, first) as (i, g, e):
                            nc.vector.tensor_copy(slot_col[:, 1, :], slot_te[:, :, bass.ds(e, 1)].rearrange("p t e -> p (t e)"))
                            nc.vector.tensor_copy(weight_col[:, :], weight_te[:, :, bass.ds(e, 1)].rearrange("p t e -> p (t e)"))
                            dve.drain()
                            for t in range(TT):
                                nc.vector.tensor_scalar(pick_w[:, t, :], K["slot_iota"], slot_col[:, 1, t:t + 1],
                                                        weight_col[:, t:t + 1], ALU.is_equal, ALU.mult)
                            dve.drain().then_inc(pick_w_ready, 1)
                            dve.wait_ge(gathered, g + 1)
                            pick_next(e + 1, g)
                            dve.wait_ge(ring.used, i * SLOTS + (used0 + 4))
                            for s in range(2):
                                pairs = ps[:, 2 * s:2 * s + 2, :].rearrange("p b (n two) -> p b n two", two=2)
                                half = slice(512 * s, 512 * s + 512)
                                nc.vector.tensor_scalar(glu[:, half].rearrange("p (b n) -> p b n", b=2), pairs[:, :, :, 0], LIMIT, None,
                                                        ALU.min).then_inc(glu_ready, 1)
                                nc.vector.tensor_scalar(lin[:, half].rearrange("p (b n) -> p b n", b=2), pairs[:, :, :, 1], -LIMIT, LIMIT,
                                                        ALU.max, ALU.min)
                            dve.drain()
                            for s in range(2):
                                half = slice(512 * s, 512 * s + 512)
                                nc.vector.scalar_tensor_tensor(lin[:, half], lin[:, half], 1.0, glu[:, half], ALU.add, ALU.mult)
                            dve.drain()
                            for s in range(2):
                                half = slice(512 * s, 512 * s + 512)
                                dve.wait_ge(sig_ready, i * 2 + (s + 1))
                                nc.vector.tensor_tensor(lin[:, half], lin[:, half], sig_glu[:, half], ALU.mult).then_inc(hidden_ready, 1)
                            for o in range(8):
                                dst = acc[:, o // 2, 512 * (o % 2):512 * (o % 2) + 512]
                                dve.wait_ge(combined, i * 8 + (o + 1))
                                nc.vector.tensor_tensor(dst, dst, ps[:, o % 4, :], ALU.add).then_inc(added, 1)

        def reset_ring():
            nums = [s.num for s in ring.loaded] + [ring.used.num]
            nc.all_engine_barrier(sems_to_clear=range(min(nums), max(nums) + 1))
            ring.base = ring.issued = ring.taken = moe_at + SLOTS
            ring.slots = SLOTS - 2

        experts_pass(0, True)
        reset_ring()
        experts_pass(T // P - 1, False)
        reset_ring()
        with stage("scaled") as (block, _scaled):
            @block.sync
            def _(sp):
                ring.load(sp, ring.slots)

            @block.vector
            def _(dve):
                for t in range(TT):
                    nc.vector.tensor_tensor(acc[:, t, :], acc[:, t, :], gate_rows[:, 1, :], ALU.mult)
                dve.drain()
                for t in range(TT):
                    nc.vector.tensor_tensor(x_tok[:, t, :], x_tok[:, t, :], acc[:, t, :], ALU.add)
        moe.close()
        first_block.close()

        arena = ring.buf[:, ring.slots:SLOTS, :].rearrange("p s n -> p (s n)")
        h1T = sb(ctx, "h1T", [P, DK, T])
        norm_stage(h1T, lambda k: col("norm1", k), None)

        dn_out = sb(ctx, "dn_out", [P, TT, BW])
        dn = ctx.enter_context(ExitStack())
        k_tok = sb(dn, "k_tok", [P, TT, BW])
        v_tok = sb(dn, "v_tok", [P, TT, BW])
        qT, kT = chan(xn_flat, 0), chan(xn_flat, 2048)
        raw = sb(dn, "conv_raw", [P, BC, T + 2])
        vT = dn_out[:, :, :]
        scratch_a = arena[:, 0:2048].rearrange("p (a b) -> p a b", a=4)

        def conv_silu(dst, j):
            project(h1T, [[("chan", s, ACT.Copy, raw[:, m, 1:1 + T]) for m, s in enumerate(chunks())]], scratch_a)
            with stage("convolved") as (block, convolved):
                @block.vector
                def _(dve):
                    nc.vector.memset(raw[:, :, 0:1], 0.0)
                    nc.vector.memset(raw[:, :, T + 1:T + 2], 0.0)
                    dve.drain()
                    for c in range(BC):
                        taps = [col("dn_conv", 3 * (4 * j + c) + k) for k in range(3)]
                        nc.vector.tensor_scalar(dst[:, c, :], raw[:, c, 0:T], taps[0], None, ALU.mult)
                        for k in range(1, 3):
                            dve.drain()
                            last = nc.vector.scalar_tensor_tensor(dst[:, c, :], raw[:, c, k:k + T], taps[k], dst[:, c, :],
                                                                  ALU.mult, ALU.add)
                        last.then_inc(convolved, 1)

                @block.scalar
                def _(act):
                    for c in range(BC):
                        act.wait_ge(convolved, c + 1)
                        nc.scalar.activation(dst[:, c, :], dst[:, c, :], ACT.Silu)

        for dst, j in ((qT, 0), (kT, 1), (vT, 2)):
            conv_silu(dst, j)

        g_tok = sb(dn, "g_tok", [P, TT, 16])
        beta = sb(dn, "beta", [P, TT, 16])
        g_cum = sb(dn, "g_cum", [P, TT, 16])
        e_g = sb(dn, "e_g", [P, TT, 16])
        e_rest = sb(dn, "e_rest", [P, TT, 16])
        w_ab = arena[:, 4096:4096 + DK * 32].rearrange("p (k n) -> p k n", k=DK)
        tmp_ab = arena[:, 4608:4608 + 64].rearrange("p (t n) -> p t n", t=TT)
        exp_alog = arena[:, 4672:4688]
        gt = arena[:, 4704:4704 + 64].rearrange("p (t n) -> p t n", t=TT)
        with stage("ab_loaded", "squared", "summed", "rooted", "normed", "turned", "turned_read", "ab_ready", "ab_biased",
                   "ab_exp", "g_ready", "cum_ready", "cum_read") as (
                block, ab_loaded, squared, summed, rooted, normed, turned, turned_read, ab_ready, ab_biased, ab_exp,
                g_ready, cum_ready, cum_read):
            @block.sync
            def _(sp):
                sp.dma_start(w_ab, w_in2[:, 2048:2080].rearrange("(k p) n -> p k n", p=P)).then_inc(ab_loaded, 16)

            @block.tensor
            def _(pe):
                pe.wait_ge(ab_loaded, 16)
                for t in range(TT):
                    for k in range(DK):
                        last = nc.tensor.matmul(ps[:, 7, 32 * t:32 * t + 32], h1T[:, k, P * t:P * t + P], w_ab[:, k, :],
                                                start=(k == 0), stop=(k == DK - 1))
                last.then_inc(ab_ready, 1)
                for m in range(8):
                    pe.wait_ge(squared, m + 1)
                    if m >= 2:
                        pe.wait_ge(rooted, m - 1)
                    nc.tensor.matmul(ps[:, m % 2, :], head_sum, scratch_a[:, m % 2, :], start=True, stop=True).then_inc(summed, 1)
                for n in range(8):
                    src, t = (kT, n) if n < 4 else (vT, n - 4)
                    if n == 0:
                        pe.wait_ge(normed, 8)
                    if n >= 3:
                        pe.wait_ge(turned_read, n - 2)
                    for c in range(BC):
                        last = nc.tensor.transpose(ps[:, 2 + n % 3, P * c:P * c + P], src[:, c, P * t:P * t + P], ident)
                    last.then_inc(turned, 1)
                pe.wait_ge(g_ready, 1)
                for d, cum in ((0, "cum_f"), (1, "cum_b")):
                    for t in range(TT):
                        nc.tensor.matmul(ps[:, 5, 16 * t + 8 * d:16 * t + 8 * d + 8], K[cum], g_tok[:, t, 8 * d:8 * d + 8],
                                         start=True, stop=True)
                nc.tensor.matmul(ps[:, 6, 0:64], head_sum, g_tok[:, :, :].rearrange("p t n -> p (t n)"),
                                 start=True, stop=True).then_inc(cum_ready, 1)

            @block.scalar
            def _(act):
                def root(m):
                    act.wait_ge(summed, m + 1)
                    if m >= 2:
                        act.wait_ge(normed, m - 1)
                    nc.scalar.activation(scratch_a[:, 2 + m % 2, :], ps[:, m % 2, :], ACT.Sqrt, bias=col("eps")).then_inc(rooted, 1)

                for m in range(8):
                    src = (qT if m < 4 else kT)[:, m % 4, :]
                    if m >= 2:
                        act.wait_ge(summed, m - 1)
                    nc.scalar.activation(scratch_a[:, m % 2, :], src, ACT.Square).then_inc(squared, 1)
                    if m >= 1:
                        root(m - 1)
                root(7)
                for n in range(8):
                    act.wait_ge(turned, n + 1)
                    dst = k_tok[:, n, :] if n < 4 else v_tok[:, n - 4, :]
                    nc.scalar.activation(dst, ps[:, 2 + n % 3, :], ACT.Copy).then_inc(turned_read, 1)
                act.wait_ge(ab_ready, 1)
                ab = ps[:, 7, 0:P].rearrange("p (t n) -> p t n", t=TT)
                nc.scalar.activation(exp_alog, col("dn_a_log", 0, 16), ACT.Exp)
                act.wait_ge(ab_biased, 1)
                nc.scalar.activation(beta[:, :, :], ab[:, :, 16:32], ACT.Sigmoid)
                nc.scalar.activation(gt, gt, ACT.Exp, scale=-1.0)
                act.drain()
                nc.scalar.activation(gt, gt, ACT.Ln, bias=col("one"))
                act.drain().then_inc(ab_exp, 1)
                act.wait_ge(cum_ready, 1)
                act.wait_ge(cum_read, 1)
                nc.scalar.activation(e_g[:, :, :], g_cum[:, :, :], ACT.Exp)
                nc.scalar.activation(e_rest[:, :, :], tmp_ab, ACT.Exp)

            @block.vector
            def _(dve):
                for m in range(8):
                    buf = (qT if m < 4 else kT)[:, m % 4, :]
                    rinv = scratch_a[:, 2 + m % 2, :]
                    dve.wait_ge(rooted, m + 1)
                    nc.vector.reciprocal(rinv, rinv)
                    dve.drain()
                    nc.vector.scalar_tensor_tensor(buf, buf, HD ** -0.5 if m < 4 else 1.0, rinv, ALU.mult, ALU.mult)\
                        .then_inc(normed, 1)
                dve.wait_ge(ab_ready, 1)
                ab = ps[:, 7, 0:P].rearrange("p (t n) -> p t n", t=TT)
                nc.vector.tensor_tensor(tmp_ab, ab[:, :, 0:16], col("dn_dt_bias", 0, 16).unsqueeze(1).to_broadcast([P, TT, 16]), ALU.add)
                dve.drain()
                nc.vector.scalar_tensor_tensor(gt, tmp_ab, -1.0, tmp_ab, ALU.mult, ALU.max)
                dve.drain().then_inc(ab_biased, 1)
                nc.vector.tensor_scalar(tmp_ab, tmp_ab, 0.0, None, ALU.max)
                dve.wait_ge(ab_exp, 1)
                dve.drain()
                nc.vector.tensor_tensor(tmp_ab, tmp_ab, gt, ALU.add)
                dve.drain()
                nc.vector.scalar_tensor_tensor(g_tok[:, :, :], tmp_ab, -1.0, exp_alog.unsqueeze(1).to_broadcast([P, TT, 16]),
                                               ALU.mult, ALU.mult)
                dve.drain().then_inc(g_ready, 1)
                dve.wait_ge(cum_ready, 1)
                nc.vector.tensor_copy(g_cum[:, :, :], ps[:, 5, 0:64].rearrange("p (t n) -> p t n", t=TT))
                dve.drain()
                nc.vector.tensor_tensor(tmp_ab, ps[:, 6, 0:64].rearrange("p (t n) -> p t n", t=TT), g_cum[:, :, :], ALU.subtract)
                dve.drain().then_inc(cum_read, 1)

        dirs = []
        for d in range(2):
            base = 3072 * d
            dirs.append(dict(
                u=arena[:, base:base + 512].rearrange("p (q c v) -> p q c v", q=2, c=BC),
                wT=arena[:, base + 512:base + 1024].rearrange("p (c i) -> p c i", c=BC),
                qkT=arena[:, base + 1024:base + 2048].rearrange("p (q c i) -> p q c i", q=2, c=BC),
                q_decT=arena[:, base + 2048:base + 2560].rearrange("p (c i) -> p c i", c=BC),
                k_dec=arena[:, base + 2560:base + 3072].rearrange("p (q c k) -> p q c k", q=2, c=BC)))
        state = arena[:, 6144:6656].rearrange("p (d c v) -> p d c v", d=2, c=BC)
        e_total = arena[:, 6656:6656 + 16].rearrange("p (d c n) -> p d c n", d=2, c=BC)
        v_new = arena[:, 6720:6720 + 1024].rearrange("p (d q c v) -> p d q c v", d=2, q=2, c=BC)
        joins = sb(dn, "joins", [P, 2, 6, P])
        lev = sb(dn, "levels", [P, 2, 4, 512])
        product = arena[:, 6720:6720 + 1024].rearrange("p (q n) -> p q n", q=2)
        raw_flat = raw[:, :, :].rearrange("p c t -> p (c t)")
        e_rows = raw_flat[:, 0:512].rearrange("p (c i) -> p c i", c=BC)
        kbg = raw_flat[:, 512:1024].rearrange("p (q c k) -> p q c k", q=2, c=BC)
        vb = raw_flat[:, 1024:1536].rearrange("p (q c k) -> p q c k", q=2, c=BC)
        kscale = sb(dn, "kscale", [P, 8])

        with stage("joins_loaded") as (block, joins_loaded):
            @block.sync
            def _(sp):
                sp.dma_start(joins[:, :, :, :], a["joins"].rearrange("p (w l n) -> p w l n", w=2, l=6)).then_inc(joins_loaded, 16)
                sp.wait_ge(joins_loaded, 16)

            @block.vector
            def _(dve):
                nc.vector.memset(state, 0.0)
                nc.vector.memset(v_new, 0.0)

        def heads_view(flat, p):
            return flat.rearrange("p (c q k) -> p c q k", c=BC, q=2)[:, :, p, :]

        def prepare(d, t):
            D_ = dirs[d]
            mask = K["le_mask"] if d == 0 else K["ge_mask"]
            cum = K["cum_f"] if d == 0 else K["cum_b"]
            join = joins[:, 1 - d]
            col8 = slice(8 * d, 8 * d + 8)
            ends = (63, 127) if d == 0 else (0, 64)
            flat4 = lambda x: x.rearrange("p c i -> p (c i)")
            with stage("rows_ready", "rows_exp", "decay_in", "decay_ready", "at_ready", "joined", "inverse_ready",
                       "first_turned", "prod_ready", "prod_copied", "diff_ready", "scaled", "uw_ready", "kk_read") as (
                    block, rows_ready, rows_exp, decay_in, decay_ready, at_ready, joined, inverse_ready, first_turned,
                    prod_ready, prod_copied, diff_ready, scaled, uw_ready, kk_read):
                @block.tensor
                def _(pe):
                    for p in range(2):
                        b = 4 * p
                        r = slice(HD * p, HD * p + HD)
                        for c in range(BC):
                            h = 8 * d + 2 * c + p
                            i_ = slice(P * c, P * c + P)
                            nc.tensor.matmul(ps[:, b, i_], g_tok[:, t, h:h + 1].to_broadcast([P, P]), cum, start=True, stop=True)
                            nc.tensor.matmul(ps[:, b + 1, i_], beta[:, t, h:h + 1].to_broadcast([P, P]), ident, start=True, stop=True)
                        for c in range(BC):
                            i_ = slice(P * c, P * c + P)
                            tok = slice(P * t, P * t + P)
                            nc.tensor.matmul(ps[:, b + 2, i_], kT[r, c, tok], kT[r, c, tok], start=True, stop=True)
                            last = nc.tensor.matmul(ps[:, b + 3, i_], kT[r, c, tok], qT[r, c, tok], start=True, stop=True)
                        last.then_inc(rows_ready, 1)
                    for p in range(2):
                        pe.wait_ge(inverse_ready, p + 1)
                        for c in range(BC):
                            i_ = slice(P * c, P * c + P)
                            last = nc.tensor.transpose(ps[:, 4 * p, i_], lev[:, p, 3, i_], ident)
                        last.then_inc(first_turned, 1)
                    for l in range(1, 6):
                        for p in range(2):
                            pe.wait_ge(joined, 2 * (l - 1) + p + 1)
                            pe.wait_ge(inverse_ready, 2 * l + p + 1)
                            for c in range(BC):
                                i_ = slice(P * c, P * c + P)
                                last = nc.tensor.matmul(ps[:, 4 * p + 1, i_], lev[:, p, 1, i_], lev[:, p, 2, i_], start=True, stop=True)
                            last.then_inc(prod_ready, 1)
                        for p in range(2):
                            pe.wait_ge(prod_copied, 2 * (l - 1) + p + 1)
                            for c in range(BC):
                                i_ = slice(P * c, P * c + P)
                                last = nc.tensor.matmul(ps[:, 4 * p + 2, i_], product[:, p, i_], lev[:, p, 3, i_], start=True, stop=True)
                                if l < 5:
                                    last = nc.tensor.matmul(ps[:, 4 * p + 3, i_], lev[:, p, 3, i_], product[:, p, i_], start=True, stop=True)
                            last.then_inc(diff_ready, 1)
                    pe.wait_ge(scaled, 1)
                    for p in range(2):
                        r = slice(HD * p, HD * p + HD)
                        pe.wait_ge(inverse_ready, 12 + p + 1)
                        for c in range(BC):
                            i_ = slice(P * c, P * c + P)
                            nc.tensor.matmul(ps[:, 4 * p, HD * c:HD * c + HD], lev[:, p, 3, i_], vb[:, p, c, :], start=True, stop=True)
                            last = nc.tensor.matmul(ps[r, 4 * p + 1, i_], kbg[:, p, c, :], lev[:, p, 3, i_], start=True, stop=True)
                        last.then_inc(uw_ready, 1)

                @block.scalar
                def _(act):
                    for p in range(2):
                        r = slice(HD * p, HD * p + HD)
                        act.wait_ge(rows_ready, p + 1)
                        rows = ps[r, 4 * p, :].rearrange("p (c i) -> p c i", c=BC)
                        nc.scalar.activation(e_rows[r], rows, ACT.Exp)
                        for n in range(2):
                            last = nc.scalar.activation(e_total[r, d, :, n:n + 1], rows[:, :, ends[n]:ends[n] + 1], ACT.Exp)
                        act.drain().then_inc(rows_exp, 1)
                        act.wait_ge(decay_in, p + 1)
                        nc.scalar.activation(D_["qkT"][:, p], D_["qkT"][:, p], ACT.Exp).then_inc(decay_ready, 1)
                    for l in range(1, 6):
                        for p in range(2):
                            act.wait_ge(prod_ready, 2 * (l - 1) + p + 1)
                            nc.scalar.activation(product[:, p, :], ps[:, 4 * p + 1, :], ACT.Copy).then_inc(prod_copied, 1)
                    for p in range(2):
                        r = slice(HD * p, HD * p + HD)
                        act.wait_ge(uw_ready, p + 1)
                        nc.scalar.activation(D_["u"][:, p], ps[:, 4 * p, 0:256].rearrange("p (c v) -> p c v", c=BC), ACT.Copy)
                        nc.scalar.activation(D_["wT"][r], ps[r, 4 * p + 1, :].rearrange("p (c i) -> p c i", c=BC), ACT.Copy)

                @block.gpsimd
                def _(pool):
                    for l in range(1, 6):
                        for p in range(2):
                            if l == 1:
                                pool.wait_ge(at_ready, p + 1)
                            else:
                                pool.wait_ge(prod_copied, 2 * (l - 2) + p + 1)
                            nc.gpsimd.tensor_tensor(lev[:, p, 1, :].rearrange("p (c i) -> p c i", c=BC),
                                                    lev[:, p, 0, :].rearrange("p (c i) -> p c i", c=BC),
                                                    join[:, l, :].unsqueeze(1).to_broadcast([P, BC, P]), ALU.mult).then_inc(joined, 1)

                @block.vector
                def _(dve):
                    v4 = lambda x: x.rearrange("p (c i) -> p c i", c=BC)
                    for p in range(2):
                        gcol = g_cum[:, t, col8].rearrange("p (c q) -> p c q", q=2)[:, :, p:p + 1]
                        dve.wait_ge(rows_exp, p + 1)
                        x = D_["qkT"][:, p]
                        nc.vector.tensor_tensor(x, v4(ps[:, 4 * p, :]), gcol.to_broadcast([P, BC, P]), ALU.subtract)
                        dve.drain()
                        nc.vector.tensor_tensor(x, x, mask.unsqueeze(1).to_broadcast([P, BC, P]), ALU.add).then_inc(decay_in, 1)
                    for p in range(2):
                        x, at = D_["qkT"][:, p], v4(lev[:, p, 0, :])
                        dve.wait_ge(decay_ready, p + 1)
                        nc.vector.tensor_tensor(at, x, v4(ps[:, 4 * p + 1, :]), ALU.mult)
                        dve.drain()
                        nc.vector.tensor_tensor(at, at, v4(ps[:, 4 * p + 2, :]), ALU.mult)
                        nc.vector.tensor_tensor(x, x, v4(ps[:, 4 * p + 3, :]), ALU.mult)
                        dve.drain().then_inc(at_ready, 1)
                        tt = v4(lev[:, p, 3, :])
                        nc.vector.tensor_tensor(tt, at, join[:, 0, :].unsqueeze(1).to_broadcast([P, BC, P]), ALU.mult)
                        dve.drain()
                        nc.vector.tensor_tensor(tt, ident.unsqueeze(1).to_broadcast([P, BC, P]), tt, ALU.subtract)
                        dve.drain().then_inc(inverse_ready, 1)
                    for p in range(2):
                        dve.wait_ge(first_turned, p + 1)
                        nc.vector.tensor_copy(lev[:, p, 2, :], ps[:, 4 * p, :])
                        dve.drain().then_inc(inverse_ready, 1)
                    nc.vector.tensor_tensor(kscale[:, :], beta[:, t, col8], e_g[:, t, col8], ALU.mult)
                    dve.drain()
                    for p in range(2):
                        r = slice(HD * p, HD * p + HD)
                        pick = lambda x: x.rearrange("p (c q) -> p c q", q=2)[:, :, p:p + 1].to_broadcast([P, BC, HD])
                        kk, vv = heads_view(k_tok[:, t, :], p), heads_view(v_tok[:, t, :], p)
                        nc.vector.tensor_tensor(vb[:, p], vv, pick(beta[:, t, col8]), ALU.mult)
                        nc.vector.tensor_tensor(kbg[:, p], kk, pick(kscale[:, :]), ALU.mult)
                        nc.vector.tensor_tensor(D_["k_dec"][:, p], kk, pick(e_rest[:, t, col8]), ALU.mult)
                        dve.wait_ge(rows_exp, p + 1)
                        nc.vector.tensor_tensor(D_["q_decT"][r], qT[r, :, P * t:P * t + P], e_rows[r], ALU.mult)
                    dve.drain().then_inc(scaled, 1)
                    for l in range(1, 6):
                        for p in range(2):
                            dve.wait_ge(diff_ready, 2 * (l - 1) + p + 1)
                            if l < 5:
                                nc.vector.tensor_tensor(lev[:, p, 2, :], lev[:, p, 2, :], ps[:, 4 * p + 3, :], ALU.subtract)
                            nc.vector.tensor_tensor(lev[:, p, 3, :], lev[:, p, 3, :], ps[:, 4 * p + 2, :], ALU.subtract)
                            dve.drain().then_inc(inverse_ready, 1)

        def recur(step):
            turns = [(0, step, 0), (1, TT - 1 - step, 1), (0, step, 1), (1, TT - 1 - step, 0)]
            with stage("ws_ready", "v_ready", "o_ready", "s_ready", "s_scaled", "o_read") as (
                    block, ws_ready, v_ready, o_ready, s_ready, s_scaled, o_read):
                @block.tensor
                def _(pe):
                    for n, (d, t, ch) in enumerate(turns):
                        D_ = dirs[d]
                        tok = slice(HD * ch, HD * ch + HD)
                        b = 4 * d
                        if n >= 2:
                            pe.wait_ge(s_ready, n - 1)
                            pe.wait_ge(o_read, n - 1)
                        for p in range(2):
                            r = slice(HD * p, HD * p + HD)
                            for c in range(BC):
                                last = nc.tensor.matmul(ps[tok, b + p, HD * c:HD * c + HD], D_["wT"][r, c, tok], state[r, d, c, :],
                                                        start=True, stop=True)
                        last.then_inc(ws_ready, 1)
                        pe.wait_ge(v_ready, n + 1)
                        for p in range(2):
                            r = slice(HD * p, HD * p + HD)
                            for c in range(BC):
                                o = ps[tok, b + 2 + p, HD * c:HD * c + HD]
                                nc.tensor.matmul(o, D_["q_decT"][r, c, tok], state[r, d, c, :], start=True, stop=False)
                                last = nc.tensor.matmul(o, D_["qkT"][:, p, c, tok], v_new[:, d, p, c, :], start=False, stop=True)
                        last.then_inc(o_ready, 1)
                        for p in range(2):
                            r = slice(HD * p, HD * p + HD)
                            for c in range(BC):
                                last = nc.tensor.matmul(ps[r, b, 256 + HD * c:256 + HD * c + HD], D_["k_dec"][tok, p, c, :],
                                                        v_new[tok, d, p, c, :], start=True, stop=True)
                        last.then_inc(s_scaled, 1)

                @block.vector
                def _(dve):
                    for n, (d, t, ch) in enumerate(turns):
                        D_ = dirs[d]
                        tok = slice(HD * ch, HD * ch + HD)
                        b = 4 * d
                        cv = lambda x: x.rearrange("p (c v) -> p c v", c=BC)
                        dve.wait_ge(ws_ready, n + 1)
                        for p in range(2):
                            nc.vector.tensor_tensor(v_new[tok, d, p], D_["u"][tok, p], cv(ps[tok, b + p, 0:256]), ALU.subtract)
                        dve.drain().then_inc(v_ready, 1)
                        dve.wait_ge(o_ready, n + 1)
                        for p in range(2):
                            dst = heads_view(dn_out[tok, t, :], p)
                            src = cv(ps[tok, b + 2 + p, 0:256])
                            if step < 2:
                                nc.vector.tensor_copy(dst, src)
                            else:
                                nc.vector.tensor_tensor(dst, dst, src, ALU.add)
                        dve.drain().then_inc(o_read, 1)
                        nc.vector.tensor_tensor(state[:, d], state[:, d], e_total[:, d, :, ch:ch + 1].to_broadcast([P, BC, HD]), ALU.mult)
                        dve.drain()
                        dve.wait_ge(s_scaled, n + 1)
                        nc.vector.tensor_tensor(state[:, d], state[:, d], cv(ps[:, b, 256:512]), ALU.add)
                        dve.drain().then_inc(s_ready, 1)

        for step in range(TT):
            prepare(0, step)
            prepare(1, TT - 1 - step)
            recur(step)
        z = k_tok
        project(h1T, [[("token", slice(0, 512), (lambda k, t=t: h1T[:, k, P * t:P * t + P]), ACT.Silu, z[:, t, :]) for t in range(TT)]],
                scratch_a)
        flat = dn_out[:, :, :].rearrange("p t n -> p (t n)")
        by_head = flat.rearrange("p (h v) -> p h v", v=HD)
        squares = v_tok[:, :, :].rearrange("p t n -> p (t n)")
        with stage("sums_ready", "rooted", "rows_ready", "turned") as (block, sums_ready, rooted, rows_ready, turned):
            @block.vector
            def _(dve):
                nc.vector.tensor_tensor(squares, flat, flat, ALU.mult)
                dve.drain()
                nc.vector.tensor_reduce(small[:, 0:32], squares.rearrange("p (h v) -> p h v", v=HD), AX.X, ALU.add)\
                    .then_inc(sums_ready, 1)
                dve.wait_ge(rooted, 1)
                nc.vector.reciprocal(small[:, 32:64], small[:, 32:64])
                dve.drain()
                nc.vector.tensor_tensor(by_head, by_head, small[:, 32:64].unsqueeze(2).to_broadcast([P, 32, HD]), ALU.mult)
                dve.drain()
                nc.vector.tensor_tensor(by_head, by_head, col("dn_out_norm", 0, HD).unsqueeze(1).to_broadcast([P, 32, HD]), ALU.mult)
                dve.drain()
                nc.vector.tensor_tensor(flat, flat, z[:, :, :].rearrange("p t n -> p (t n)"), ALU.mult).then_inc(rows_ready, 1)

            @block.tensor
            def _(pe):
                pe.wait_ge(rows_ready, 1)
                for c in range(BC):
                    for t in range(TT):
                        last = nc.tensor.transpose(ps[:, c, P * t:P * t + P], dn_out[:, t, P * c:P * c + P], ident)
                last.then_inc(turned, 1)

            @block.scalar
            def _(act):
                act.wait_ge(sums_ready, 1)
                nc.scalar.activation(small[:, 32:64], small[:, 0:32], ACT.Sqrt, scale=1.0 / HD, bias=col("eps")).then_inc(rooted, 1)
                act.wait_ge(turned, 1)
                for c in range(BC):
                    nc.scalar.activation(dn_out[:, c, :], ps[:, c, :], ACT.Copy)
        dn.close()

        att = ctx.enter_context(ExitStack())
        o_g = sb(att, "group_out", [P, 3, BC, T])
        stats_g = [sb(att, f"stats{g}", [P, 3, 32]) for g in range(3)]
        lse = sb(att, "lse", [P, 3, TT, 8])
        lse_t = sb(att, "lse_t", [8, 3, T])
        lse_m = sb(att, "lse_max", [8, T])
        selector = sb(att, "selector", [8, BC, P])
        s_buf2 = arena[:, 0:2048].rearrange("p (a b) -> p a b", a=2)
        scratch_b = arena[:, 0:2048].rearrange("p (a b) -> p a b", a=4)
        p_turned2 = arena[:, 2048:3072]
        v_g = arena[:, 3072:5120].rearrange("p (t n) -> p t n", t=TT)
        alibi_at = arena[:, 5120:8192]
        q_gain = small[:, 0:1]

        for g in range(3):
            step_ = 1 if g == 0 else 4

            def tokens(t, step_=step_):
                return slice(P * t, P * t + P) if step_ == 1 else slice(t, T, step_)

            w_alibi = 8 * (3 * P if g == 0 else P)
            with stage("alibi_loaded") as (block, alibi_loaded):
                @block.sync
                def _(sp):
                    sp.dma_start(alibi_at[:, 0:w_alibi], a[f"alibi{g}"]).then_inc(alibi_loaded, 16)
                    if g == 0:
                        sp.dma_start(selector[:, :, :], a["selector"].rearrange("h (c n) -> h c n", c=BC)).then_inc(alibi_loaded, 16)
                    sp.wait_ge(alibi_loaded, 32 if g == 0 else 16)

                @block.vector
                def _(dve):
                    nc.vector.tensor_scalar(q_gain, col("attn_qnorm"), HD ** -0.5, None, ALU.mult)
            project(h1T, [[("norm", s, q_gain, qT[:, m, :], True) for m, s in enumerate(chunks())],
                          [("norm", s, col("attn_knorm"), kT[:, m, :], True) for m, s in enumerate(chunks())],
                          [("token", slice(0, 512), (lambda k, sl=tokens(t): h1T[:, k, sl]), ACT.Copy, v_g[:, t, :]) for t in range(TT)]],
                    scratch_b)
            alibi = alibi_at[:, 0:w_alibi].rearrange("p (h x) -> p h x", h=8)
            units = []
            for t in range(TT):
                if g == 0:
                    lo, hi = max(t - 1, 0), min(t + 1, TT - 1)
                    w = P * (hi - lo + 1)
                    x0 = P * (lo - t + 1)
                    nt = hi - lo + 1
                    for c in range(BC):
                        rows = [slice(HD * p, HD * p + HD) for p in range(2)]
                        units.append(dict(
                            scores=[(512 * p, w, qT[rows[p], c, P * t:P * t + P], kT[rows[p], c, P * lo:P * lo + w]) for p in range(2)],
                            seg=(2, 512, w), bias=alibi[:, 2 * c:2 * c + 2, x0:x0 + w],
                            turns=[512 * p + P * m for p in range(2) for m in range(nt)],
                            pv=[(rows[p], 0, [(v_g[:, lo + m, HD * (2 * c + p):HD * (2 * c + p) + HD], nt * p + m) for m in range(nt)])
                                for p in range(2)],
                            out=[(o_g[:, 0, c, P * t:P * t + P], slice(0, P), slice(0, P))]))
                else:
                    sc, pv = [], []
                    for p in range(2):
                        r = slice(HD * p, HD * p + HD)
                        for c in range(BC):
                            sc.append((512 * p + P * c, P, qT[r, c, tokens(t)], kT[r, c, tokens(t)]))
                            pv.append((r, P * c, [(v_g[:, t, HD * (2 * c + p):HD * (2 * c + p) + HD], 4 * p + c)]))
                    units.append(dict(
                        scores=sc, seg=(8, P, P), bias=alibi[:, :, :], turns=[P * j for j in range(8)], pv=pv,
                        out=[(o_g[:, g, :, tokens(t)], slice(0, P), slice(0, 512))]))
            attention(units, stats_g[g], s_buf2, p_turned2)

        o_bT = o_g[:, 0]
        with stage("logs_ready", "lse_ready", "turned", "turned_read", "lse_sub", "lse_exp", "weights_ready", "spread", "spread_read") as (
                block, logs_ready, lse_ready, turned, turned_read, lse_sub, lse_exp, weights_ready, spread, spread_read):
            @block.scalar
            def _(act):
                for g in range(3):
                    nc.scalar.activation(stats_g[g][:, 1, :], stats_g[g][:, 1, :], ACT.Ln)
                act.drain().then_inc(logs_ready, 1)
                for g in range(3):
                    act.wait_ge(turned, g + 1)
                    src = ps[0:8, g, :]
                    if g == 0:
                        nc.scalar.activation(lse_t[:, g, :], src, ACT.Copy)
                    else:
                        nc.scalar.activation(lse_t[:, g, :].rearrange("h (j r) -> h r j", r=4), src.rearrange("h (r j) -> h r j", r=4), ACT.Copy)
                act.drain().then_inc(turned_read, 1)
                act.wait_ge(lse_sub, 1)
                nc.scalar.activation(lse_t[:, :, :], lse_t[:, :, :], ACT.Exp).then_inc(lse_exp, 1)

            @block.tensor
            def _(pe):
                pe.wait_ge(lse_ready, 1)
                for g in range(3):
                    for t in range(TT):
                        last = nc.tensor.transpose(ps[0:8, g, P * t:P * t + P], lse[:, g, t, :], ident)
                    last.then_inc(turned, 1)
                pe.wait_ge(weights_ready, 1)
                for n in range(12):
                    g, c = n // BC, n % BC
                    if n >= 4:
                        pe.wait_ge(spread_read, n - 3)
                    nc.tensor.matmul(ps[:, 4 + n % 4, :], selector[:, c, :], lse_t[:, g, :], start=True, stop=True).then_inc(spread, 1)

            @block.vector
            def _(dve):
                dve.wait_ge(logs_ready, 1)
                for g in range(3):
                    def order(x):
                        if g == 0:
                            return x.rearrange("p (t h) -> p t h", t=TT)
                        return x.rearrange("p (t q c) -> p t c q", t=TT, q=2)
                    dst = lse[:, g] if g == 0 else lse[:, g].rearrange("p t (c q) -> p t c q", q=2)
                    nc.vector.tensor_tensor(dst, order(stats_g[g][:, 1, :]), order(stats_g[g][:, 0, :]), ALU.subtract)
                dve.drain().then_inc(lse_ready, 1)
                dve.wait_ge(turned_read, 1)
                nc.vector.tensor_tensor(lse_m[:, :], lse_t[:, 0, :], lse_t[:, 1, :], ALU.max)
                dve.drain()
                nc.vector.tensor_tensor(lse_m[:, :], lse_m[:, :], lse_t[:, 2, :], ALU.max)
                dve.drain()
                nc.vector.tensor_tensor(lse_t[:, :, :], lse_t[:, :, :], lse_m[:, :].unsqueeze(1).to_broadcast([8, 3, T]), ALU.subtract)
                dve.drain().then_inc(lse_sub, 1)
                dve.wait_ge(lse_exp, 1)
                nc.vector.tensor_tensor(lse_m[:, :], lse_t[:, 0, :], lse_t[:, 1, :], ALU.add)
                dve.drain()
                nc.vector.tensor_tensor(lse_m[:, :], lse_m[:, :], lse_t[:, 2, :], ALU.add)
                dve.drain()
                nc.vector.reciprocal(lse_m[:, :], lse_m[:, :])
                dve.drain()
                nc.vector.tensor_tensor(lse_t[:, :, :], lse_t[:, :, :], lse_m[:, :].unsqueeze(1).to_broadcast([8, 3, T]), ALU.mult)
                dve.drain().then_inc(weights_ready, 1)
                for n in range(12):
                    g, c = n // BC, n % BC
                    dve.wait_ge(spread, n + 1)
                    nc.vector.tensor_tensor(o_g[:, g, c, :], o_g[:, g, c, :], ps[:, 4 + n % 4, :], ALU.mult).then_inc(spread_read, 1)
                dve.drain()
                nc.vector.tensor_tensor(o_bT, o_bT, o_g[:, 1], ALU.add)
                dve.drain()
                nc.vector.tensor_tensor(o_bT, o_bT, o_g[:, 2], ALU.add)

        merge_branches(h1T, [dn_out[:, :, :], o_bT], chan(xn_flat, 0, DK),
                       arena[:, 0:1024].rearrange("p (a b) -> p a b", a=2), arena[:, 1024:2048].rearrange("p (a b) -> p a b", a=2))
        project_out(chan(xn_flat, 0, DK), DK, None)
        att.close()

        norm_stage(h1T, lambda k: col("norm2", k), None)
        ffn = ctx.enter_context(ExitStack())
        actT = sb(ffn, "ffn_hidden", [P, FFC, T])
        raw2 = arena[:, 0:2 * 4 * (T + 2)].rearrange("p (b m t) -> p b m t", b=2, m=4)
        conv2 = xn_flat.rearrange("p (b m t) -> p b m t", b=2, m=4)
        NT = FFC // 2
        with stage("pads_ready", "up_ready", "raw_ready", "convolved", "gates_ready", "hidden_ready") as (
                block, pads_ready, up_ready, raw_ready, convolved, gates_ready, hidden_ready):
            @block.sync
            def _(sp):
                ring.load(sp, NT)

            @block.tensor
            def _(pe):
                n = 0
                for j in range(NT):
                    w = ring.take(pe)
                    for m in range(4):
                        if n >= 8:
                            pe.wait_ge(raw_ready, n - 7)
                        for k in range(DK):
                            last = nc.tensor.matmul(ps[:, n % 8, :], w[:, k, P * m:P * m + P], h1T[:, k, :], start=(k == 0), stop=(k == DK - 1))
                        last.then_inc(up_ready, 1)
                        n += 1
                    pe.wait_ge(up_ready, n)
                    nc.tensor.nop().then_inc(ring.used, 1)

            @block.scalar
            def _(act):
                def silu(j):
                    act.wait_ge(convolved, 4 * j + 2)
                    for m in range(2):
                        nc.scalar.activation(conv2[:, j % 2, m, :], conv2[:, j % 2, m, :], ACT.Silu).then_inc(gates_ready, 1)

                act.wait_ge(pads_ready, 1)
                for j in range(NT):
                    for m in range(4):
                        n = 4 * j + m
                        act.wait_ge(up_ready, n + 1)
                        if j >= 2:
                            act.wait_ge(convolved, n - 7)
                        nc.scalar.activation(raw2[:, j % 2, m, 1:1 + T], ps[:, n % 8, :], ACT.Copy).then_inc(raw_ready, 1)
                    if j >= 1:
                        silu(j - 1)
                silu(NT - 1)

            @block.vector
            def _(dve):
                def hidden(j):
                    for m in range(2):
                        dve.wait_ge(gates_ready, 2 * j + m + 1)
                        nc.vector.tensor_tensor(actT[:, 2 * j + m, :], conv2[:, j % 2, m, :], conv2[:, j % 2, 2 + m, :], ALU.mult)

                nc.vector.memset(raw2[:, :, :, 0:1], 0.0)
                nc.vector.memset(raw2[:, :, :, T + 1:T + 2], 0.0)
                dve.drain().then_inc(pads_ready, 1)
                for j in range(NT):
                    for m in range(4):
                        f = 2 * j + m if m < 2 else FFC + 2 * j + m - 2
                        dst, src = conv2[:, j % 2, m, :], raw2[:, j % 2, m, :]
                        dve.wait_ge(raw_ready, 4 * j + m + 1)
                        nc.vector.tensor_scalar(dst, src[:, 0:T], col("ffn_conv", 3 * f), None, ALU.mult)
                        for k in range(1, 3):
                            dve.drain()
                            last = nc.vector.scalar_tensor_tensor(dst, src[:, k:k + T], col("ffn_conv", 3 * f + k), dst, ALU.mult, ALU.add)
                        last.then_inc(convolved, 1)
                    if j >= 1:
                        hidden(j - 1)
                        dve.drain()
                hidden(NT - 1)

        with stage("down_ready", "rows_ready", "stored") as (block, down_ready, rows_ready, stored):
            @block.tensor
            def _(pe):
                f = 0
                for j in range(6):
                    w = ring.take(pe)
                    n_k = 4 if j < 5 else 2
                    for t in range(TT):
                        for h in range(2):
                            for k in range(n_k):
                                last = nc.tensor.matmul(ps[:, 2 * t + h, :], actT[:, f + k, P * t:P * t + P], w[:, k, 512 * h:512 * h + 512],
                                                        start=(f + k == 0), stop=(f + k == FFC - 1))
                        if j == 5:
                            last.then_inc(down_ready, 1)
                    if j < 5:
                        last.then_inc(ring.used, 1)
                    f += n_k

            @block.vector
            def _(dve):
                for t in range(TT):
                    dve.wait_ge(down_ready, t + 1)
                    nc.vector.tensor_tensor(x_tok[:, t, :], x_tok[:, t, :], ps[:, 2 * t:2 * t + 2, :].rearrange("p b n -> p (b n)"),
                                            ALU.add).then_inc(rows_ready, 1)

            @block.sync
            def _(sp):
                ring.load(sp, 6)
                for t in range(TT):
                    sp.wait_ge(rows_ready, t + 1)
                    sp.dma_start(out[0, P * t:P * t + P, :], x_tok[:, t, :]).then_inc(stored, 16)
                sp.wait_ge(stored, 16 * TT)


_OUTS = [((1, T, D), "float32")]


def host_arrays(i):
    arrays = {k: np.ascontiguousarray(i[k]) for k in
              ("x", "b_ada", "w_ada", "w_in", "w_branch", "w_out", "w_router", "w1", "b1", "w2", "b2", "rel_bias", "w_in_2",
               "w_dn_out_2", "w_attn_out_2", "w_o_2", "w_ffn_up_2", "w_ffn_down_2")}
    c = constants()
    arrays["const"] = np.concatenate([c[n] for n, _ in CONST_W], 1)
    arrays["joins"] = np.concatenate([c["join_lo"], c["join_up"]], 1)
    arrays["columns"] = pack_columns(i)
    order = [0, 1, 2, 3] + [4 + 4 * g + j for g in range(2) for j in SWA_ORDER]
    arrays["rel_bias"] = np.ascontiguousarray(arrays["rel_bias"][:, order])
    arrays["lru_a"] = pack_blocks(i["lru_wa"])
    arrays["lru_x"] = pack_blocks(i["lru_wx"])
    arrays["bucket_onehot"], arrays["bucket_mask"] = bias_constants()
    heads = np.arange(8)[:, None, None]
    arrays["selector"] = (heads == 2 * np.arange(BC)[None, :, None] + np.arange(P)[None, None, :] // HD)\
        .astype(np.float32).reshape(8, -1)
    arrays["alibi0"], arrays["alibi1"], arrays["alibi2"] = alibi_constants()
    return arrays


def kernel(**inputs):
    import concourse.bacc as _bacc
    from concourse.bass_utils import run_bass_kernel_spmd as _run

    nc = _bacc.Bacc("TRN2", target_bir_lowering=False, num_devices=1)
    arrays, args = {}, {}
    for name, x in host_arrays(inputs).items():
        arrays[f"in_{name}"] = x
        args[name] = nc.dram_tensor(f"in_{name}", x.shape, mybir.dt.from_np(x.dtype), kind="ExternalInput").ap()
    shape, dtype = _OUTS[0]
    out = nc.dram_tensor("out_0", shape, mybir.dt.from_np(np.dtype(dtype)), kind="ExternalOutput").ap()
    build(nc, args, out)
    r = _run(nc, [arrays], core_ids=[0])
    return r.results[0]["out_0"]
```

```python
from contextlib import ExitStack, contextmanager
import math

import numpy as np

import concourse.bass as bass
from concourse import mybir

F32 = mybir.dt.float32
U32 = mybir.dt.uint32
I32 = mybir.dt.int32
F32R = mybir.dt.float32r
ACT = mybir.ActivationFunctionType
ALU = mybir.AluOpType
AX = mybir.AxisListType

P = 128
T = 512
TT = T // P
D = 1024
DK = D // P
EPS = 1e-6
NEG = -1e30
BW = 512
BC = BW // P
HD = 64
E = 32
TOPK = 4
DFF = 1024
FFC = 2816 // P
BUCKETS, N_BIAS_HEADS = 32, 12
TOEP = 640
LAMBDA_INIT = 0.8 - 0.6 * math.exp(0.0)
SWA_ORDER = (0, 2, 1, 3)
UNIT_F = 2048


def constants():
    c = {}
    eye = np.eye(P, dtype=np.float32)
    i = np.arange(P)
    c["ident"] = eye
    c["flip"] = eye[::-1].copy()
    c["head_sum"] = (i[:, None] // HD == i[None, :] // HD).astype(np.float32)
    c["ones"] = np.ones((P, P), np.float32)
    same = i[:, None] // HD == i[None, :] // HD
    c["cum_f"] = (same & (i[:, None] <= i[None, :])).astype(np.float32)
    c["cum_b"] = (same & (i[:, None] >= i[None, :])).astype(np.float32)
    c["before"] = (i[:, None] < i[None, :]).astype(np.float32)
    c["slot_iota"] = np.broadcast_to(i.astype(np.float32), (P, P)).copy()
    c["ge_mask"] = np.where(same & (i[:, None] >= i[None, :]), 0, NEG).astype(np.float32)
    c["le_mask"] = np.ascontiguousarray(c["ge_mask"].T)
    lev = np.zeros((6, P, P), np.float32)
    for l in range(6):
        b = 1 << l
        lev[l] = (i[:, None] // (2 * b) == i[None, :] // (2 * b)) & (i[:, None] // b % 2 == 1) & (i[None, :] // b % 2 == 0)
    c["join_lo"] = lev.transpose(1, 0, 2).reshape(P, 6 * P).copy()
    c["join_up"] = lev.transpose(2, 0, 1).reshape(P, 6 * P).copy()
    return c


CONST_W = [("ident", P), ("flip", P), ("head_sum", P), ("ones", P), ("cum_f", P), ("cum_b", P), ("before", P),
           ("slot_iota", P), ("ge_mask", P), ("le_mask", P)]
JOIN_W = 12 * P


def t5_bucket_np(dist):
    exact = BUCKETS // 2
    ratio = np.log(np.maximum(dist, 1).astype(np.float32) / exact) / math.log(128 / exact)
    large = exact + (ratio * (BUCKETS - exact)).astype(np.int32)
    return np.where(dist < exact, dist, np.minimum(large, BUCKETS - 1))


def bias_constants():
    dist = 511 - np.arange(TOEP)
    ok = dist >= 0
    onehot = np.zeros((BUCKETS, TOEP), np.float32)
    onehot[t5_bucket_np(np.maximum(dist, 0)), np.arange(TOEP)] = 1.0
    onehot[:, ~ok] = 0
    mask = np.zeros((N_BIAS_HEADS, TOEP), np.float32)
    mask[:, ~ok] = NEG
    mask[4:, dist >= P] = NEG
    return onehot, mask


def alibi_constants():
    slopes = (2.0 ** (-8.0 * np.arange(1, 25, dtype=np.float32) / 24)).astype(np.float32).reshape(3, 8)
    q = np.arange(P)[:, None]
    k = np.arange(3 * P)[None, :] - P
    rel = np.abs(q - k)
    g0 = np.stack([np.where(rel <= 64, -slopes[0, h] * rel.astype(np.float32), NEG) for h in range(8)], 1)
    k = np.arange(P)[None, :]
    rel = np.abs(q - k)
    g1 = np.stack([np.where(rel <= 64, -slopes[1, h] * (rel * 4).astype(np.float32), NEG) for h in range(8)], 1)
    rel = np.abs(q // 4 - k // 4)
    g2 = np.stack([np.where(q % 4 == k % 4, -slopes[2, h] * (rel * 16).astype(np.float32), NEG) for h in range(8)], 1)
    by_parity = [0, 2, 4, 6, 1, 3, 5, 7]
    return [np.ascontiguousarray(x.reshape(P, -1).astype(np.float32)) for x in (g0, g1[:, by_parity], g2[:, by_parity])]


COLS, _at = {}, 0
for _name, _n in [("c", DK), ("norm_mix", DK), ("norm_ffn", DK), ("b_ada", 48), ("conv_w", 4 * BC), ("conv_b", BC),
                  ("lru_ba", BC), ("lru_bx", BC), ("lru_lambda", BC), ("diff_qnorm", 1), ("diff_knorm", 1),
                  ("swa_qnorm", 1), ("swa_knorm", 1), ("diff_subln", 1), ("diff_lambda", 4 * HD), ("swa_sinks", 8),
                  ("b_router", E), ("norm1", DK), ("norm2", DK), ("dn_conv", 36), ("ffn_conv", 132),
                  ("attn_qnorm", 1), ("attn_knorm", 1), ("dn_a_log", 16), ("dn_dt_bias", 16), ("dn_out_norm", HD),
                  ("eps", 1), ("one", 1)]:
    COLS[_name] = (_at, _n)
    _at += _n
NCOLS = _at


def pack_columns(i):
    def col(a):
        return np.asarray(a).reshape(-1, P).T

    def rep(a):
        return np.broadcast_to(np.asarray(a).reshape(1, -1), (P, np.asarray(a).size))

    def taps(a):
        a = np.asarray(a)
        return a.reshape(a.shape[0], -1, P).transpose(2, 1, 0).reshape(P, -1)

    def twice(a):
        return np.concatenate([np.asarray(a).reshape(-1)] * 2).reshape(P, 1)

    parts = {
        "c": col(i["c"]), "norm_mix": col(i["norm_mix"]), "norm_ffn": col(i["norm_ffn"]), "b_ada": col(i["b_ada"]),
        "conv_w": taps(i["conv_w"][0]), "conv_b": col(i["conv_b"]), "lru_ba": col(i["lru_ba"]),
        "lru_bx": col(i["lru_bx"]), "lru_lambda": col(i["lru_lambda"]), "diff_qnorm": twice(i["diff_qnorm"]),
        "diff_knorm": twice(i["diff_knorm"]), "swa_qnorm": twice(i["swa_qnorm"]), "swa_knorm": twice(i["swa_knorm"]),
        "diff_subln": col(i["diff_subln"]), "diff_lambda": rep(i["diff_lambda"]), "swa_sinks": rep(np.asarray(i["swa_sinks"]).reshape(2, 4)[:, list(SWA_ORDER)]),
        "b_router": rep(i["b_router"]), "norm1": col(i["norm1_w_2"]), "norm2": col(i["norm2_w_2"]),
        "dn_conv": taps(i["dn_conv_w_2"][0]), "ffn_conv": taps(i["ffn_conv_w_2"][0]),
        "attn_qnorm": twice(i["attn_q_norm_w_2"]), "attn_knorm": twice(i["attn_k_norm_w_2"]),
        "dn_a_log": rep(i["dn_a_log_2"]), "dn_dt_bias": rep(i["dn_dt_bias_2"]), "dn_out_norm": rep(i["dn_out_norm_w_2"]),
        "eps": np.full((P, 1), EPS, np.float32), "one": np.ones((P, 1), np.float32),
    }
    for name, (_, n) in COLS.items():
        assert parts[name].shape == (P, n), name
    return np.ascontiguousarray(np.concatenate([parts[n] for n in COLS], 1))


def pack_blocks(a):
    a = np.asarray(a)[0]
    out = np.zeros((P, BC, P), np.float32)
    for h in range(8):
        r = HD * (h % 2)
        out[r:r + HD, h // 2, r:r + HD] = a[h]
    return out.reshape(P, -1)


def twin(nc, stack, name, shape):
    at = -(-nc.sbuf_base // 32) * 32
    full = stack.enter_context(nc.sbuf_tensor(name, shape, F32))
    return full, nc.alloc_sbuf_tensor_at(name + "_part", shape, F32R, offset=at)


def product(nc, out, x, y, start, stop):
    nc.tensor.matmul(out, x[0], y[0], start=start, stop=False)
    nc.tensor.matmul(out, x[1], y[0], start=False, stop=False)
    return nc.tensor.matmul(out, x[0], y[1], start=False, stop=stop)


class WeightRing:

    def __init__(self, nc, ctx):
        self.nc = nc
        self.buf, self.part = twin(nc, ctx, "weight_ring", [P, 12, UNIT_F])
        self.loaded = [ctx.enter_context(nc.semaphore(f"weights_loaded{s}")) for s in range(4)]
        self.used = ctx.enter_context(nc.semaphore("weights_used"))
        self.rounded = ctx.enter_context(nc.semaphore("weights_rounded"))
        self.split = ctx.enter_context(nc.semaphore("weights_split"))
        self.units = []
        self.issued = 0
        self.taken = 0
        self.done = {"act": 0, "dve": 0}
        self.base = 0
        self.limit = None
        self.slots = 4

    def restart(self, at):
        self.base = self.issued = self.taken = self.done["act"] = self.done["dve"] = at

    def add(self, source, *dims):
        self.units.append((source, dims))

    def add_pair(self, source, a_, b_, by_rows):
        for h in range(2):
            if by_rows:
                self.add(source[:, a_ // 2 * h:a_ // 2 * h + a_ // 2, :], a_ // 2, b_)
            else:
                self.add(source[:, :, b_ // 2 * h:b_ // 2 * h + b_ // 2], a_, b_ // 2)

    def size(self, t):
        dims = self.units[t][1]
        return dims[0] * dims[1]

    def view(self, where, slot, dims):
        return where[:, slot, 0:dims[0] * dims[1]].rearrange("p (a b) -> p a b", a=dims[0])

    def slot(self, t):
        return (t - self.base) % self.slots

    def hi_slot(self, t):
        return self.slots + (t - self.base) % (self.slots // 2)

    def landed(self, t):
        return 16 * sum(len(self.units[u][0]) if isinstance(self.units[u][0], list) else 1
                        for u in range(self.base, t + 1) if self.slot(u) == self.slot(t))

    def load(self, sp, n):
        for _ in range(n):
            if self.issued >= len(self.units):
                return
            t = self.issued
            source, dims = self.units[t]
            s = self.slot(t)
            if t - self.base >= self.slots:
                sp.wait_ge(self.used, t - self.base - self.slots + 1)
            view = self.view(self.buf, s, dims)
            if isinstance(source, list):
                w = dims[1] // len(source)
                for g, part in enumerate(source):
                    sp.dma_start(view[:, :, w * g:w * g + w], part).then_inc(self.loaded[s], 16)
            else:
                sp.dma_start(view, source).then_inc(self.loaded[s], 16)
            self.issued += 1

    def settle(self, sp):
        for t in range(max(self.base, self.issued - self.slots), self.issued):
            sp.wait_ge(self.loaded[self.slot(t)], self.landed(t))

    def ahead(self, who, eng, upto):
        end = len(self.units) if self.limit is None else self.limit
        while self.done[who] <= upto and self.done[who] < end:
            t = self.done[who]
            n = self.size(t)
            full, lo = self.buf[:, self.slot(t), 0:n], self.part[:, self.slot(t), 0:n]
            hi = self.part[:, self.hi_slot(t), 0:n]
            if who == "act":
                eng.wait_ge(self.loaded[self.slot(t)], self.landed(t))
                if t - self.base >= self.slots // 2:
                    eng.wait_ge(self.used, t - self.base - self.slots // 2 + 1)
                self.nc.scalar.activation(hi, full, ACT.Copy).then_inc(self.rounded, 1)
            else:
                eng.wait_ge(self.rounded, t - self.base + 1)
                self.nc.vector.tensor_tensor(lo, full, hi, ALU.subtract).then_inc(self.split, 1)
            self.done[who] += 1

    def take(self, pe):
        t = self.taken
        self.taken += 1
        pe.wait_ge(self.split, t - self.base + 1)
        dims = self.units[t][1]
        return self.view(self.part, self.hi_slot(t), dims), self.view(self.part, self.slot(t), dims)


def cols_of(w, k, c0, n=P):
    return w[0][:, k, c0:c0 + n], w[1][:, k, c0:c0 + n]


def build(nc, a, out):
    ctx = ExitStack()
    with ctx:
        dma_ok = ctx.enter_context(nc.allow_non_contiguous_dma(reason="weight tiles are strided"))
        ring = WeightRing(nc, ctx)

        def sb(stack, name, shape, dt=F32):
            return stack.enter_context(nc.sbuf_tensor(name, shape, dt))

        x_tok, x_part = twin(nc, ctx, "x_tok", [P, TT, D])
        xn_tok, xn_part = twin(nc, ctx, "xn_tok", [P, TT, D])
        cols = sb(ctx, "cols", [P, NCOLS])
        const_w = sum(n for _, n in CONST_W)
        const = sb(ctx, "const", [P, const_w])
        small = sb(ctx, "small", [P, 64])
        ps = ctx.enter_context(nc.psum_tensor("ps", [P, 8, 512], F32))
        K = {}
        at = 0
        for name, n in CONST_W:
            K[name] = const[:, at:at + n]
            at += n
        ident, head_sum, ones = K["ident"], K["head_sum"], K["ones"]

        def col(name, j=0, n=1):
            base, _ = COLS[name]
            return cols[:, base + j:base + j + n]

        @contextmanager
        def stage(*names):
            with ExitStack() as s:
                sems = [s.enter_context(nc.semaphore(n)) for n in names]
                with nc.Block() as block:
                    yield [block] + sems
                nums = [x.num for x in sems]
                nc.all_engine_barrier(sems_to_clear=range(min(nums), max(nums) + 1))

        def wide(w, c0):
            return w[:, c0:c0 + 512].rearrange("(k p) n -> p k n", p=P)

        def tall(w, r0, k=4):
            return w[r0:r0 + P * k, :].rearrange("(k p) n -> p k n", p=P)

        w_ada, w_in, w_in2 = a["w_ada"][0], a["w_in"][0], a["w_in_2"][0]
        for j in range(12):
            ring.add_pair(wide(w_ada, 512 * j), DK, 512, by_rows=True)
        for j in range(6):
            ring.add_pair(wide(w_in, 512 * j), DK, 512, by_rows=(j == 4))
        w_kv = a["w_kv"].rearrange("(k p) n -> p k n", p=P)
        ring.add(w_kv[:, :, 0:256], DK, 256)
        ring.add(w_kv[:, :, 256:384], DK, P)
        for n in range(3):
            for j in range(2):
                ring.add(tall(a["w_branch"][0, n], 0)[:, :, 512 * j:512 * j + 512], BC, 512)
                ring.add_pair(wide(w_in, 3328 + 1024 * n + 512 * j), DK, 512, by_rows=False)
        for j in range(2):
            ring.add_pair(wide(a["w_out"][0], 512 * j), DK, 512, by_rows=True)
        moe_at = ring.limit = len(ring.units)

        def expert(w, e):
            return w[0, e] if isinstance(e, int) else w[0, bass.ds(e, 1)].rearrange("e k n -> (e k) n")

        def up_tiles(e):
            w1 = expert(a["w1"], e)
            return [(w1[256 * j:256 * j + 256, :].rearrange("(k p) n -> p k n", p=P), (2, 2 * DFF)) for j in range(4)]

        def down_tiles(e):
            w2 = expert(a["w2"], e)
            return [(w2[512 * j:512 * j + 512, :].rearrange("(k p) n -> p k n", p=P), (4, D)) for j in range(2)]

        for src, (rows, n) in up_tiles(0)[0:2]:
            ring.add_pair(src, rows, n, by_rows=True)
        block2_at = len(ring.units)
        for j in range(4):
            ring.add_pair(wide(w_in2, 512 * j), DK, 512, by_rows=(j == 3))
        for g in range(3):
            for j in range(3):
                ring.add_pair(wide(w_in2, 2080 + 1536 * j + 512 * g), DK, 512, by_rows=(j == 2))
        for w, c0 in (("w_dn_out_2", 6688), ("w_attn_out_2", 7712)):
            for j in range(2):
                ring.add(tall(a[w][0], 0)[:, :, 512 * j:512 * j + 512], BC, 512)
                ring.add_pair(wide(w_in2, c0 + 512 * j), DK, 512, by_rows=False)
        for j in range(2):
            ring.add_pair(wide(a["w_o_2"][0], 512 * j), DK, 512, by_rows=True)
        up = a["w_ffn_up_2"][0].rearrange("(k p) (g f) -> p k g f", p=P, g=2)
        for j in range(FFC):
            ring.add([up[:, :, g, P * j:P * j + P] for g in range(2)], DK, 2 * P)
        for j in range(FFC // 2):
            ring.add(tall(a["w_ffn_down_2"][0], 256 * j, 2), 2, D)

        first_block = ctx.enter_context(ExitStack())
        mod_cols = sb(first_block, "mod_cols", [P, 48])
        gate_rows = sb(first_block, "gate_rows", [P, 2, D])
        mod = ctx.enter_context(ExitStack())
        cond, cond_lo = twin(nc, mod, "cond", [P, DK])
        cond_hi = sb(mod, "cond_hi", [P, DK], F32R)
        row_buf = sb(mod, "row_buf", [P, 2, 512])
        g_bias = sb(mod, "g_bias", [1, 2, D])
        with stage("small_loaded", "x_loaded", "cond_rounded", "cond_ready", "row_ready", "row_copied", "cols_ready") as (
                block, small_loaded, x_loaded, cond_rounded, cond_ready, row_ready, row_copied, cols_ready):
            @block.sync
            def _(sp):
                sp.dma_start(cols[:, :], a["columns"]).then_inc(small_loaded, 16)
                ring.load(sp, 4 + 8)
                sp.dma_start(x_tok[:, :, :], a["x"][0].rearrange("(t p) d -> p t d", p=P)).then_inc(x_loaded, 16)
                ring.load(sp, 16)
                sp.wait_ge(x_loaded, 16)

            @block.gpsimd
            def _(pool):
                pass

            @block.scalar
            def _(act):
                act.dma_start(const[:, :], a["const"]).then_inc(small_loaded, 16)
                act.dma_start(g_bias[:, 0, :], a["b_ada"][0:1, 2048:3072]).then_inc(small_loaded, 16)
                act.dma_start(g_bias[:, 1, :], a["b_ada"][0:1, 5120:6144]).then_inc(small_loaded, 16)
                act.wait_ge(small_loaded, 64)
                nc.scalar.activation(cond[:, :], col("c", 0, DK), ACT.Silu)
                act.drain()
                nc.scalar.activation(cond_hi[:, :], cond[:, :], ACT.Copy).then_inc(cond_rounded, 1)
                ring.ahead("act", act, 1)
                for j in range(12):
                    ring.ahead("act", act, 2 * j + 3)
                    act.wait_ge(row_ready, j + 1)
                    if j >= 2:
                        act.wait_ge(cols_ready, j - 1)
                    gate = {4: (0, 0), 5: (0, 1), 10: (1, 0), 11: (1, 1)}.get(j)
                    dst = row_buf[:, j % 2, :] if gate is None else gate_rows[:, gate[0], 512 * gate[1]:512 * gate[1] + 512]
                    nc.scalar.activation(dst, ps[:, j % 2, :], ACT.Copy).then_inc(row_copied, 1)

            @block.tensor
            def _(pe):
                pe.wait_ge(small_loaded, 64)
                pe.wait_ge(cond_ready, 1)

                def pick(j):
                    pe.wait_ge(row_copied, j + 1)
                    src = row_buf[:, j % 2, :]
                    for c in range(4):
                        last = nc.tensor.matmul(ps[:, 2, 4 * j + c:4 * j + c + 1], src[:, P * c:P * c + P] if j not in (4, 5, 10, 11) else ident[:, 0:P],
                                                ident[:, 0:1], start=True, stop=True)
                    last.then_inc(cols_ready, 1)

                for j in range(12):
                    if j >= 2:
                        pe.wait_ge(row_copied, j - 1)
                    gate = j in (4, 5, 10, 11)
                    if gate:
                        b = g_bias[0:1, 0 if j < 6 else 1, 512 * (j % 2):512 * (j % 2) + 512]
                        nc.tensor.matmul(ps[:, j % 2, :], ones[0:1, :], b, start=True, stop=False)
                    for half in range(2):
                        w = ring.take(pe)
                        for k in range(4):
                            c = 4 * half + k
                            spread = [x[:, c:c + 1].to_broadcast([P, P]) for x in (cond_hi, cond_lo)]
                            last = product(nc, ps[:, j % 2, :], spread, cols_of(w, k, 0, 512), c == 0 and not gate, c == DK - 1)
                        last.then_inc(ring.used if half == 0 else row_ready, 1)
                    pe.wait_ge(row_ready, j + 1)
                    nc.tensor.nop().then_inc(ring.used, 1)
                    if j >= 1:
                        pick(j - 1)
                pick(11)

            @block.vector
            def _(dve):
                dve.wait_ge(cond_rounded, 1)
                nc.vector.tensor_tensor(cond_lo[:, :], cond[:, :], cond_hi[:, :], ALU.subtract).then_inc(cond_ready, 1)
                ring.ahead("dve", dve, 2 * 12)
                dve.wait_ge(cols_ready, 12)
                nc.vector.tensor_tensor(mod_cols[:, :], ps[:, 2, 0:48], col("b_ada", 0, 48), ALU.add)
                dve.drain()
                for at_, norm in ((8, "norm_mix"), (32, "norm_ffn")):
                    nc.vector.scalar_tensor_tensor(mod_cols[:, at_:at_ + 8], mod_cols[:, at_:at_ + 8], 1.0,
                                                   col(norm, 0, 8), ALU.add, ALU.mult)
        mod.close()

        def norm_stage(hT, scale, shift, hi=None, lo=None):
            with stage("root_ready", "rows_ready", "turned", "turn_copied", "rounded") as (
                    block, root_ready, rows_ready, turned, turn_copied, rounded):
                @block.scalar
                def _(act):
                    for t in range(TT):
                        nc.scalar.activation(xn_tok[:, t, :], x_tok[:, t, :], ACT.Square, accum_out=small[:, t:t + 1])
                    act.drain()
                    nc.scalar.activation(small[:, 4:8], small[:, 0:4], ACT.Sqrt, scale=1.0 / D, bias=col("eps"))\
                        .then_inc(root_ready, 1)
                    for k in range(DK):
                        act.wait_ge(turned, k + 1)
                        nc.scalar.activation(hT[:, k, :], ps[:, k % 4, :], ACT.Identity, scale=scale(k),
                                             bias=shift(k) if shift else 0.0).then_inc(turn_copied, 1)
                        if hi is not None:
                            act.wait_ge(turn_copied, k + 1)
                            nc.scalar.activation(hi[:, k, :], hT[:, k, :], ACT.Copy).then_inc(rounded, 1)

                @block.vector
                def _(dve):
                    dve.wait_ge(root_ready, 1)
                    nc.vector.reciprocal(small[:, 8:12], small[:, 4:8])
                    dve.drain()
                    for t in range(TT):
                        nc.vector.tensor_scalar(xn_tok[:, t, :], x_tok[:, t, :], small[:, 8 + t:9 + t], None,
                                                ALU.mult).then_inc(rows_ready, 1)
                    if hi is not None:
                        for k in range(DK):
                            dve.wait_ge(rounded, k + 1)
                            nc.vector.tensor_tensor(lo[:, k, :], hT[:, k, :], hi[:, k, :], ALU.subtract)

                @block.tensor
                def _(pe):
                    pe.wait_ge(rows_ready, TT)
                    for k in range(DK):
                        if k >= 4:
                            pe.wait_ge(turn_copied, k - 3)
                        for t in range(TT):
                            last = nc.tensor.transpose(ps[:, k % 4, P * t:P * t + P], xn_tok[:, t, P * k:P * k + P], ident)
                        last.then_inc(turned, 1)

        mixer = ctx.enter_context(ExitStack())
        in_ring = lambda x: x[:, 6:8, :].rearrange("p s n -> p (s n)").rearrange("p (k t) -> p k t", k=DK)
        hT_full, hT_lo = in_ring(ring.buf), in_ring(ring.part)
        hT_hi = sb(mixer, "hT_hi", [P, DK, T], F32R)
        hT = (hT_hi, hT_lo)
        norm_stage(hT_full, lambda k: mod_cols[:, 8 + k:9 + k], lambda k: mod_cols[:, k:k + 1], *hT)
        def project(hT, tiles, act_scratch):
            groups = [(ti, g) for ti, gs in enumerate(tiles) for g in gs]
            norms = [n for n, (_, g) in enumerate(groups) if g[0] == "norm"]
            unit_of, units = [], 0
            for gs in tiles:
                token = gs[0][0] == "token"
                unit_of += [units + (1 if token else gi // 2) for gi in range(len(gs))]
                units += 2 if token else (len(gs) + 1) // 2
            first_unit = ring.taken
            with stage("group_ready", "squared", "summed", "rooted", "bank_free0", "bank_free1", "bank_free2",
                       "bank_free3") as (block, group_ready, squared, summed, rooted, *bank_free):
                def freed(eng, n):
                    eng.wait_ge(bank_free[n % 4], n // 4 + 1)

                @block.sync
                def _(sp):
                    ring.load(sp, units)

                @block.tensor
                def _(pe):
                    def sum_heads(m):
                        pe.wait_ge(squared, m + 1)
                        if m >= 2:
                            pe.wait_ge(rooted, m - 1)
                        nc.tensor.matmul(ps[:, 4 + m % 2, :], head_sum, act_scratch[:, m % 2, :], start=True, stop=True)\
                            .then_inc(summed, 1)

                    n, m = 0, 0
                    for gs in tiles:
                        if gs[0][0] == "token":
                            if n and groups[n - 1][1][0] == "norm":
                                sum_heads(m)
                                m += 1
                            for half in range(2):
                                w = ring.take(pe)
                                for t, g in enumerate(gs):
                                    if n + t >= 4 and half == 0:
                                        freed(pe, n + t - 4)
                                    for k in range(4):
                                        c = 4 * half + k
                                        last = product(nc, ps[:, (n + t) % 4, :], (g[1](hT[0], c), g[1](hT[1], c)), cols_of(w, k, 0, 512),
                                                       c == 0, c == DK - 1)
                                    if half == 1:
                                        last.then_inc(group_ready, 1)
                                if half == 0:
                                    last.then_inc(ring.used, 1)
                            n += 4
                            pe.wait_ge(group_ready, n)
                            nc.tensor.nop().then_inc(ring.used, 1)
                            continue
                        for gi, g in enumerate(gs):
                            if gi % 2 == 0:
                                w = ring.take(pe)
                            if n >= 4:
                                freed(pe, n - 4)
                            for k in range(DK):
                                last = product(nc, ps[:, n % 4, :], cols_of(w, k, P * (gi % 2)), (hT[0][:, k, :], hT[1][:, k, :]),
                                               k == 0, k == DK - 1)
                            last.then_inc(group_ready, 1)
                            n += 1
                            if n >= 2 and groups[n - 2][1][0] == "norm":
                                sum_heads(m)
                                m += 1
                            if gi % 2 == 1 or gi == len(gs) - 1:
                                pe.wait_ge(group_ready, n)
                                nc.tensor.nop().then_inc(ring.used, 1)
                    if groups[-1][1][0] == "norm":
                        sum_heads(m)

                @block.scalar
                def _(act):
                    def root(m):
                        act.wait_ge(summed, m + 1)
                        if m >= 2:
                            freed(act, norms[m - 2])
                        g = groups[norms[m]][1]
                        nc.scalar.activation(act_scratch[:, 2 + m % 2, :], ps[:, 4 + m % 2, :], ACT.Sqrt,
                                             scale=(1.0 / HD if g[3] else 1.0), bias=col("eps")).then_inc(rooted, 1)

                    m, rooted_ = 0, 0
                    for n, (_, g) in enumerate(groups):
                        if g[0] == "token" and rooted_ < m:
                            root(rooted_)
                            rooted_ += 1
                        ring.ahead("act", act, first_unit + unit_of[n] + 1)
                        act.wait_ge(group_ready, n + 1)
                        if g[0] == "norm":
                            if m >= 2:
                                act.wait_ge(summed, m - 1)
                            nc.scalar.activation(act_scratch[:, m % 2, :], ps[:, n % 4, :], ACT.Square).then_inc(squared, 1)
                            m += 1
                        elif g[0] == "chan":
                            nc.scalar.activation(g[2], ps[:, n % 4, :], g[1]).then_inc(bank_free[n % 4], 1)
                        else:
                            nc.scalar.activation(g[3], ps[:, n % 4, :], g[2]).then_inc(bank_free[n % 4], 1)
                        if n >= 1 and groups[n - 1][1][0] == "norm" and g[0] != "token":
                            root(rooted_)
                            rooted_ += 1
                    if rooted_ < m:
                        root(rooted_)

                @block.vector
                def _(dve):
                    for m, n in enumerate(norms):
                        _, gain, dst, _ = groups[n][1]
                        ring.ahead("dve", dve, first_unit + unit_of[n] + 1)
                        rinv = act_scratch[:, 2 + m % 2, :]
                        dve.wait_ge(rooted, m + 1)
                        nc.vector.reciprocal(rinv, rinv)
                        dve.drain()
                        nc.vector.scalar_tensor_tensor(dst, ps[:, n % 4, :], gain, rinv, ALU.mult, ALU.mult)\
                            .then_inc(bank_free[n % 4], 1)
                    ring.ahead("dve", dve, first_unit + units)

        oT, oT_part = twin(nc, mixer, "branchesT", [P, 3, BC, T])
        work, work_part = twin(nc, mixer, "work", [P, 4096 + 1024])
        x_flat = x_tok[:, :, :].rearrange("p t d -> p (t d)")
        xn_flat = xn_tok[:, :, :].rearrange("p t d -> p (t d)")

        def chan(buf, at_, n=BC, w=T):
            return buf[:, at_:at_ + n * w].rearrange("p (c t) -> p c t", c=n)

        scratch4 = work[:, 0:2048].rearrange("p (a b) -> p a b", a=4)

        xp = chan(x_flat, 0, BC, T + 4)
        gelu, xc = chan(xn_flat, 0), chan(xn_flat, 2048)
        r_gate, i_gate = oT[:, 1], oT[:, 2]
        a_dec, mult_ = chan(x_flat, 0), chan(x_flat, 2048)
        lru_w = work[:, 2048:3072].rearrange("p (g c j) -> p g c j", g=2, c=BC)
        a_scale = small[:, 16:20]
        project(hT, [[("chan", ACT.Copy, xp[:, m, 3:3 + T]) for m in range(BC)],
                     [("chan", ACT.Gelu_apprx_tanh, gelu[:, m, :]) for m in range(BC)]], scratch4)
        with stage("lru_loaded", "lam_exp", "lam_abs", "lam_ln", "conv_ready", "gates_ready", "gates_done", "decay_ready",
                   "tanh_ready", "square_ready", "mult_ready") as (
                block, lru_loaded, lam_exp, lam_abs, lam_ln, conv_ready, gates_ready, gates_done, decay_ready,
                tanh_ready, square_ready, mult_ready):
            @block.sync
            def _(sp):
                sp.dma_start(lru_w[:, 0], a["lru_a"].rearrange("p (c j) -> p c j", c=BC)).then_inc(lru_loaded, 16)
                sp.dma_start(lru_w[:, 1], a["lru_x"].rearrange("p (c j) -> p c j", c=BC)).then_inc(lru_loaded, 16)
                sp.wait_ge(lru_loaded, 32)

            @block.vector
            def _(dve):
                nc.vector.scalar_tensor_tensor(small[:, 20:24], col("lru_lambda", 0, BC), -1.0, col("lru_lambda", 0, BC),
                                               ALU.mult, ALU.max).then_inc(lam_abs, 1)
                nc.vector.memset(xp[:, :, 0:3], 0.0)
                dve.drain()
                for c in range(BC):
                    taps = [col("conv_w", 4 * c + k) for k in range(4)]
                    nc.vector.tensor_scalar(xc[:, c, :], xp[:, c, 0:T], taps[0], col("conv_b", c), ALU.mult, ALU.add)
                    for k in range(1, 4):
                        dve.drain()
                        last = nc.vector.scalar_tensor_tensor(xc[:, c, :], xp[:, c, k:k + T], taps[k], xc[:, c, :],
                                                              ALU.mult, ALU.add)
                    last.then_inc(conv_ready, 1)
                dve.wait_ge(lam_exp, 2)
                nc.vector.tensor_scalar(small[:, 24:28], col("lru_lambda", 0, BC), -1.0, 0.0, ALU.mult, ALU.max)
                dve.drain()
                nc.vector.tensor_tensor(small[:, 24:28], small[:, 24:28], small[:, 20:24], ALU.add)
                dve.drain()
                nc.vector.tensor_scalar(a_scale, small[:, 24:28], -8.0, None, ALU.mult).then_inc(lam_ln, 1)
                dve.wait_ge(decay_ready, 1)
                nc.vector.tensor_tensor(xc[:, :, :], xc[:, :, :], i_gate[:, :, :], ALU.mult)
                dve.drain()
                nc.vector.tensor_tensor(i_gate[:, :, :], a_dec[:, :, :], a_dec[:, :, :], ALU.mult)
                dve.wait_ge(tanh_ready, 1)
                dve.drain()
                nc.vector.scalar_tensor_tensor(mult_[:, :, :], i_gate[:, :, :], 1.0, mult_[:, :, :], ALU.add, ALU.mult)\
                    .then_inc(square_ready, 1)
                dve.wait_ge(mult_ready, 1)
                nc.vector.tensor_tensor(xc[:, :, :], xc[:, :, :], mult_[:, :, :], ALU.mult)
                dve.drain()
                for c in range(BC):
                    nc.vector.tensor_tensor_scan(oT[:, 0, c, :], a_dec[:, c, :], xc[:, c, :], 0.0, ALU.mult, ALU.add)
                dve.drain()
                nc.vector.tensor_tensor(oT[:, 0], oT[:, 0], gelu[:, :, :], ALU.mult)

            @block.tensor
            def _(pe):
                pe.wait_ge(lru_loaded, 32)
                for c in range(BC):
                    pe.wait_ge(conv_ready, c + 1)
                    nc.tensor.matmul(ps[:, 2 * c, :], lru_w[:, 0, c, :], xc[:, c, :], start=True, stop=True)
                    nc.tensor.matmul(ps[:, 2 * c + 1, :], lru_w[:, 1, c, :], xc[:, c, :], start=True, stop=True)\
                        .then_inc(gates_ready, 1)

            @block.scalar
            def _(act):
                act.wait_ge(lam_abs, 1)
                nc.scalar.activation(small[:, 20:24], small[:, 20:24], ACT.Exp, scale=-1.0).then_inc(lam_exp, 1)
                act.wait_ge(lam_exp, 1)
                nc.scalar.activation(small[:, 20:24], small[:, 20:24], ACT.Ln, bias=col("one")).then_inc(lam_exp, 1)
                for c in range(BC):
                    act.wait_ge(gates_ready, c + 1)
                    nc.scalar.activation(r_gate[:, c, :], ps[:, 2 * c, :], ACT.Sigmoid, bias=col("lru_ba", c))
                    nc.scalar.activation(i_gate[:, c, :], ps[:, 2 * c + 1, :], ACT.Sigmoid, bias=col("lru_bx", c))
                act.drain()
                act.wait_ge(lam_ln, 1)
                for c in range(BC):
                    last = nc.scalar.activation(a_dec[:, c, :], r_gate[:, c, :], ACT.Exp, scale=a_scale[:, c:c + 1])
                act.drain().then_inc(decay_ready, 1)
                for c in range(BC):
                    nc.scalar.activation(mult_[:, c, :], r_gate[:, c, :], ACT.Tanh, scale=a_scale[:, c:c + 1])
                act.drain().then_inc(tanh_ready, 1)
                act.wait_ge(square_ready, 1)
                nc.scalar.activation(mult_[:, :, :], mult_[:, :, :], ACT.Sqrt, scale=-1.0).then_inc(mult_ready, 1)
        def attention(units, stats, s_buf, p_turned):
            N = len(units)
            at_ = [sum(u["seg"][0] for u in units[:i]) for i in range(N + 1)]

            def seg_view(flat, u):
                n, pitch, w = u["seg"]
                return flat[:, 0:n * pitch].rearrange("p (n w) -> p n w", n=n)[:, :, 0:w]

            s_bank = [ps[:, 2 * b:2 * b + 2, :].rearrange("p b n -> p (b n)") for b in range(2)]
            t_bank = ps[:, 4:6, :].rearrange("p b n -> p (b n)")
            with stage("scores_ready", "scores_read", "maxima_ready", "exps_ready", "probs_ready", "turned", "turned_read",
                       "values_ready", "values_read", "sinks_ready") as (
                    block, scores_ready, scores_read, maxima_ready, exps_ready, probs_ready, turned, turned_read,
                    values_ready, values_read, sinks_ready):
                @block.tensor
                def _(pe):
                    def turn(i):
                        u = units[i]
                        pe.wait_ge(probs_ready, i + 1)
                        if i >= 1:
                            pe.wait_ge(turned_read, i)
                        for j, c in enumerate(u["turns"]):
                            last = nc.tensor.transpose(t_bank[:, P * j:P * j + P], s_buf[:, i % 3, c:c + P], ident)
                        last.then_inc(turned, 1)

                    def weigh(i):
                        u = units[i]
                        pe.wait_ge(turned_read, i + 1)
                        if i >= 2:
                            pe.wait_ge(values_read, i - 1)
                        for rows, c, terms in u["pv"]:
                            for n, (v, j) in enumerate(terms):
                                last = nc.tensor.matmul(ps[rows, 6 + i % 2, c:c + P], v, p_turned[:, P * j:P * j + P],
                                                        start=(n == 0), stop=(n == len(terms) - 1))
                        last.then_inc(values_ready, 1)

                    for i in range(N + 2):
                        if i >= 2:
                            turn(i - 2)
                        if i < N:
                            if i >= 2:
                                pe.wait_ge(scores_read, i - 1)
                            for c, w, lhsT, rhs in units[i]["scores"]:
                                last = nc.tensor.matmul(s_bank[i % 2][:, c:c + w], lhsT, rhs, start=True, stop=True)
                            last.then_inc(scores_ready, 1)
                        if i >= 2:
                            weigh(i - 2)

                @block.scalar
                def _(act):
                    for i in range(N + 2):
                        if i >= 2:
                            act.wait_ge(turned, i - 1)
                            if i >= 3:
                                act.wait_ge(values_ready, i - 2)
                            m = P * len(units[i - 2]["turns"])
                            nc.scalar.activation(p_turned[:, 0:m], t_bank[:, 0:m], ACT.Copy).then_inc(turned_read, 1)
                        if i < N:
                            u = units[i]
                            n, pitch, w = u["seg"]
                            act.wait_ge(maxima_ready, i + 1)
                            if u.get("sinks") is not None:
                                sl = stats[:, 2, at_[i]:at_[i + 1]]
                                nc.scalar.activation(sl, sl, ACT.Exp).then_inc(sinks_ready, 1)
                            for j in range(n):
                                s = s_buf[:, i % 3, pitch * j:pitch * j + w]
                                last = nc.scalar.activation(s, s, ACT.Exp, bias=stats[:, 0, at_[i] + j:at_[i] + j + 1],
                                                            accum_out=stats[:, 1, at_[i] + j:at_[i] + j + 1])
                            act.drain().then_inc(exps_ready, 1)

                @block.vector
                def _(dve):
                    def read_out(i):
                        dve.wait_ge(values_ready, i + 1)
                        for dst, rows, c in units[i]["out"]:
                            src = ps[rows, 6 + i % 2, c]
                            if len(dst.shape) == 3:
                                src = src.rearrange("p (a b) -> p a b", a=dst.shape[1])
                            last = nc.vector.tensor_copy(dst, src)
                        last.then_inc(values_read, 1)

                    n_sinks = 0
                    for i in range(N + 3):
                        if i < N:
                            u = units[i]
                            n, pitch, w = u["seg"]
                            neg_m = stats[:, 0, at_[i]:at_[i + 1]]
                            dve.wait_ge(scores_ready, i + 1)
                            if i >= 3:
                                dve.wait_ge(turned, i - 2)
                            s = seg_view(s_buf[:, i % 3, :], u)
                            nc.vector.tensor_tensor(s, seg_view(s_bank[i % 2], u), u["bias"], ALU.add).then_inc(scores_read, 1)
                            dve.drain()
                            if u.get("sinks") is None:
                                nc.vector.tensor_reduce(neg_m, s, AX.X, ALU.max, negate=True)
                            else:
                                nc.vector.tensor_reduce(neg_m, s, AX.X, ALU.max)
                                dve.drain()
                                nc.vector.tensor_tensor(neg_m, neg_m, u["sinks"], ALU.max)
                                dve.drain()
                                nc.vector.tensor_scalar(neg_m, neg_m, -1.0, None, ALU.mult)
                                dve.drain()
                                nc.vector.tensor_tensor(stats[:, 2, at_[i]:at_[i + 1]], u["sinks"], neg_m, ALU.add)
                            dve.drain().then_inc(maxima_ready, 1)
                        if 1 <= i <= N:
                            k = i - 1
                            u = units[k]
                            n, pitch, w = u["seg"]
                            sums, recip = stats[:, 1, at_[k]:at_[k + 1]], stats[:, 2, at_[k]:at_[k + 1]]
                            s = seg_view(s_buf[:, k % 3, :], u)
                            dve.wait_ge(exps_ready, k + 1)
                            if u.get("sinks") is not None:
                                n_sinks += 1
                                dve.wait_ge(sinks_ready, n_sinks)
                                nc.vector.tensor_tensor(sums, sums, recip, ALU.add)
                                dve.drain()
                            nc.vector.reciprocal(recip, sums)
                            dve.drain()
                            if u.get("lam") is None:
                                nc.vector.tensor_tensor(s, s, recip.unsqueeze(2).to_broadcast([P, n, w]), ALU.mult)\
                                    .then_inc(probs_ready, 1)
                            else:
                                nc.vector.tensor_tensor(recip[:, 1:2], recip[:, 1:2], u["lam"], ALU.mult)
                                nc.vector.tensor_scalar(s[:, 0, :], s[:, 0, :], recip[:, 0:1], None, ALU.mult)
                                dve.drain()
                                nc.vector.scalar_tensor_tensor(s[:, 0, :], s[:, 1, :], recip[:, 1:2], s[:, 0, :],
                                                               ALU.mult, ALU.add).then_inc(probs_ready, 1)
                        if i >= 3:
                            read_out(i - 3)

        stats = sb(mixer, "stats", [P, 3, 96])
        s_buf = ring.buf[:, 8:10, :].rearrange("p s n -> p (s n)")[:, 0:3072].rearrange("p (a b) -> p a b", a=3)
        p_turned = work[:, 2048:3072]

        dqT, dkT = chan(xn_flat, 0), chan(xn_flat, 2048)
        dv = x_flat[:, 0:2048].rearrange("p (t e) -> p t e", t=TT)
        diff_bias = x_flat[:, 2048:4096].rearrange("p (h x) -> p h x", h=4)
        swa_bias = work[:, 3072:5120].rearrange("p (h x) -> p h x", h=8)
        gains = small[:, 32:34]
        minus_lam = small[:, 34:35]

        def token_groups(dst):
            return [("token", (lambda h, k, t=t: h[:, k, P * t:P * t + P]), ACT.Copy, dst[:, t, :])
                    for t in range(TT)]

        bias_rows = nc.dram_tensor("bias_rows", (N_BIAS_HEADS, TOEP), F32)
        with stage("bias_loaded", "lam_sums", "lam_exps", "rows_ready", "rows_summed", "rows_stored", "shifted", "flipped") as (
                block, bias_loaded, lam_sums, lam_exps, rows_ready, rows_summed, rows_stored, shifted, flipped):
            onehot, mask = work[0:BUCKETS, 0:TOEP], work[0:N_BIAS_HEADS, 640:1280]
            rel_bias, rows = work[0:BUCKETS, 1280:1280 + N_BIAS_HEADS], work[0:N_BIAS_HEADS, 1408:2048]
            shift_d = xn_flat[:, 0:2048].rearrange("p (h x) -> p h x", h=4)
            shift_s = xn_flat[:, 2048:4096].rearrange("p (h x) -> p h x", h=8)
            half = TOEP // 2

            @block.sync
            def _(sp):
                sp.dma_start(onehot, a["bucket_onehot"]).then_inc(bias_loaded, 16)
                sp.dma_start(mask, a["bucket_mask"]).then_inc(bias_loaded, 16)
                sp.dma_start(rel_bias, a["rel_bias"]).then_inc(bias_loaded, 16)
                sp.wait_ge(rows_summed, 1)
                sp.dma_start(bias_rows.ap(), rows).then_inc(rows_stored, 16)
                sp.wait_ge(rows_stored, 16)
                src = bass.AP(tensor=bias_rows.ap().tensor, offset=0, ap=[[1, P], [TOEP, 4], [1, 512]])
                sp.dma_start(shift_d, src).then_inc(shifted, 16)
                src = bass.AP(tensor=bias_rows.ap().tensor, offset=4 * TOEP + 256, ap=[[1, P], [TOEP, 8], [1, 256]])
                sp.dma_start(shift_s, src).then_inc(shifted, 16)

            @block.tensor
            def _(pe):
                pe.wait_ge(bias_loaded, 48)
                for j in range(2):
                    last = nc.tensor.matmul(ps[0:N_BIAS_HEADS, j, 0:half], rel_bias, onehot[:, half * j:half * j + half],
                                            start=True, stop=True)
                last.then_inc(rows_ready, 1)
                pe.wait_ge(rows_summed, 1)
                pe.wait_ge(shifted, 32)
                for j in range(8):
                    src = shift_d[:, j, :] if j < 4 else shift_s[:, 2 * j - 8:2 * j - 6, :]
                    nc.tensor.matmul(ps[:, j, :], K["flip"], src, start=True, stop=True).then_inc(flipped, 1)

            @block.scalar
            def _(act):
                act.wait_ge(lam_sums, 1)
                nc.scalar.activation(small[:, 36:38], small[:, 36:38], ACT.Exp).then_inc(lam_exps, 1)
                for j in range(4):
                    act.wait_ge(flipped, j + 1)
                    nc.scalar.activation(diff_bias[:, j, :], ps[:, j, :], ACT.Copy)

            @block.vector
            def _(dve):
                nc.vector.tensor_scalar(gains[:, 0:1], col("diff_qnorm"), HD ** -0.5, None, ALU.mult)
                nc.vector.tensor_scalar(gains[:, 1:2], col("swa_qnorm"), HD ** -0.5, None, ALU.mult)
                lv = [col("diff_lambda", HD * j, HD) for j in range(4)]
                prod = work[:, 3072:3072 + 2 * HD].rearrange("p (a b) -> p a b", a=2)
                nc.vector.tensor_tensor(prod[:, 0, :], lv[0], lv[1], ALU.mult)
                nc.vector.tensor_tensor(prod[:, 1, :], lv[2], lv[3], ALU.mult)
                dve.drain()
                nc.vector.tensor_reduce(small[:, 36:38], prod, AX.X, ALU.add).then_inc(lam_sums, 1)
                dve.wait_ge(rows_ready, 1)
                for j in range(2):
                    last = nc.vector.tensor_tensor(rows[:, half * j:half * j + half], ps[0:N_BIAS_HEADS, j, 0:half],
                                                   mask[:, half * j:half * j + half], ALU.add)
                dve.drain().then_inc(rows_summed, 1)
                dve.wait_ge(lam_exps, 1)
                nc.vector.tensor_tensor(minus_lam, small[:, 37:38], small[:, 36:37], ALU.subtract)
                dve.drain()
                nc.vector.tensor_scalar(minus_lam, minus_lam, -LAMBDA_INIT, None, ALU.add)
                for j in range(4, 8):
                    dve.wait_ge(flipped, j + 1)
                    nc.vector.tensor_copy(swa_bias[:, 2 * j - 8:2 * j - 6, :], ps[:, j, :].rearrange("p (h x) -> p h x", h=2))

        project(hT, [[("norm", gains[:, 0:1], dqT[:, m, :], True) for m in range(BC)],
                     [("norm", col("diff_knorm"), dkT[:, m, :], True) for m in range(BC)],
                     token_groups(dv)], scratch4)
        units = []
        for h in range(4):
            for t in range(TT):
                w = P * (t + 1)
                units.append(dict(
                    scores=[(512 * m, w, dqT[HD * m:HD * m + HD, h, P * t:P * t + P], dkT[HD * m:HD * m + HD, h, 0:w]) for m in range(2)],
                    seg=(2, 512, w), lam=minus_lam,
                    bias=diff_bias[:, h, P * (3 - t):512].unsqueeze(1).to_broadcast([P, 2, w]),
                    turns=[P * j for j in range(t + 1)],
                    pv=[(slice(0, P), 0, [(dv[:, j, P * h:P * h + P], j) for j in range(t + 1)])],
                    out=[(oT[:, 1, h, P * t:P * t + P], slice(0, P), slice(0, P))]))
        attention(units, stats, s_buf, p_turned)

        with stage("squared", "summed", "rooted") as (block, squared, summed, rooted):
            @block.tensor
            def _(pe):
                for h in range(4):
                    pe.wait_ge(squared, h + 1)
                    nc.tensor.matmul(ps[:, h, :], ones, scratch4[:, h, :], start=True, stop=True).then_inc(summed, 1)

            @block.scalar
            def _(act):
                for h in range(4):
                    nc.scalar.activation(scratch4[:, h, :], oT[:, 1, h, :], ACT.Square).then_inc(squared, 1)
                for h in range(4):
                    act.wait_ge(summed, h + 1)
                    nc.scalar.activation(scratch4[:, h, :], ps[:, h, :], ACT.Sqrt, scale=1.0 / P, bias=col("eps")).then_inc(rooted, 1)

            @block.vector
            def _(dve):
                nc.vector.tensor_scalar(small[:, 40:41], col("diff_subln"), 1.0 - LAMBDA_INIT, None, ALU.mult)
                for h in range(4):
                    dve.wait_ge(rooted, h + 1)
                    nc.vector.reciprocal(scratch4[:, h, :], scratch4[:, h, :])
                    dve.drain()
                    nc.vector.scalar_tensor_tensor(oT[:, 1, h, :], oT[:, 1, h, :], small[:, 40:41], scratch4[:, h, :],
                                                   ALU.mult, ALU.mult)

        sqT = chan(xn_flat, 0)
        skT = chan(xn_flat, 2048, 2)
        sv = xn_flat[:, 3072:3584].rearrange("p (t e) -> p t e", t=TT)
        scratch_x = x_flat[:, 0:2048].rearrange("p (a b) -> p a b", a=4)
        svT = xn_flat[:, 3584:4096]
        project(hT, [[("norm", gains[:, 1:2], sqT[:, m, :], True) for m in range(BC)],
                     [("norm", col("swa_knorm"), skT[:, g, :], True) for g in range(2)] + [("chan", ACT.Copy, svT)]], scratch_x)
        with stage("turned") as (block, turned):
            @block.tensor
            def _(pe):
                for t in range(TT):
                    last = nc.tensor.transpose(ps[:, 0, P * t:P * t + P], svT[:, P * t:P * t + P], ident)
                last.then_inc(turned, 1)

            @block.scalar
            def _(act):
                act.wait_ge(turned, 1)
                nc.scalar.activation(sv, ps[:, 0, :].rearrange("p (t e) -> p t e", t=TT), ACT.Copy)
        units = []
        for t in range(TT):
            for g in range(2):
                w = 2 * P if t else P
                k0 = P * (t - 1) if t else 0
                sc, pv, o = [], [], []
                for j in range(4):
                    h = 4 * g + SWA_ORDER[j]
                    r = slice(HD * (h % 2), HD * (h % 2) + HD)
                    sc.append((2 * P * j, w, sqT[r, h // 2, P * t:P * t + P], skT[r, g, k0:k0 + w]))
                    nt = w // P
                    pv.append((r, P * (SWA_ORDER[j] // 2), [(sv[:, (t - 1 if t else 0) + m, HD * g:HD * g + HD], nt * j + m) for m in range(nt)]))
                units.append(dict(
                    scores=sc, seg=(4, 2 * P, w), bias=swa_bias[:, 4 * g:4 * g + 4, 2 * P - w:2 * P],
                    sinks=col("swa_sinks", 4 * g, 4), turns=[2 * P * j + P * m for j in range(4) for m in range(w // P)],
                    pv=pv, out=[(oT[:, 2, 2 * g:2 * g + 2, P * t:P * t + P], slice(0, P), slice(0, 2 * P))]))
        attention(units, stats, s_buf, p_turned)
        def merge_branches(hT, sources, mergedT, sig, gated):
            NB = len(sources)
            first_unit = ring.taken
            with stage("source_rounded", "source_ready", "gate_ready", "branch_ready", "sig_ready", "merged") as (
                    block, source_rounded, source_ready, gate_ready, branch_ready, sig_ready, merged):
                @block.sync
                def _(sp):
                    ring.load(sp, 6 * NB)

                @block.tensor
                def _(pe):
                    for p in range(2 * NB):
                        w = ring.take(pe)
                        pe.wait_ge(source_ready, p // 2 + 1)
                        for m in range(4):
                            if p:
                                pe.wait_ge(merged, 4 * (p - 1) + m + 1)
                            for k in range(BC):
                                _, hi, lo = sources[p // 2]
                                last = product(nc, ps[:, 4 + m, :], cols_of(w, k, P * m), (hi[:, k, :], lo[:, k, :]), k == 0, k == BC - 1)
                            last.then_inc(branch_ready, 1)
                        pe.wait_ge(branch_ready, 4 * p + 4)
                        nc.tensor.nop().then_inc(ring.used, 1)
                        for m in range(4):
                            if m % 2 == 0:
                                w = ring.take(pe)
                            if p:
                                pe.wait_ge(sig_ready, 4 * (p - 1) + m + 1)
                            for k in range(DK):
                                last = product(nc, ps[:, m, :], cols_of(w, k, P * (m % 2)), (hT[0][:, k, :], hT[1][:, k, :]), k == 0, k == DK - 1)
                            last.then_inc(gate_ready, 1)
                            if m % 2 == 1:
                                pe.wait_ge(gate_ready, 4 * p + m + 1)
                                nc.tensor.nop().then_inc(ring.used, 1)

                @block.scalar
                def _(act):
                    def round_source(n):
                        full, hi, _ = sources[n]
                        nc.scalar.activation(hi, full, ACT.Copy).then_inc(source_rounded, 1)

                    round_source(0)
                    for p in range(2 * NB):
                        ring.ahead("act", act, first_unit + 3 * p + 1)
                        if p % 2 == 0 and p // 2 + 1 < NB:
                            round_source(p // 2 + 1)
                        for m in range(4):
                            i = 4 * p + m
                            ring.ahead("act", act, first_unit + 3 * p + 2 + m // 2)
                            act.wait_ge(gate_ready, i + 1)
                            if i >= 2:
                                act.wait_ge(merged, i - 1)
                            nc.scalar.activation(sig[:, i % 2, :], ps[:, m, :], ACT.Sigmoid).then_inc(sig_ready, 1)

                @block.vector
                def _(dve):
                    def split_source(n):
                        full, hi, lo = sources[n]
                        dve.wait_ge(source_rounded, n + 1)
                        nc.vector.tensor_tensor(lo, full, hi, ALU.subtract).then_inc(source_ready, 1)

                    split_source(0)
                    for p in range(2 * NB):
                        ring.ahead("dve", dve, first_unit + 3 * p + 1)
                        if p % 2 == 0 and p // 2 + 1 < NB:
                            split_source(p // 2 + 1)
                        for m in range(4):
                            i, row = 4 * p + m, 4 * (p % 2) + m
                            ring.ahead("dve", dve, first_unit + 3 * p + 2 + m // 2)
                            dve.wait_ge(branch_ready, i + 1)
                            dve.wait_ge(sig_ready, i + 1)
                            dst = mergedT[:, row, :] if p < 2 else gated[:, i % 2, :]
                            nc.vector.tensor_tensor(dst, sig[:, i % 2, :], ps[:, 4 + m, :], ALU.mult).then_inc(merged, 1)
                            if p >= 2:
                                dve.drain()
                                nc.vector.tensor_tensor(mergedT[:, row, :], mergedT[:, row, :], gated[:, i % 2, :], ALU.add)

        half_x = lambda x, n: x.rearrange("p t d -> p (t d)")[:, 2048 * n:2048 * n + 2048].rearrange("p (c t) -> p c t", c=BC)
        his = [half_x(x_part[:, :, :], 0), half_x(x_part[:, :, :], 1), work_part[:, 2048:4096].rearrange("p (c t) -> p c t", c=BC)]
        merge_branches(hT, [(oT[:, n], his[n], oT_part[:, n]) for n in range(3)], chan(xn_flat, 0, DK),
                       work[:, 0:1024].rearrange("p (a b) -> p a b", a=2), work[:, 1024:2048].rearrange("p (a b) -> p a b", a=2))

        def project_out(srcT, gate, load_x=False):
            full, hi, lo = srcT
            first_unit = ring.taken
            with stage("rounded", "split", "out_ready", "x_loaded") as (block, rounded, split, out_ready, x_loaded):
                @block.sync
                def _(sp):
                    if load_x:
                        sp.dma_start(x_tok[:, :, :], a["x"][0].rearrange("(t p) d -> p t d", p=P)).then_inc(x_loaded, 16)
                    ring.load(sp, 4)

                @block.tensor
                def _(pe):
                    for j in range(2):
                        for half in range(2):
                            w = ring.take(pe)
                            for t in range(TT):
                                for k in range(4):
                                    c = 4 * half + k
                                    if t == 0 and j == 0:
                                        pe.wait_ge(split, c + 1)
                                    last = product(nc, ps[:, 4 * j + t, :], cols_of((hi, lo), c, P * t), cols_of(w, k, 0, 512),
                                                   c == 0, c == DK - 1)
                                if half == 1:
                                    last.then_inc(out_ready, 1)
                            if half == 0:
                                last.then_inc(ring.used, 1)
                        pe.wait_ge(out_ready, 4 * j + 4)
                        nc.tensor.nop().then_inc(ring.used, 1)

                @block.scalar
                def _(act):
                    for k in range(DK):
                        nc.scalar.activation(hi[:, k, :], full[:, k, :], ACT.Copy).then_inc(rounded, 1)
                    ring.ahead("act", act, first_unit + 4)

                @block.vector
                def _(dve):
                    for k in range(DK):
                        dve.wait_ge(rounded, k + 1)
                        nc.vector.tensor_tensor(lo[:, k, :], full[:, k, :], hi[:, k, :], ALU.subtract).then_inc(split, 1)
                    for j in range(2):
                        ring.ahead("dve", dve, first_unit + 2 * j + 2)
                        for t in range(TT):
                            x = x_tok[:, t, 512 * j:512 * j + 512]
                            dve.wait_ge(out_ready, 4 * j + t + 1)
                            src = ps[:, 4 * j + t, :]
                            if gate is not None:
                                src = work[:, 512 * t:512 * t + 512]
                                nc.vector.tensor_tensor(src, ps[:, 4 * j + t, :], gate[:, 512 * j:512 * j + 512], ALU.mult)
                                dve.drain()
                            if load_x and j == 0 and t == 0:
                                dve.wait_ge(x_loaded, 16)
                            nc.vector.tensor_tensor(x, x, src, ALU.add)
                    ring.ahead("dve", dve, first_unit + 4)

        as_chunks = lambda x: x.rearrange("p t d -> p (t d)").rearrange("p (c t) -> p c t", c=DK)
        mergedT = (chan(xn_flat, 0, DK), hT_hi, as_chunks(xn_part[:, :, :]))
        project_out(mergedT, gate_rows[:, 0, :], load_x=True)
        mixer.close()
        moe = ctx.enter_context(ExitStack())
        weight_te = sb(moe, "weight_te", [P, TT, E])
        slot_te = sb(moe, "slot_te", [P, TT, E + 1])
        most = sb(moe, "most_tokens", [P, 1], I32)
        router = ctx.enter_context(ExitStack())
        hfT = sb(router, "hfT", [P, DK, T])
        norm_stage(hfT, lambda k: mod_cols[:, 32 + k:33 + k], lambda k: mod_cols[:, 24 + k:25 + k])
        w_router = sb(router, "w_router", [P, DK, E])
        b2_sb = sb(router, "b2_sb", [E, D])
        logits = sb(router, "logits", [P, TT, E])
        chosen = sb(router, "chosen", [P, TT, E])
        hot = sb(router, "hot", [P, 2, TT, E])
        top = sb(router, "top", [P, TT, 8])
        top_at = sb(router, "top_at", [P, TT, 8], U32)
        top_atf = sb(router, "top_atf", [P, TT, 8])
        soft = sb(router, "soft", [P, TT, TOPK])
        weight_et = sb(router, "weight_et", [E, T])
        iota_e = K["slot_iota"][:, 0:E].unsqueeze(1).to_broadcast([P, TT, E])
        with stage("router_loaded", "logits_ready", "tops_ready", "exps_ready", "chosen_ready", "places_ready", "places_read",
                   "turned", "turned_read", "init_ready", "init_read") as (
                block, router_loaded, logits_ready, tops_ready, exps_ready, chosen_ready, places_ready, places_read,
                turned, turned_read, init_ready, init_read):
            @block.sync
            def _(sp):
                sp.dma_start(w_router[:, :, :], a["w_router"][0].rearrange("(k p) e -> p k e", p=P)).then_inc(router_loaded, 16)
                sp.dma_start(b2_sb[:, :], a["b2"][0]).then_inc(router_loaded, 16)
                sp.wait_ge(router_loaded, 32)
                ring.settle(sp)

            @block.tensor
            def _(pe):
                pe.wait_ge(router_loaded, 32)
                for t in range(TT):
                    for k in range(DK):
                        last = nc.tensor.matmul(ps[:, 0, E * t:E * t + E], hfT[:, k, P * t:P * t + P], w_router[:, k, :],
                                                start=(k == 0), stop=(k == DK - 1))
                last.then_inc(logits_ready, 1)
                pe.wait_ge(chosen_ready, 1)
                for t in range(TT):
                    for s in range(t + 1):
                        nc.tensor.matmul(ps[:, 1, E * t:E * t + E], K["before"] if s == t else ones, chosen[:, s, :],
                                         start=(s == 0), stop=(s == t))
                for s in range(TT):
                    last = nc.tensor.matmul(ps[:, 1, E * TT:E * TT + E], ones, chosen[:, s, :], start=(s == 0), stop=(s == TT - 1))
                last.then_inc(places_ready, 1)
                for t in range(TT):
                    last = nc.tensor.transpose(ps[0:E, 2, P * t:P * t + P], weight_te[:, t, :], ident)
                last.then_inc(turned, 1)
                pe.wait_ge(turned_read, 1)
                pe.wait_ge(places_read, 1)
                for t in range(TT):
                    for j in range(2):
                        nc.tensor.matmul(ps[:, 2 * t + j, :], weight_et[:, P * t:P * t + P], b2_sb[:, 512 * j:512 * j + 512],
                                         start=True, stop=True).then_inc(init_ready, 1)

            @block.scalar
            def _(act):
                act.wait_ge(tops_ready, 1)
                nc.scalar.activation(soft[:, :, :], soft[:, :, :], ACT.Exp).then_inc(exps_ready, 1)
                act.wait_ge(turned, 1)
                nc.scalar.activation(weight_et[:, :], ps[0:E, 2, :], ACT.Copy).then_inc(turned_read, 1)

            @block.vector
            def _(dve):
                nc.vector.memset(weight_te[:, :, :], 0.0)
                nc.vector.memset(chosen[:, :, :], 0.0)
                nc.vector.memset(slot_te[:, :, :], -1.0)
                dve.wait_ge(logits_ready, 1)
                nc.vector.tensor_tensor(logits[:, :, :], ps[:, 0, 0:E * TT].rearrange("p (t e) -> p t e", t=TT),
                                        col("b_router", 0, E).unsqueeze(1).to_broadcast([P, TT, E]), ALU.add)
                dve.drain()
                for t in range(TT):
                    nc.vector.max(top[:, t, :], logits[:, t, :])
                dve.drain()
                for t in range(TT):
                    nc.vector.max_index(top_at[:, t, :], top[:, t, :], logits[:, t, :])
                nc.vector.tensor_tensor(soft[:, :, :], top[:, :, 0:TOPK], top[:, :, 0:1].to_broadcast([P, TT, TOPK]), ALU.subtract)
                dve.drain().then_inc(tops_ready, 1)
                nc.vector.tensor_copy(top_atf[:, :, :], top_at[:, :, :])
                dve.wait_ge(exps_ready, 1)
                nc.vector.tensor_reduce(small[:, 0:TT], soft[:, :, :], AX.X, ALU.add)
                dve.drain()
                nc.vector.reciprocal(small[:, 4:4 + TT], small[:, 0:TT])
                dve.drain()
                nc.vector.tensor_tensor(soft[:, :, :], soft[:, :, :], small[:, 4:4 + TT].unsqueeze(2).to_broadcast([P, TT, TOPK]), ALU.mult)
                dve.drain()
                for j in range(TOPK):
                    nc.vector.tensor_tensor(hot[:, 0], iota_e, top_atf[:, :, j:j + 1].to_broadcast([P, TT, E]), ALU.is_equal)
                    dve.drain()
                    nc.vector.tensor_tensor(chosen[:, :, :], chosen[:, :, :], hot[:, 0], ALU.add)
                    nc.vector.tensor_tensor(hot[:, 1], hot[:, 0], soft[:, :, j:j + 1].to_broadcast([P, TT, E]), ALU.mult)
                    dve.drain()
                    nc.vector.tensor_tensor(weight_te[:, :, :], weight_te[:, :, :], hot[:, 1], ALU.add)
                    dve.drain()
                dve.drain().then_inc(chosen_ready, 1)
                dve.wait_ge(places_ready, 1)
                places = ps[:, 1, 0:E * TT].rearrange("p (t e) -> p t e", t=TT)
                nc.vector.scalar_tensor_tensor(slot_te[:, :, 0:E], places, 1.0, chosen[:, :, :], ALU.add, ALU.mult)
                nc.vector.tensor_reduce(small[:, 12:13], ps[:, 1, E * TT:E * TT + E], AX.X, ALU.max)
                dve.drain()
                nc.vector.tensor_scalar(slot_te[:, :, 0:E], slot_te[:, :, 0:E], -1.0, None, ALU.add)
                nc.vector.tensor_copy(most[:, :], small[:, 12:13])
                dve.drain().then_inc(places_read, 1)
                gated_bias = hfT[:, :, :].rearrange("p k t -> p (k t)").rearrange("p (t d) -> p t d", t=TT)
                for t in range(TT):
                    dve.wait_ge(init_ready, 2 * t + 2)
                    nc.vector.tensor_tensor(gated_bias[:, t, :], ps[:, 2 * t:2 * t + 2, :].rearrange("p b n -> p (b n)"),
                                            gate_rows[:, 1, :], ALU.mult)
                dve.drain()
                for t in range(TT):
                    nc.vector.tensor_tensor(x_tok[:, t, :], x_tok[:, t, :], gated_bias[:, t, :], ALU.add)
        router.close()

        xg_hi = sb(moe, "gathered_hi", [P, DK, P], F32R)
        xg_full, xg_lo = twin(nc, moe, "gathered_lo", [P, DK, P])
        one_of_four = sb(moe, "one_of_four", [4, 4], F32R)
        b1_hi = sb(moe, "b1_hi", [4, 512], F32R)
        b1_full, b1_lo = twin(nc, moe, "b1_lo", [4, 512])
        pick_g = sb(moe, "pick_gather", [P, TT, P])
        pick_c = sb(moe, "pick_combine", [P, TT, P])
        turner = sb(moe, "turner", [P, TT, P + 1])
        pickT = sb(moe, "pick_T", [P, T], F32R)
        w_slot = sb(moe, "weight_of_slot", [P, 1])
        w_four = sb(moe, "weight_by_tile", [P, 2, 2, 1])
        slot_col = sb(moe, "slot_col", [P, 2, TT])
        glu = sb(moe, "glu", [P, DFF])
        sig_glu = sb(moe, "sig_glu", [P, DFF])
        lin = sb(moe, "lin", [P, DFF])
        hid_hi = sb(moe, "hidden_hi", [P, DK, P], F32R)
        hid_lo = sb(moe, "hidden_lo", [P, DK, P], F32R)
        y_hi = sb(moe, "expert_out_hi", [P, D], F32R)
        y_out, y_lo = twin(nc, moe, "expert_out_lo", [P, D])
        LIMIT, ALPHA = 7.0, 1.702
        gate_f = gate_rows[:, 1, :]

        def experts_pass(rounds, prefetched):
            free0 = 0 if prefetched else 8
            HALVES = 12 * E
            slot0 = moe_at % 4 // 2 if prefetched else 0

            class Turn:
                def __init__(self, r, k, e, s):
                    self.first, self.last = s == 0, s == 12 * E - 4
                    self.more = s < 12 * (E - 1) - 4
                    self.e = e
                    self.i = e if r is None else r * E + e
                    self.q0 = k * 24 if r is None else r * HALVES + k * 24
                    self.s = s

                def half(self, o):
                    s = self.s + o
                    return self.q0 + s, (s // 2 + slot0) % 4, s % 2, s % 4

                def landed(self, o):
                    return self.q0 * 2 + 16 * ((self.s + o) // 8 + 1)

            def each_turn(eng, prologue, turn):
                def one_round(r):
                    prologue(Turn(r, 0, 0, 0))
                    turn(Turn(r, 0, 0, 0))
                    with eng.Fori(0, E // 2 - 1) as k:
                        turn(Turn(r, k, k * 2 + 1, 8))
                        turn(Turn(r, k, k * 2 + 2, 20))
                    turn(Turn(r, 0, E - 1, 12 * (E - 1) - 4))
                    turn(Turn(r, 0, E, 12 * E - 4))
                if rounds:
                    with eng.Fori(0, rounds) as r:
                        one_round(r)
                else:
                    one_round(None)

            @contextmanager
            def when_needed(eng):
                if rounds:
                    n = eng.value_load(most[0:1, 0:1], min_val=0, max_val=T)
                    with eng.If(n > P):
                        yield
                else:
                    yield

            def of_expert(table, e):
                return table[:, :, e:e + 1] if isinstance(e, int) else table[:, :, bass.ds(e, 1)]

            def full_half(h):
                return ring.buf[:, 2 * h[1] + h[2], :]

            def lo_half(h):
                return ring.part[:, 2 * h[1] + h[2], :]

            def hi_half(h):
                return ring.part[:, 8 + h[3], :]

            with stage("picked", "gathered", "xg_rounded", "xg_ready", "glu_ready", "sig_ready", "hidden_ready", "turned",
                       "hid_rounded", "hid_ready", "pick_c_ready", "pick_turned", "pick_read", "y_full", "y_rounded", "y_ready",
                       "combined", "added", "b1_loaded", "b1_rounded", "b1_ready", "w_rounded", "w_split") as (
                    block, picked, gathered, xg_rounded, xg_ready, glu_ready, sig_ready, hidden_ready, turned,
                    hid_rounded, hid_ready, pick_c_ready, pick_turned, pick_read, y_full, y_rounded, y_ready,
                    combined, added, b1_loaded, b1_rounded, b1_ready, w_rounded, w_split):
                b1 = a["b1"][0]

                @block.sync
                def _(sp):
                    def load_b1(e):
                        row = b1[e:e + 1, :] if isinstance(e, int) else b1[bass.ds(e, 1), :]
                        sp.dma_start(b1_full[:, :], row.rearrange("e (n f) -> (e n) f", n=4)).then_inc(b1_loaded, 16)

                    def load_tile(t, o, src, dims):
                        q, slot, _, _ = t.half(o)
                        if not (t.first and prefetched):
                            sp.wait_ge(ring.used, q + (free0 - 6))
                        room = ring.buf[:, 2 * slot:2 * slot + 2, :].rearrange("p s n -> p (s n)").rearrange("p (a b) -> p a b", a=dims[0])
                        sp.dma_start(room, src).then_inc(ring.loaded[slot], 16)

                    def prologue(t):
                        if rounds:
                            sp.wait_ge(ring.used, t.q0 + free0)
                        load_b1(0)
                        if prefetched:
                            for o in (0, 2):
                                sp.nop().then_inc(ring.loaded[t.half(o)[1]], 16)

                    def turn(t):
                        o = 0
                        if not t.last:
                            for src, dims in up_tiles(t.e):
                                if not (t.first and prefetched and o < 4):
                                    load_tile(t, o, src, dims)
                                o += 2
                        if not t.first:
                            o = 0 if t.last else 8
                            for n, (src, dims) in enumerate(down_tiles(t.e + (-1))):
                                load_tile(t, o + 2 * n, src, dims)
                        if t.more:
                            sp.wait_ge(ring.used, t.half(0)[0] + (1 + free0))
                            load_b1(t.e + 1)

                    with when_needed(sp):
                        each_turn(sp, prologue, turn)

                @block.tensor
                def _(pe):
                    def gather(n):
                        pe.wait_ge(picked, n)
                        for c in range(DK):
                            for t in range(TT):
                                last = nc.tensor.matmul(ps[:, 4 + c // 4, P * (c % 4):P * (c % 4) + P],
                                                        xn_tok[:, t, P * c:P * c + P], pick_g[:, t, :],
                                                        start=(t == 0), stop=(t == TT - 1))
                        last.then_inc(gathered, 1)

                    def up(t):
                        pe.wait_ge(b1_ready, t.i + 1)
                        for n in range(4):
                            if not t.first:
                                pe.wait_ge(added, t.i * 8 + (n - 3))
                            elif rounds:
                                pe.wait_ge(added, t.i * 8 + (n + 5))
                            one = one_of_four[:, n:n + 1].to_broadcast([4, P])
                            nc.tensor.matmul(ps[:, n, :], one, b1_hi[:, :], start=True, stop=False)
                            nc.tensor.matmul(ps[:, n, :], one, b1_lo[:, :], start=False, stop=False)
                        pe.wait_ge(xg_ready, t.i + 1)
                        for k in range(DK):
                            h = t.half(k)
                            w_hi, w_lo = hi_half(h), lo_half(h)
                            x_hi, x_lo = xg_hi[:, k, :], xg_lo[:, k, :]
                            pe.wait_ge(w_split, h[0] + 1)
                            for n in range(4):
                                f = slice(512 * n, 512 * n + 512)
                                last = product(nc, ps[:, n, :], (x_hi, x_lo), (w_hi[:, f], w_lo[:, f]), False, k == DK - 1)
                            last.then_inc(ring.used, 1)

                    def down(t):
                        for m in range(4):
                            h = t.half(m if t.last else 8 + m)
                            w_hi = hi_half(h).rearrange("p (k n) -> p k n", k=2)
                            w_lo = lo_half(h).rearrange("p (k n) -> p k n", k=2)
                            pe.wait_ge(w_split, h[0] + 1)
                            for k in range(2):
                                x_hi, x_lo = (x[:, 2 * m + k, :] for x in (hid_hi, hid_lo))
                                for n in range(2):
                                    f = slice(512 * n, 512 * n + 512)
                                    last = product(nc, ps[:, 6 + n, :], (x_hi, x_lo), (w_hi[:, k, f], w_lo[:, k, f]),
                                                   m == 0 and k == 0, m == 3 and k == 1)
                            last.then_inc(ring.used, 1)

                    def prologue(t):
                        gather(t.i + 1)

                    def turn(t):
                        if not t.last:
                            up(t)
                        if not t.first:
                            pe.wait_ge(pick_c_ready, t.i)
                            for j in range(TT):
                                last = nc.tensor.matmul(ps[:, 4 + j // 2, (P + 1) * (j % 2):(P + 1) * (j % 2) + P + 1],
                                                        pick_c[:, j, :], turner[:, j, :], start=True, stop=True)
                            last.then_inc(pick_turned, 1)
                            pe.wait_ge(hid_ready, t.i * 2)
                            down(t)
                        if not t.last:
                            if t.more:
                                if not t.first:
                                    pe.wait_ge(pick_read, t.i)
                                gather(t.i + 2)
                            if not t.first:
                                pe.wait_ge(y_full, t.i)
                            for s in range(2):
                                pe.wait_ge(hidden_ready, t.i * 2 + (s + 1))
                                for c in range(4):
                                    last = nc.tensor.transpose(ps[:, 6 + s, P * c:P * c + P], lin[:, 512 * s + P * c:512 * s + P * c + P], ident)
                                last.then_inc(turned, 1)
                        if not t.first:
                            pe.wait_ge(y_ready, t.i)
                            for o in range(8):
                                if t.last and o < 4 or o >= 4:
                                    pe.wait_ge(added, t.i * 8 + (o - 3))
                                f = slice(512 * (o % 2), 512 * (o % 2) + 512)
                                pick = pickT[:, P * (o // 2):P * (o // 2) + P]
                                nc.tensor.matmul(ps[:, o % 4, :], pick, y_hi[:, f], start=True, stop=False)
                                nc.tensor.matmul(ps[:, o % 4, :], pick, y_lo[:, f], start=False, stop=True)\
                                    .then_inc(combined, 1)

                    with when_needed(pe):
                        nc.tensor.nop().then_inc(pick_turned, 1)
                        if not prefetched:
                            nc.tensor.nop().then_inc(ring.used, 8)
                        each_turn(pe, prologue, turn)

                @block.gpsimd
                def _(pool):
                    def one_hot(dst, e, n):
                        slot = of_expert(slot_te, e).rearrange("p t e -> p (t e)")
                        nc.gpsimd.tensor_tensor(slot_col[:, n, :], slot, ones[:, 0:TT], ALU.mult)
                        pool.drain()
                        for t in range(TT):
                            nc.gpsimd.tensor_scalar(dst[:, t, :], K["slot_iota"], slot_col[:, n, t:t + 1], None, ALU.is_equal)

                    def prologue(t):
                        if rounds:
                            pool.drain()
                            nc.gpsimd.tensor_scalar(slot_te[:, :, :], slot_te[:, :, :], -float(P), None, ALU.add)
                            pool.drain()
                        one_hot(pick_g, 0, 0)
                        pool.drain().then_inc(picked, 1)

                    def turn(t):
                        if not t.first:
                            pool.wait_ge(pick_turned, t.i)
                            w = of_expert(weight_te, t.e + (-1))
                            nc.gpsimd.tensor_tensor(turner[:, :, P:P + 1], w, ones[:, 0:TT].unsqueeze(2), ALU.mult)
                            one_hot(pick_c, t.e + (-1), 1)
                            pool.drain().then_inc(pick_c_ready, 1)
                        if t.more:
                            pool.wait_ge(gathered, t.i + 1)
                            one_hot(pick_g, t.e + 1, 0)
                            pool.drain().then_inc(picked, 1)

                    with when_needed(pool):
                        for t in range(TT):
                            nc.gpsimd.tensor_copy(turner[:, t, 0:P], ident)
                        each_turn(pool, prologue, turn)

                @block.scalar
                def _(act):
                    def round_half(t, o, waits=True):
                        h = t.half(o)
                        act.wait_ge(ring.loaded[h[1]], t.landed(o))
                        if waits:
                            act.wait_ge(ring.used, h[0] + (free0 - 3))
                        nc.scalar.activation(hi_half(h), full_half(h), ACT.Copy).then_inc(w_rounded, 1)

                    def round_b1(n):
                        act.wait_ge(b1_loaded, n * 16 + 16)
                        nc.scalar.activation(b1_hi[:, :], b1_full[:, :], ACT.Copy).then_inc(b1_rounded, 1)

                    def modulate(n):
                        act.wait_ge(gathered, n)
                        for c in range(DK):
                            nc.scalar.activation(xg_full[:, c, :], ps[:, 4 + c // 4, P * (c % 4):P * (c % 4) + P], ACT.Identity,
                                                 scale=mod_cols[:, 32 + c:33 + c], bias=mod_cols[:, 24 + c:25 + c])
                        act.drain()
                        nc.scalar.activation(xg_hi[:, :, :], xg_full[:, :, :], ACT.Copy).then_inc(xg_rounded, 1)

                    def prologue(t):
                        round_b1(t.i)
                        for o in range(4):
                            round_half(t, o, waits=bool(rounds))
                        modulate(t.i + 1)

                    def turn(t):
                        ahead = 4
                        def round_some(n):
                            nonlocal ahead
                            for _ in range(n):
                                round_half(t, ahead)
                                ahead += 1
                        if not t.first:
                            for s in range(2):
                                act.wait_ge(turned, t.i * 2 + (s - 1))
                                nc.scalar.activation(hid_hi[:, 4 * s:4 * s + 4, :],
                                                     ps[:, 6 + s, :].rearrange("p (c n) -> p c n", c=4), ACT.Copy).then_inc(hid_rounded, 1)
                        if not t.last:
                            round_some(8)
                            for s in range(2):
                                act.wait_ge(glu_ready, t.i * 2 + (s + 1))
                                nc.scalar.activation(sig_glu[:, 512 * s:512 * s + 512], glu[:, 512 * s:512 * s + 512], ACT.Sigmoid,
                                                     scale=ALPHA).then_inc(sig_ready, 1)
                        if not t.first:
                            act.wait_ge(pick_turned, t.i + 1)
                            for b in range(2):
                                src = ps[:, 4 + b, 0:2 * (P + 1)].rearrange("p (j n) -> p j n", j=2)
                                nc.scalar.activation(pickT[:, 2 * P * b:2 * P * b + 2 * P].rearrange("p (j n) -> p j n", j=2),
                                                     src[:, :, 0:P], ACT.Copy)
                                nc.scalar.activation(w_four[:, b], src[:, :, P:P + 1], ACT.Copy)
                            act.drain().then_inc(pick_read, 1)
                        if not t.last:
                            round_some(0 if t.first else 2)
                            if t.more:
                                round_b1(t.i + 1)
                        if not t.first:
                            act.wait_ge(y_full, t.i)
                            nc.scalar.activation(y_hi[:, :], y_out[:, :], ACT.Copy).then_inc(y_rounded, 1)
                        if not t.last:
                            round_some(0 if t.first else 1)
                            if t.more:
                                modulate(t.i + 2)
                            round_some(0 if t.first else 1)

                    with when_needed(act):
                        nc.scalar.activation(one_of_four[:, :], ident[0:4, 0:4], ACT.Copy)
                        act.drain()
                        each_turn(act, prologue, turn)

                @block.vector
                def _(dve):
                    def split_half(t, o):
                        h = t.half(o)
                        dve.wait_ge(w_rounded, h[0] + 1)
                        nc.vector.tensor_tensor(lo_half(h), full_half(h), hi_half(h), ALU.subtract).then_inc(w_split, 1)

                    def split_b1(n):
                        dve.wait_ge(b1_rounded, n + 1)
                        nc.vector.tensor_tensor(b1_lo[:, :], b1_full[:, :], b1_hi[:, :], ALU.subtract).then_inc(b1_ready, 1)

                    def split_inputs(n):
                        dve.wait_ge(xg_rounded, n)
                        nc.vector.tensor_tensor(xg_lo[:, :, :], xg_full[:, :, :], xg_hi[:, :, :], ALU.subtract)\
                            .then_inc(xg_ready, 1)

                    def prologue(t):
                        split_b1(t.i)
                        for o in range(4):
                            split_half(t, o)
                        split_inputs(t.i + 1)

                    def turn(t):
                        ahead = 4
                        def split_some(n):
                            nonlocal ahead
                            for _ in range(n):
                                split_half(t, ahead)
                                ahead += 1
                        if not t.first:
                            for s in range(2):
                                dve.wait_ge(hid_rounded, t.i * 2 + (s - 1))
                                nc.vector.tensor_tensor(hid_lo[:, 4 * s:4 * s + 4, :],
                                                        ps[:, 6 + s, :].rearrange("p (c n) -> p c n", c=4),
                                                        hid_hi[:, 4 * s:4 * s + 4, :], ALU.subtract).then_inc(hid_ready, 1)
                        if not t.last:
                            split_some(7)
                            dve.wait_ge(ring.used, t.half(7)[0] + (1 + free0))
                            for s in range(2):
                                pairs = ps[:, 2 * s:2 * s + 2, :].rearrange("p b (n two) -> p b n two", two=2)
                                half = slice(512 * s, 512 * s + 512)
                                nc.vector.tensor_scalar(glu[:, half].rearrange("p (b n) -> p b n", b=2), pairs[:, :, :, 0], LIMIT, None,
                                                        ALU.min).then_inc(glu_ready, 1)
                                nc.vector.tensor_scalar(lin[:, half].rearrange("p (b n) -> p b n", b=2), pairs[:, :, :, 1], -LIMIT, LIMIT,
                                                        ALU.max, ALU.min)
                            split_some(1)
                            dve.drain()
                            for s in range(2):
                                half = slice(512 * s, 512 * s + 512)
                                nc.vector.scalar_tensor_tensor(lin[:, half], lin[:, half], 1.0, glu[:, half], ALU.add, ALU.mult)
                            dve.drain()
                            for s in range(2):
                                half = slice(512 * s, 512 * s + 512)
                                dve.wait_ge(sig_ready, t.i * 2 + (s + 1))
                                nc.vector.tensor_tensor(lin[:, half], lin[:, half], sig_glu[:, half], ALU.mult).then_inc(hidden_ready, 1)
                            split_some(0 if t.first else 2)
                            if t.more:
                                split_b1(t.i + 1)
                        if not t.first:
                            dve.wait_ge(pick_read, t.i)
                            nc.vector.tensor_reduce(w_slot[:, :], w_four[:, :, :, :].rearrange("p a b n -> p (a b n)"), AX.X, ALU.add)
                            dve.drain()
                            dve.wait_ge(ring.used, t.half(3 if t.last else 11)[0] + (1 + free0))
                            nc.vector.scalar_tensor_tensor(y_out[:, :], ps[:, 6:8, :].rearrange("p b n -> p (b n)"), w_slot[:, :], gate_f,
                                                           ALU.mult, ALU.mult)
                            dve.drain().then_inc(y_full, 1)
                            dve.wait_ge(y_rounded, t.i)
                            nc.vector.tensor_tensor(y_lo[:, :], y_out[:, :], y_hi[:, :], ALU.subtract).then_inc(y_ready, 1)
                        if not t.first:
                            for o in range(8):
                                dst = x_tok[:, o // 2, 512 * (o % 2):512 * (o % 2) + 512]
                                dve.wait_ge(combined, t.i * 8 + (o - 7))
                                nc.vector.tensor_tensor(dst, dst, ps[:, o % 4, :], ALU.add).then_inc(added, 1)
                        if t.more:
                            split_inputs(t.i + 2)
                        if not t.last:
                            split_some(0 if t.first else 2)

                    with when_needed(dve):
                        nc.vector.engine_nop().then_inc(added, 8)
                        each_turn(dve, prologue, turn)

        def reset_ring():
            nums = [s.num for s in ring.loaded + [ring.used, ring.rounded, ring.split]]
            nc.all_engine_barrier(sems_to_clear=range(min(nums), max(nums) + 1))

        reset_ring()
        experts_pass(0, True)
        reset_ring()
        experts_pass(T // P - 1, False)
        reset_ring()
        ring.restart(block2_at)
        ring.limit = None
        moe.close()
        with stage("loads_issued") as (block, _):
            @block.sync
            def _(sp):
                ring.load(sp, ring.slots)

            @block.scalar
            def _(act):
                ring.ahead("act", act, ring.taken)

            @block.vector
            def _(dve):
                ring.ahead("dve", dve, ring.taken)
        first_block.close()

        arena, arena_part = (x[:, 8:12, :].rearrange("p s n -> p (s n)") for x in (ring.buf, ring.part))
        h1T_full, h1T_lo = in_ring(ring.buf), in_ring(ring.part)
        h1T_hi = sb(ctx, "h1T_hi", [P, DK, T], F32R)
        h1T = (h1T_hi, h1T_lo)
        norm_stage(h1T_full, lambda k: col("norm1", k), None, *h1T)

        dn_out, dn_out_part = twin(nc, ctx, "dn_out", [P, TT, BW])
        dn = ctx.enter_context(ExitStack())
        k_tok = sb(dn, "k_tok", [P, TT, BW])
        v_tok = sb(dn, "v_tok", [P, TT, BW])
        qT, kT = chan(xn_flat, 0), chan(xn_flat, 2048)
        raw = sb(dn, "conv_raw", [P, BC, T + 2])
        vT = dn_out[:, :, :]
        scratch_a = arena[:, 0:2048].rearrange("p (a b) -> p a b", a=4)

        def conv_silu(dst, j):
            project(h1T, [[("chan", ACT.Copy, raw[:, m, 1:1 + T]) for m in range(BC)]], scratch_a)
            with stage("convolved") as (block, convolved):
                @block.vector
                def _(dve):
                    nc.vector.memset(raw[:, :, 0:1], 0.0)
                    nc.vector.memset(raw[:, :, T + 1:T + 2], 0.0)
                    dve.drain()
                    for c in range(BC):
                        taps = [col("dn_conv", 3 * (4 * j + c) + k) for k in range(3)]
                        nc.vector.tensor_scalar(dst[:, c, :], raw[:, c, 0:T], taps[0], None, ALU.mult)
                        for k in range(1, 3):
                            dve.drain()
                            last = nc.vector.scalar_tensor_tensor(dst[:, c, :], raw[:, c, k:k + T], taps[k], dst[:, c, :],
                                                                  ALU.mult, ALU.add)
                        last.then_inc(convolved, 1)

                @block.scalar
                def _(act):
                    for c in range(BC):
                        act.wait_ge(convolved, c + 1)
                        nc.scalar.activation(dst[:, c, :], dst[:, c, :], ACT.Silu)

        for dst, j in ((qT, 0), (kT, 1), (vT, 2)):
            conv_silu(dst, j)

        g_tok = sb(dn, "g_tok", [P, TT, 16])
        beta = sb(dn, "beta", [P, TT, 16])
        g_cum = sb(dn, "g_cum", [P, TT, 16])
        e_g = sb(dn, "e_g", [P, TT, 16])
        e_rest = sb(dn, "e_rest", [P, TT, 16])
        w_ab = arena[:, 4096:4096 + DK * 32].rearrange("p (k n) -> p k n", k=DK)
        tmp_ab = arena[:, 4608:4608 + 64].rearrange("p (t n) -> p t n", t=TT)
        exp_alog = arena[:, 4672:4688]
        gt = arena[:, 4704:4704 + 64].rearrange("p (t n) -> p t n", t=TT)
        with stage("ab_loaded", "squared", "summed", "rooted", "normed", "turned", "turned_read", "ab_ready", "ab_biased",
                   "ab_exp", "g_ready", "cum_ready", "cum_read") as (
                block, ab_loaded, squared, summed, rooted, normed, turned, turned_read, ab_ready, ab_biased, ab_exp,
                g_ready, cum_ready, cum_read):
            @block.sync
            def _(sp):
                sp.dma_start(w_ab, w_in2[:, 2048:2080].rearrange("(k p) n -> p k n", p=P)).then_inc(ab_loaded, 16)

            @block.tensor
            def _(pe):
                pe.wait_ge(ab_loaded, 16)
                for t in range(TT):
                    for k in range(DK):
                        for n, part in enumerate((h1T_hi[:, k, P * t:P * t + P].bitcast(F32), h1T_lo[:, k, P * t:P * t + P].bitcast(F32))):
                            last = nc.tensor.matmul(ps[:, 7, 32 * t:32 * t + 32], part, w_ab[:, k, :],
                                                    start=(k == 0 and n == 0), stop=(k == DK - 1 and n == 1))
                last.then_inc(ab_ready, 1)
                for m in range(8):
                    pe.wait_ge(squared, m + 1)
                    if m >= 2:
                        pe.wait_ge(rooted, m - 1)
                    nc.tensor.matmul(ps[:, m % 2, :], head_sum, scratch_a[:, m % 2, :], start=True, stop=True).then_inc(summed, 1)
                for n in range(8):
                    src, t = (kT, n) if n < 4 else (vT, n - 4)
                    if n == 0:
                        pe.wait_ge(normed, 8)
                    if n >= 3:
                        pe.wait_ge(turned_read, n - 2)
                    for c in range(BC):
                        last = nc.tensor.transpose(ps[:, 2 + n % 3, P * c:P * c + P], src[:, c, P * t:P * t + P], ident)
                    last.then_inc(turned, 1)
                pe.wait_ge(g_ready, 1)
                for d, cum in ((0, "cum_f"), (1, "cum_b")):
                    for t in range(TT):
                        nc.tensor.matmul(ps[:, 5, 16 * t + 8 * d:16 * t + 8 * d + 8], K[cum], g_tok[:, t, 8 * d:8 * d + 8],
                                         start=True, stop=True)
                nc.tensor.matmul(ps[:, 6, 0:64], head_sum, g_tok[:, :, :].rearrange("p t n -> p (t n)"),
                                 start=True, stop=True).then_inc(cum_ready, 1)

            @block.scalar
            def _(act):
                def root(m):
                    act.wait_ge(summed, m + 1)
                    if m >= 2:
                        act.wait_ge(normed, m - 1)
                    nc.scalar.activation(scratch_a[:, 2 + m % 2, :], ps[:, m % 2, :], ACT.Sqrt, bias=col("eps")).then_inc(rooted, 1)

                for m in range(8):
                    src = (qT if m < 4 else kT)[:, m % 4, :]
                    if m >= 2:
                        act.wait_ge(summed, m - 1)
                    nc.scalar.activation(scratch_a[:, m % 2, :], src, ACT.Square).then_inc(squared, 1)
                    if m >= 1:
                        root(m - 1)
                root(7)
                for n in range(8):
                    act.wait_ge(turned, n + 1)
                    dst = k_tok[:, n, :] if n < 4 else v_tok[:, n - 4, :]
                    nc.scalar.activation(dst, ps[:, 2 + n % 3, :], ACT.Copy).then_inc(turned_read, 1)
                act.wait_ge(ab_ready, 1)
                ab = ps[:, 7, 0:P].rearrange("p (t n) -> p t n", t=TT)
                nc.scalar.activation(exp_alog, col("dn_a_log", 0, 16), ACT.Exp)
                act.wait_ge(ab_biased, 1)
                nc.scalar.activation(beta[:, :, :], ab[:, :, 16:32], ACT.Sigmoid)
                nc.scalar.activation(gt, gt, ACT.Exp, scale=-1.0)
                act.drain()
                nc.scalar.activation(gt, gt, ACT.Ln, bias=col("one"))
                act.drain().then_inc(ab_exp, 1)
                act.wait_ge(cum_ready, 1)
                act.wait_ge(cum_read, 1)
                nc.scalar.activation(e_g[:, :, :], g_cum[:, :, :], ACT.Exp)
                nc.scalar.activation(e_rest[:, :, :], tmp_ab, ACT.Exp)

            @block.vector
            def _(dve):
                for m in range(8):
                    buf = (qT if m < 4 else kT)[:, m % 4, :]
                    rinv = scratch_a[:, 2 + m % 2, :]
                    dve.wait_ge(rooted, m + 1)
                    nc.vector.reciprocal(rinv, rinv)
                    dve.drain()
                    nc.vector.scalar_tensor_tensor(buf, buf, HD ** -0.5 if m < 4 else 1.0, rinv, ALU.mult, ALU.mult)\
                        .then_inc(normed, 1)
                dve.wait_ge(ab_ready, 1)
                ab = ps[:, 7, 0:P].rearrange("p (t n) -> p t n", t=TT)
                nc.vector.tensor_tensor(tmp_ab, ab[:, :, 0:16], col("dn_dt_bias", 0, 16).unsqueeze(1).to_broadcast([P, TT, 16]), ALU.add)
                dve.drain()
                nc.vector.scalar_tensor_tensor(gt, tmp_ab, -1.0, tmp_ab, ALU.mult, ALU.max)
                dve.drain().then_inc(ab_biased, 1)
                nc.vector.tensor_scalar(tmp_ab, tmp_ab, 0.0, None, ALU.max)
                dve.wait_ge(ab_exp, 1)
                dve.drain()
                nc.vector.tensor_tensor(tmp_ab, tmp_ab, gt, ALU.add)
                dve.drain()
                nc.vector.scalar_tensor_tensor(g_tok[:, :, :], tmp_ab, -1.0, exp_alog.unsqueeze(1).to_broadcast([P, TT, 16]),
                                               ALU.mult, ALU.mult)
                dve.drain().then_inc(g_ready, 1)
                dve.wait_ge(cum_ready, 1)
                nc.vector.tensor_copy(g_cum[:, :, :], ps[:, 5, 0:64].rearrange("p (t n) -> p t n", t=TT))
                dve.drain()
                nc.vector.tensor_tensor(tmp_ab, ps[:, 6, 0:64].rearrange("p (t n) -> p t n", t=TT), g_cum[:, :, :], ALU.subtract)
                dve.drain().then_inc(cum_read, 1)

        dirs = []
        for d in range(2):
            base = 3072 * d
            dirs.append(dict(
                u=arena[:, base:base + 512].rearrange("p (q c v) -> p q c v", q=2, c=BC),
                wT=arena[:, base + 512:base + 1024].rearrange("p (c i) -> p c i", c=BC),
                qkT=arena[:, base + 1024:base + 2048].rearrange("p (q c i) -> p q c i", q=2, c=BC),
                q_decT=arena[:, base + 2048:base + 2560].rearrange("p (c i) -> p c i", c=BC),
                k_dec=arena[:, base + 2560:base + 3072].rearrange("p (q c k) -> p q c k", q=2, c=BC)))
        state = arena[:, 6144:6656].rearrange("p (d c v) -> p d c v", d=2, c=BC)
        e_total = arena[:, 6656:6656 + 16].rearrange("p (d c n) -> p d c n", d=2, c=BC)
        v_new = arena[:, 6720:6720 + 1024].rearrange("p (d q c v) -> p d q c v", d=2, q=2, c=BC)
        joins = sb(dn, "joins", [P, 2, 6, P])
        lev = sb(dn, "levels", [P, 2, 4, 512])
        step_product = arena[:, 6720:6720 + 1024].rearrange("p (q n) -> p q n", q=2)
        raw_flat = raw[:, :, :].rearrange("p c t -> p (c t)")
        e_rows = raw_flat[:, 0:512].rearrange("p (c i) -> p c i", c=BC)
        kbg = raw_flat[:, 512:1024].rearrange("p (q c k) -> p q c k", q=2, c=BC)
        vb = raw_flat[:, 1024:1536].rearrange("p (q c k) -> p q c k", q=2, c=BC)
        kscale = sb(dn, "kscale", [P, 8])

        with stage("joins_loaded") as (block, joins_loaded):
            @block.sync
            def _(sp):
                sp.dma_start(joins[:, :, :, :], a["joins"].rearrange("p (w l n) -> p w l n", w=2, l=6)).then_inc(joins_loaded, 16)
                sp.wait_ge(joins_loaded, 16)

            @block.vector
            def _(dve):
                nc.vector.memset(state, 0.0)
                nc.vector.memset(v_new, 0.0)

        def heads_view(flat, p):
            return flat.rearrange("p (c q k) -> p c q k", c=BC, q=2)[:, :, p, :]

        def prepare(d, t):
            D_ = dirs[d]
            mask = K["le_mask"] if d == 0 else K["ge_mask"]
            cum = K["cum_f"] if d == 0 else K["cum_b"]
            join = joins[:, 1 - d]
            col8 = slice(8 * d, 8 * d + 8)
            ends = (63, 127) if d == 0 else (0, 64)
            flat4 = lambda x: x.rearrange("p c i -> p (c i)")
            with stage("rows_ready", "rows_exp", "decay_in", "decay_ready", "at_ready", "joined", "inverse_ready",
                       "first_turned", "prod_ready", "prod_copied", "diff_ready", "scaled", "uw_ready", "kk_read") as (
                    block, rows_ready, rows_exp, decay_in, decay_ready, at_ready, joined, inverse_ready, first_turned,
                    prod_ready, prod_copied, diff_ready, scaled, uw_ready, kk_read):
                @block.tensor
                def _(pe):
                    for p in range(2):
                        b = 4 * p
                        r = slice(HD * p, HD * p + HD)
                        for c in range(BC):
                            h = 8 * d + 2 * c + p
                            i_ = slice(P * c, P * c + P)
                            nc.tensor.matmul(ps[:, b, i_], g_tok[:, t, h:h + 1].to_broadcast([P, P]), cum, start=True, stop=True)
                            nc.tensor.matmul(ps[:, b + 1, i_], beta[:, t, h:h + 1].to_broadcast([P, P]), ident, start=True, stop=True)
                        for c in range(BC):
                            i_ = slice(P * c, P * c + P)
                            tok = slice(P * t, P * t + P)
                            nc.tensor.matmul(ps[:, b + 2, i_], kT[r, c, tok], kT[r, c, tok], start=True, stop=True)
                            last = nc.tensor.matmul(ps[:, b + 3, i_], kT[r, c, tok], qT[r, c, tok], start=True, stop=True)
                        last.then_inc(rows_ready, 1)
                    for p in range(2):
                        pe.wait_ge(inverse_ready, p + 1)
                        for c in range(BC):
                            i_ = slice(P * c, P * c + P)
                            last = nc.tensor.transpose(ps[:, 4 * p, i_], lev[:, p, 3, i_], ident)
                        last.then_inc(first_turned, 1)
                    for l in range(1, 6):
                        for p in range(2):
                            pe.wait_ge(joined, 2 * (l - 1) + p + 1)
                            pe.wait_ge(inverse_ready, 2 * l + p + 1)
                            for c in range(BC):
                                i_ = slice(P * c, P * c + P)
                                last = nc.tensor.matmul(ps[:, 4 * p + 1, i_], lev[:, p, 1, i_], lev[:, p, 2, i_], start=True, stop=True)
                            last.then_inc(prod_ready, 1)
                        for p in range(2):
                            pe.wait_ge(prod_copied, 2 * (l - 1) + p + 1)
                            for c in range(BC):
                                i_ = slice(P * c, P * c + P)
                                last = nc.tensor.matmul(ps[:, 4 * p + 2, i_], step_product[:, p, i_], lev[:, p, 3, i_], start=True, stop=True)
                                if l < 5:
                                    last = nc.tensor.matmul(ps[:, 4 * p + 3, i_], lev[:, p, 3, i_], step_product[:, p, i_], start=True, stop=True)
                            last.then_inc(diff_ready, 1)
                    pe.wait_ge(scaled, 1)
                    for p in range(2):
                        r = slice(HD * p, HD * p + HD)
                        pe.wait_ge(inverse_ready, 12 + p + 1)
                        for c in range(BC):
                            i_ = slice(P * c, P * c + P)
                            nc.tensor.matmul(ps[:, 4 * p, HD * c:HD * c + HD], lev[:, p, 3, i_], vb[:, p, c, :], start=True, stop=True)
                            last = nc.tensor.matmul(ps[r, 4 * p + 1, i_], kbg[:, p, c, :], lev[:, p, 3, i_], start=True, stop=True)
                        last.then_inc(uw_ready, 1)

                @block.scalar
                def _(act):
                    for p in range(2):
                        r = slice(HD * p, HD * p + HD)
                        act.wait_ge(rows_ready, p + 1)
                        rows = ps[r, 4 * p, :].rearrange("p (c i) -> p c i", c=BC)
                        nc.scalar.activation(e_rows[r], rows, ACT.Exp)
                        for n in range(2):
                            last = nc.scalar.activation(e_total[r, d, :, n:n + 1], rows[:, :, ends[n]:ends[n] + 1], ACT.Exp)
                        act.drain().then_inc(rows_exp, 1)
                        act.wait_ge(decay_in, p + 1)
                        nc.scalar.activation(D_["qkT"][:, p], D_["qkT"][:, p], ACT.Exp).then_inc(decay_ready, 1)
                    for l in range(1, 6):
                        for p in range(2):
                            act.wait_ge(prod_ready, 2 * (l - 1) + p + 1)
                            nc.scalar.activation(step_product[:, p, :], ps[:, 4 * p + 1, :], ACT.Copy).then_inc(prod_copied, 1)
                    for p in range(2):
                        r = slice(HD * p, HD * p + HD)
                        act.wait_ge(uw_ready, p + 1)
                        nc.scalar.activation(D_["u"][:, p], ps[:, 4 * p, 0:256].rearrange("p (c v) -> p c v", c=BC), ACT.Copy)
                        nc.scalar.activation(D_["wT"][r], ps[r, 4 * p + 1, :].rearrange("p (c i) -> p c i", c=BC), ACT.Copy)

                @block.gpsimd
                def _(pool):
                    for l in range(1, 6):
                        for p in range(2):
                            if l == 1:
                                pool.wait_ge(at_ready, p + 1)
                            else:
                                pool.wait_ge(prod_copied, 2 * (l - 2) + p + 1)
                            nc.gpsimd.tensor_tensor(lev[:, p, 1, :].rearrange("p (c i) -> p c i", c=BC),
                                                    lev[:, p, 0, :].rearrange("p (c i) -> p c i", c=BC),
                                                    join[:, l, :].unsqueeze(1).to_broadcast([P, BC, P]), ALU.mult).then_inc(joined, 1)

                @block.vector
                def _(dve):
                    v4 = lambda x: x.rearrange("p (c i) -> p c i", c=BC)
                    for p in range(2):
                        gcol = g_cum[:, t, col8].rearrange("p (c q) -> p c q", q=2)[:, :, p:p + 1]
                        dve.wait_ge(rows_exp, p + 1)
                        x = D_["qkT"][:, p]
                        nc.vector.tensor_tensor(x, v4(ps[:, 4 * p, :]), gcol.to_broadcast([P, BC, P]), ALU.subtract)
                        dve.drain()
                        nc.vector.tensor_tensor(x, x, mask.unsqueeze(1).to_broadcast([P, BC, P]), ALU.add).then_inc(decay_in, 1)
                    for p in range(2):
                        x, at = D_["qkT"][:, p], v4(lev[:, p, 0, :])
                        dve.wait_ge(decay_ready, p + 1)
                        nc.vector.tensor_tensor(at, x, v4(ps[:, 4 * p + 1, :]), ALU.mult)
                        dve.drain()
                        nc.vector.tensor_tensor(at, at, v4(ps[:, 4 * p + 2, :]), ALU.mult)
                        nc.vector.tensor_tensor(x, x, v4(ps[:, 4 * p + 3, :]), ALU.mult)
                        dve.drain().then_inc(at_ready, 1)
                        tt = v4(lev[:, p, 3, :])
                        nc.vector.tensor_tensor(tt, at, join[:, 0, :].unsqueeze(1).to_broadcast([P, BC, P]), ALU.mult)
                        dve.drain()
                        nc.vector.tensor_tensor(tt, ident.unsqueeze(1).to_broadcast([P, BC, P]), tt, ALU.subtract)
                        dve.drain().then_inc(inverse_ready, 1)
                    for p in range(2):
                        dve.wait_ge(first_turned, p + 1)
                        nc.vector.tensor_copy(lev[:, p, 2, :], ps[:, 4 * p, :])
                        dve.drain().then_inc(inverse_ready, 1)
                    nc.vector.tensor_tensor(kscale[:, :], beta[:, t, col8], e_g[:, t, col8], ALU.mult)
                    dve.drain()
                    for p in range(2):
                        r = slice(HD * p, HD * p + HD)
                        pick = lambda x: x.rearrange("p (c q) -> p c q", q=2)[:, :, p:p + 1].to_broadcast([P, BC, HD])
                        kk, vv = heads_view(k_tok[:, t, :], p), heads_view(v_tok[:, t, :], p)
                        nc.vector.tensor_tensor(vb[:, p], vv, pick(beta[:, t, col8]), ALU.mult)
                        nc.vector.tensor_tensor(kbg[:, p], kk, pick(kscale[:, :]), ALU.mult)
                        nc.vector.tensor_tensor(D_["k_dec"][:, p], kk, pick(e_rest[:, t, col8]), ALU.mult)
                        dve.wait_ge(rows_exp, p + 1)
                        nc.vector.tensor_tensor(D_["q_decT"][r], qT[r, :, P * t:P * t + P], e_rows[r], ALU.mult)
                    dve.drain().then_inc(scaled, 1)
                    for l in range(1, 6):
                        for p in range(2):
                            dve.wait_ge(diff_ready, 2 * (l - 1) + p + 1)
                            if l < 5:
                                nc.vector.tensor_tensor(lev[:, p, 2, :], lev[:, p, 2, :], ps[:, 4 * p + 3, :], ALU.subtract)
                            nc.vector.tensor_tensor(lev[:, p, 3, :], lev[:, p, 3, :], ps[:, 4 * p + 2, :], ALU.subtract)
                            dve.drain().then_inc(inverse_ready, 1)

        def recur(step):
            turns = [(0, step, 0), (1, TT - 1 - step, 1), (0, step, 1), (1, TT - 1 - step, 0)]
            with stage("ws_ready", "v_ready", "o_ready", "s_ready", "s_scaled", "o_read") as (
                    block, ws_ready, v_ready, o_ready, s_ready, s_scaled, o_read):
                @block.tensor
                def _(pe):
                    for n, (d, t, ch) in enumerate(turns):
                        D_ = dirs[d]
                        tok = slice(HD * ch, HD * ch + HD)
                        b = 4 * d
                        if n >= 2:
                            pe.wait_ge(s_ready, n - 1)
                            pe.wait_ge(o_read, n - 1)
                        for p in range(2):
                            r = slice(HD * p, HD * p + HD)
                            for c in range(BC):
                                last = nc.tensor.matmul(ps[tok, b + p, HD * c:HD * c + HD], D_["wT"][r, c, tok], state[r, d, c, :],
                                                        start=True, stop=True)
                        last.then_inc(ws_ready, 1)
                        pe.wait_ge(v_ready, n + 1)
                        for p in range(2):
                            r = slice(HD * p, HD * p + HD)
                            for c in range(BC):
                                o = ps[tok, b + 2 + p, HD * c:HD * c + HD]
                                nc.tensor.matmul(o, D_["q_decT"][r, c, tok], state[r, d, c, :], start=True, stop=False)
                                last = nc.tensor.matmul(o, D_["qkT"][:, p, c, tok], v_new[:, d, p, c, :], start=False, stop=True)
                        last.then_inc(o_ready, 1)
                        for p in range(2):
                            r = slice(HD * p, HD * p + HD)
                            for c in range(BC):
                                last = nc.tensor.matmul(ps[r, b, 256 + HD * c:256 + HD * c + HD], D_["k_dec"][tok, p, c, :],
                                                        v_new[tok, d, p, c, :], start=True, stop=True)
                        last.then_inc(s_scaled, 1)

                @block.vector
                def _(dve):
                    for n, (d, t, ch) in enumerate(turns):
                        D_ = dirs[d]
                        tok = slice(HD * ch, HD * ch + HD)
                        b = 4 * d
                        cv = lambda x: x.rearrange("p (c v) -> p c v", c=BC)
                        dve.wait_ge(ws_ready, n + 1)
                        for p in range(2):
                            nc.vector.tensor_tensor(v_new[tok, d, p], D_["u"][tok, p], cv(ps[tok, b + p, 0:256]), ALU.subtract)
                        dve.drain().then_inc(v_ready, 1)
                        dve.wait_ge(o_ready, n + 1)
                        for p in range(2):
                            dst = heads_view(dn_out[tok, t, :], p)
                            src = cv(ps[tok, b + 2 + p, 0:256])
                            if step < 2:
                                nc.vector.tensor_copy(dst, src)
                            else:
                                nc.vector.tensor_tensor(dst, dst, src, ALU.add)
                        dve.drain().then_inc(o_read, 1)
                        nc.vector.tensor_tensor(state[:, d], state[:, d], e_total[:, d, :, ch:ch + 1].to_broadcast([P, BC, HD]), ALU.mult)
                        dve.drain()
                        dve.wait_ge(s_scaled, n + 1)
                        nc.vector.tensor_tensor(state[:, d], state[:, d], cv(ps[:, b, 256:512]), ALU.add)
                        dve.drain().then_inc(s_ready, 1)

        for step in range(TT):
            prepare(0, step)
            prepare(1, TT - 1 - step)
            recur(step)
        z = k_tok
        project(h1T, [[("token", (lambda h, k, t=t: h[:, k, P * t:P * t + P]), ACT.Silu, z[:, t, :]) for t in range(TT)]],
                scratch_a)
        flat = dn_out[:, :, :].rearrange("p t n -> p (t n)")
        by_head = flat.rearrange("p (h v) -> p h v", v=HD)
        squares = v_tok[:, :, :].rearrange("p t n -> p (t n)")
        with stage("sums_ready", "rooted", "rows_ready", "turned") as (block, sums_ready, rooted, rows_ready, turned):
            @block.vector
            def _(dve):
                nc.vector.tensor_tensor(squares, flat, flat, ALU.mult)
                dve.drain()
                nc.vector.tensor_reduce(small[:, 0:32], squares.rearrange("p (h v) -> p h v", v=HD), AX.X, ALU.add)\
                    .then_inc(sums_ready, 1)
                dve.wait_ge(rooted, 1)
                nc.vector.reciprocal(small[:, 32:64], small[:, 32:64])
                dve.drain()
                nc.vector.tensor_tensor(by_head, by_head, small[:, 32:64].unsqueeze(2).to_broadcast([P, 32, HD]), ALU.mult)
                dve.drain()
                nc.vector.tensor_tensor(by_head, by_head, col("dn_out_norm", 0, HD).unsqueeze(1).to_broadcast([P, 32, HD]), ALU.mult)
                dve.drain()
                nc.vector.tensor_tensor(flat, flat, z[:, :, :].rearrange("p t n -> p (t n)"), ALU.mult).then_inc(rows_ready, 1)

            @block.tensor
            def _(pe):
                pe.wait_ge(rows_ready, 1)
                for c in range(BC):
                    for t in range(TT):
                        last = nc.tensor.transpose(ps[:, c, P * t:P * t + P], dn_out[:, t, P * c:P * c + P], ident)
                last.then_inc(turned, 1)

            @block.scalar
            def _(act):
                act.wait_ge(sums_ready, 1)
                nc.scalar.activation(small[:, 32:64], small[:, 0:32], ACT.Sqrt, scale=1.0 / HD, bias=col("eps")).then_inc(rooted, 1)
                act.wait_ge(turned, 1)
                for c in range(BC):
                    nc.scalar.activation(dn_out[:, c, :], ps[:, c, :], ACT.Copy)
        dn.close()

        att = ctx.enter_context(ExitStack())
        o_g, o_g_part = twin(nc, att, "group_out", [P, 3, BC, T])
        stats_g = [sb(att, f"stats{g}", [P, 3, 32]) for g in range(3)]
        lse = sb(att, "lse", [P, 3, TT, 8])
        lse_t = sb(att, "lse_t", [8, 3, T])
        lse_m = sb(att, "lse_max", [8, T])
        selector = sb(att, "selector", [8, BC, P])
        s_buf2 = sb(att, "s_buf2", [P, 3, 1024])
        scratch_b = arena[:, 0:2048].rearrange("p (a b) -> p a b", a=4)
        p_turned2 = arena[:, 2048:3072]
        v_g = arena[:, 3072:5120].rearrange("p (t n) -> p t n", t=TT)
        alibi_at = arena[:, 5120:8192]
        q_gain = small[:, 0:1]

        for g in range(3):
            step_ = 1 if g == 0 else 4

            def tokens(t, step_=step_):
                return slice(P * t, P * t + P) if step_ == 1 else slice(t, T, step_)

            w_alibi = 8 * (3 * P if g == 0 else P)
            with stage("alibi_loaded") as (block, alibi_loaded):
                @block.sync
                def _(sp):
                    sp.dma_start(alibi_at[:, 0:w_alibi], a[f"alibi{g}"]).then_inc(alibi_loaded, 16)
                    if g == 0:
                        sp.dma_start(selector[:, :, :], a["selector"].rearrange("h (c n) -> h c n", c=BC)).then_inc(alibi_loaded, 16)
                    sp.wait_ge(alibi_loaded, 32 if g == 0 else 16)

                @block.vector
                def _(dve):
                    nc.vector.tensor_scalar(q_gain, col("attn_qnorm"), HD ** -0.5, None, ALU.mult)
            project(h1T, [[("norm", q_gain, qT[:, m, :], True) for m in range(BC)],
                          [("norm", col("attn_knorm"), kT[:, m, :], True) for m in range(BC)],
                          [("token", (lambda h, k, sl=tokens(t): h[:, k, sl]), ACT.Copy, v_g[:, t, :]) for t in range(TT)]],
                    scratch_b)
            alibi = alibi_at[:, 0:w_alibi].rearrange("p (h x) -> p h x", h=8)
            units = []
            for t in range(TT):
                if g == 0:
                    lo, hi = max(t - 1, 0), min(t + 1, TT - 1)
                    w = P * (hi - lo + 1)
                    x0 = P * (lo - t + 1)
                    nt = hi - lo + 1
                    for c in range(BC):
                        rows = [slice(HD * p, HD * p + HD) for p in range(2)]
                        units.append(dict(
                            scores=[(512 * p, w, qT[rows[p], c, P * t:P * t + P], kT[rows[p], c, P * lo:P * lo + w]) for p in range(2)],
                            seg=(2, 512, w), bias=alibi[:, 2 * c:2 * c + 2, x0:x0 + w],
                            turns=[512 * p + P * m for p in range(2) for m in range(nt)],
                            pv=[(rows[p], 0, [(v_g[:, lo + m, HD * (2 * c + p):HD * (2 * c + p) + HD], nt * p + m) for m in range(nt)])
                                for p in range(2)],
                            out=[(o_g[:, 0, c, P * t:P * t + P], slice(0, P), slice(0, P))]))
                else:
                    sc, pv = [], []
                    for p in range(2):
                        r = slice(HD * p, HD * p + HD)
                        for c in range(BC):
                            sc.append((512 * p + P * c, P, qT[r, c, tokens(t)], kT[r, c, tokens(t)]))
                            pv.append((r, P * c, [(v_g[:, t, HD * (2 * c + p):HD * (2 * c + p) + HD], 4 * p + c)]))
                    units.append(dict(
                        scores=sc, seg=(8, P, P), bias=alibi[:, :, :], turns=[P * j for j in range(8)], pv=pv,
                        out=[(o_g[:, g, :, tokens(t)], slice(0, P), slice(0, 512))]))
            attention(units, stats_g[g], s_buf2, p_turned2)

        o_bT = o_g[:, 0]
        with stage("logs_ready", "lse_ready", "turned", "turned_read", "lse_sub", "lse_exp", "weights_ready", "spread", "spread_read") as (
                block, logs_ready, lse_ready, turned, turned_read, lse_sub, lse_exp, weights_ready, spread, spread_read):
            @block.scalar
            def _(act):
                for g in range(3):
                    nc.scalar.activation(stats_g[g][:, 1, :], stats_g[g][:, 1, :], ACT.Ln)
                act.drain().then_inc(logs_ready, 1)
                for g in range(3):
                    act.wait_ge(turned, g + 1)
                    src = ps[0:8, g, :]
                    if g == 0:
                        nc.scalar.activation(lse_t[:, g, :], src, ACT.Copy)
                    else:
                        nc.scalar.activation(lse_t[:, g, :].rearrange("h (j r) -> h r j", r=4), src.rearrange("h (r j) -> h r j", r=4), ACT.Copy)
                act.drain().then_inc(turned_read, 1)
                act.wait_ge(lse_sub, 1)
                nc.scalar.activation(lse_t[:, :, :], lse_t[:, :, :], ACT.Exp).then_inc(lse_exp, 1)

            @block.tensor
            def _(pe):
                pe.wait_ge(lse_ready, 1)
                for g in range(3):
                    for t in range(TT):
                        last = nc.tensor.transpose(ps[0:8, g, P * t:P * t + P], lse[:, g, t, :], ident)
                    last.then_inc(turned, 1)
                pe.wait_ge(weights_ready, 1)
                for n in range(12):
                    g, c = n // BC, n % BC
                    if n >= 4:
                        pe.wait_ge(spread_read, n - 3)
                    nc.tensor.matmul(ps[:, 4 + n % 4, :], selector[:, c, :], lse_t[:, g, :], start=True, stop=True).then_inc(spread, 1)

            @block.vector
            def _(dve):
                dve.wait_ge(logs_ready, 1)
                for g in range(3):
                    def order(x):
                        if g == 0:
                            return x.rearrange("p (t h) -> p t h", t=TT)
                        return x.rearrange("p (t q c) -> p t c q", t=TT, q=2)
                    dst = lse[:, g] if g == 0 else lse[:, g].rearrange("p t (c q) -> p t c q", q=2)
                    nc.vector.tensor_tensor(dst, order(stats_g[g][:, 1, :]), order(stats_g[g][:, 0, :]), ALU.subtract)
                dve.drain().then_inc(lse_ready, 1)
                dve.wait_ge(turned_read, 1)
                nc.vector.tensor_tensor(lse_m[:, :], lse_t[:, 0, :], lse_t[:, 1, :], ALU.max)
                dve.drain()
                nc.vector.tensor_tensor(lse_m[:, :], lse_m[:, :], lse_t[:, 2, :], ALU.max)
                dve.drain()
                nc.vector.tensor_tensor(lse_t[:, :, :], lse_t[:, :, :], lse_m[:, :].unsqueeze(1).to_broadcast([8, 3, T]), ALU.subtract)
                dve.drain().then_inc(lse_sub, 1)
                dve.wait_ge(lse_exp, 1)
                nc.vector.tensor_tensor(lse_m[:, :], lse_t[:, 0, :], lse_t[:, 1, :], ALU.add)
                dve.drain()
                nc.vector.tensor_tensor(lse_m[:, :], lse_m[:, :], lse_t[:, 2, :], ALU.add)
                dve.drain()
                nc.vector.reciprocal(lse_m[:, :], lse_m[:, :])
                dve.drain()
                nc.vector.tensor_tensor(lse_t[:, :, :], lse_t[:, :, :], lse_m[:, :].unsqueeze(1).to_broadcast([8, 3, T]), ALU.mult)
                dve.drain().then_inc(weights_ready, 1)
                for n in range(12):
                    g, c = n // BC, n % BC
                    dve.wait_ge(spread, n + 1)
                    nc.vector.tensor_tensor(o_g[:, g, c, :], o_g[:, g, c, :], ps[:, 4 + n % 4, :], ALU.mult).then_inc(spread_read, 1)
                dve.drain()
                nc.vector.tensor_tensor(o_bT, o_bT, o_g[:, 1], ALU.add)
                dve.drain()
                nc.vector.tensor_tensor(o_bT, o_bT, o_g[:, 2], ALU.add)

        hi_room = [arena_part[:, 2048 * n:2048 * n + 2048].rearrange("p (c t) -> p c t", c=BC) for n in (1, 2)]
        merge_branches(h1T, [(dn_out[:, :, :], hi_room[0], dn_out_part[:, :, :]), (o_bT, hi_room[1], o_g_part[:, 0])], chan(xn_flat, 0, DK),
                       arena[:, 0:1024].rearrange("p (a b) -> p a b", a=2), arena[:, 1024:2048].rearrange("p (a b) -> p a b", a=2))
        project_out((chan(xn_flat, 0, DK), h1T_hi, as_chunks(xn_part[:, :, :])), None)
        att.close()

        norm_stage(h1T_full, lambda k: col("norm2", k), None, *h1T)
        ffn = ctx.enter_context(ExitStack())
        actT, actT_lo = twin(nc, ffn, "ffn_hidden", [P, FFC, T])
        raw2 = arena[:, 0:4 * 2 * (T + 2)].rearrange("p (b m t) -> p b m t", b=4, m=2)
        conv2 = xn_flat.rearrange("p (b m t) -> p b m t", b=4, m=2)
        first_up = ring.taken
        with stage("pads_ready", "up_ready", "raw_ready", "convolved", "gates_ready", "hidden_ready") as (
                block, pads_ready, up_ready, raw_ready, convolved, gates_ready, hidden_ready):
            @block.sync
            def _(sp):
                ring.load(sp, FFC)

            @block.tensor
            def _(pe):
                for j in range(FFC):
                    w = ring.take(pe)
                    for m in range(2):
                        n = 2 * j + m
                        if n >= 8:
                            pe.wait_ge(raw_ready, n - 7)
                        for k in range(DK):
                            last = product(nc, ps[:, n % 8, :], cols_of(w, k, P * m), (h1T_hi[:, k, :], h1T_lo[:, k, :]), k == 0, k == DK - 1)
                        last.then_inc(up_ready, 1)
                    pe.wait_ge(up_ready, 2 * j + 2)
                    nc.tensor.nop().then_inc(ring.used, 1)

            @block.scalar
            def _(act):
                def silu(j):
                    act.wait_ge(convolved, 2 * j + 1)
                    nc.scalar.activation(conv2[:, j % 4, 0, :], conv2[:, j % 4, 0, :], ACT.Silu).then_inc(gates_ready, 1)

                act.wait_ge(pads_ready, 1)
                for j in range(FFC):
                    ring.ahead("act", act, first_up + j + 1)
                    for m in range(2):
                        n = 2 * j + m
                        act.wait_ge(up_ready, n + 1)
                        if j >= 4:
                            act.wait_ge(convolved, n - 7)
                        nc.scalar.activation(raw2[:, j % 4, m, 1:1 + T], ps[:, n % 8, :], ACT.Copy).then_inc(raw_ready, 1)
                    if j >= 1:
                        silu(j - 1)
                silu(FFC - 1)

            @block.vector
            def _(dve):
                def hidden(j):
                    dve.wait_ge(gates_ready, j + 1)
                    nc.vector.tensor_tensor(actT[:, j, :], conv2[:, j % 4, 0, :], conv2[:, j % 4, 1, :], ALU.mult)

                nc.vector.memset(raw2[:, :, :, 0:1], 0.0)
                nc.vector.memset(raw2[:, :, :, T + 1:T + 2], 0.0)
                dve.drain().then_inc(pads_ready, 1)
                for j in range(FFC):
                    ring.ahead("dve", dve, first_up + j + 1)
                    for m in range(2):
                        f = j + FFC * m
                        dst, src = conv2[:, j % 4, m, :], raw2[:, j % 4, m, :]
                        dve.wait_ge(raw_ready, 2 * j + m + 1)
                        nc.vector.tensor_scalar(dst, src[:, 0:T], col("ffn_conv", 3 * f), None, ALU.mult)
                        for k in range(1, 3):
                            dve.drain()
                            last = nc.vector.scalar_tensor_tensor(dst, src[:, k:k + T], col("ffn_conv", 3 * f + k), dst, ALU.mult, ALU.add)
                        last.then_inc(convolved, 1)
                    if j >= 1:
                        hidden(j - 1)
                        dve.drain()
                hidden(FFC - 1)

        first_down = ring.taken
        ND = FFC // 2
        hid_hi2 = arena_part[:, 0:4 * 2 * T].rearrange("p (b k t) -> p b k t", b=4, k=2)
        with stage("hid_rounded", "hid_split", "down_ready", "rows_ready", "stored") as (
                block, hid_rounded, hid_split, down_ready, rows_ready, stored):
            @block.tensor
            def _(pe):
                for j in range(ND):
                    w = ring.take(pe)
                    pe.wait_ge(hid_split, j + 1)
                    for t in range(TT):
                        for h in range(2):
                            for k in range(2):
                                tok = slice(P * t, P * t + P)
                                last = product(nc, ps[:, 2 * t + h, :], (hid_hi2[:, j % 4, k, tok], actT_lo[:, 2 * j + k, tok]),
                                               cols_of(w, k, 512 * h, 512), j == 0 and k == 0, j == ND - 1 and k == 1)
                        if j == ND - 1:
                            last.then_inc(down_ready, 1)
                    if j < ND - 1:
                        last.then_inc(ring.used, 1)

            @block.scalar
            def _(act):
                for j in range(ND):
                    if j >= 4:
                        act.wait_ge(ring.used, first_down - ring.base + j - 3)
                    nc.scalar.activation(hid_hi2[:, j % 4], actT[:, 2 * j:2 * j + 2, :], ACT.Copy).then_inc(hid_rounded, 1)
                    ring.ahead("act", act, first_down + j + 1)

            @block.vector
            def _(dve):
                for j in range(ND):
                    dve.wait_ge(hid_rounded, j + 1)
                    nc.vector.tensor_tensor(actT_lo[:, 2 * j:2 * j + 2, :], actT[:, 2 * j:2 * j + 2, :], hid_hi2[:, j % 4], ALU.subtract)\
                        .then_inc(hid_split, 1)
                    ring.ahead("dve", dve, first_down + j + 1)
                for t in range(TT):
                    dve.wait_ge(down_ready, t + 1)
                    nc.vector.tensor_tensor(x_tok[:, t, :], x_tok[:, t, :], ps[:, 2 * t:2 * t + 2, :].rearrange("p b n -> p (b n)"),
                                            ALU.add).then_inc(rows_ready, 1)

            @block.sync
            def _(sp):
                ring.load(sp, ND)
                for t in range(TT):
                    sp.wait_ge(rows_ready, t + 1)
                    sp.dma_start(out[0, P * t:P * t + P, :], x_tok[:, t, :]).then_inc(stored, 16)
                sp.wait_ge(stored, 16 * TT)


_OUTS = [((1, T, D), "float32")]


def host_arrays(i):
    arrays = {k: np.ascontiguousarray(i[k]) for k in
              ("x", "b_ada", "w_ada", "w_in", "w_branch", "w_out", "w_router", "w1", "b1", "w2", "b2", "rel_bias", "w_in_2",
               "w_dn_out_2", "w_attn_out_2", "w_o_2", "w_ffn_up_2", "w_ffn_down_2")}
    c = constants()
    arrays["const"] = np.concatenate([c[n] for n, _ in CONST_W], 1)
    kv = np.asarray(i["w_in"])[0, :, 3072:3328]
    arrays["w_kv"] = np.ascontiguousarray(np.concatenate([kv[:, 0:HD], kv[:, 0:HD], kv[:, HD:P], kv[:, HD:P], kv[:, P:]], 1))
    arrays["joins"] = np.concatenate([c["join_lo"], c["join_up"]], 1)
    arrays["columns"] = pack_columns(i)
    order = [0, 1, 2, 3] + [4 + 4 * g + j for g in range(2) for j in SWA_ORDER]
    arrays["rel_bias"] = np.ascontiguousarray(arrays["rel_bias"][:, order])
    arrays["lru_a"] = pack_blocks(i["lru_wa"])
    arrays["lru_x"] = pack_blocks(i["lru_wx"])
    arrays["bucket_onehot"], arrays["bucket_mask"] = bias_constants()
    heads = np.arange(8)[:, None, None]
    arrays["selector"] = (heads == 2 * np.arange(BC)[None, :, None] + np.arange(P)[None, None, :] // HD)\
        .astype(np.float32).reshape(8, -1)
    arrays["alibi0"], arrays["alibi1"], arrays["alibi2"] = alibi_constants()
    return arrays


def kernel(**inputs):
    import concourse.bacc as _bacc
    from concourse.bass_utils import run_bass_kernel_spmd as _run

    nc = _bacc.Bacc("TRN2", target_bir_lowering=False, num_devices=1)
    arrays, args = {}, {}
    for name, x in host_arrays(inputs).items():
        arrays[f"in_{name}"] = x
        args[name] = nc.dram_tensor(f"in_{name}", x.shape, mybir.dt.from_np(x.dtype), kind="ExternalInput").ap()
    shape, dtype = _OUTS[0]
    out = nc.dram_tensor("out_0", shape, mybir.dt.from_np(np.dtype(dtype)), kind="ExternalOutput").ap()
    build(nc, args, out)
    r = _run(nc, [arrays], core_ids=[0])
    return r.results[0]["out_0"]
```
